# Optimizing a Trainium2 kernel written in Bass

```python
import math
import jax, jax.numpy as jnp
from jax import lax
import numpy as np
import jax
import jax.numpy as jnp

D_MODEL = 1024
BATCH = 1
SEQ = 256
DEPTH = 2

HEAD_DIM = 64
H_A = 8
KV_RANK = 128
H_IDX = 8
D_IDX = 64
TOPK_MAX = 256
H_B = 8
Q_BLOCK = 128
N_BUCKETS = 32
T5_MAX_DIST = 128
G_C = 8
CHUNK = 128
C_WIDTH = G_C * HEAD_DIM
G_D = 8
D_WIDTH = G_D * HEAD_DIM
CONV_W = 3
D_FF = 2816
N_EVEN = (DEPTH + 1) // 2
N_ODD = DEPTH // 2
ALPHA = (2.0 * DEPTH) ** 0.25
BETA = (8.0 * DEPTH) ** -0.25
LN_EPS = 1e-5
EVEN_WIDTHS = (H_A * HEAD_DIM, KV_RANK, H_IDX * D_IDX, D_IDX, H_IDX,
               H_B * HEAD_DIM, H_B * HEAD_DIM, H_B * HEAD_DIM, H_B)
ODD_WIDTHS = (C_WIDTH, C_WIDTH, D_WIDTH, D_WIDTH, D_WIDTH)
EVEN_PROJ = sum(EVEN_WIDTHS)
ODD_PROJ = sum(ODD_WIDTHS)
EVEN_MIX = H_A * HEAD_DIM + H_B * HEAD_DIM
ODD_MIX = C_WIDTH + D_WIDTH


def _split(h, widths):
    out, off = [], 0
    for w in widths:
        out.append(h[..., off:off + w])
        off += w
    return out

def layer_norm(x, g, b=None):
    xf = x.astype(jnp.float32)
    mu = jnp.mean(xf, axis=-1, keepdims=True)
    xc = xf - mu
    var = jnp.mean(xc * xc, axis=-1, keepdims=True)
    y = xc * lax.rsqrt(var + LN_EPS) * g.astype(jnp.float32)
    if b is not None:
        y = y + b.astype(jnp.float32)
    return y.astype(x.dtype)

def causal_dwconv(z, w):
    width, ch = w.shape
    return lax.conv_general_dilated(
        z, w[:, None, :].astype(z.dtype), window_strides=(1,),
        padding=[(width - 1, 0)], dimension_numbers=('NWC', 'WIO', 'NWC'),
        feature_group_count=ch)

def t5_bucket(dist):
    max_exact = N_BUCKETS // 2
    n = jnp.maximum(dist, 0)
    nf = jnp.maximum(n, 1).astype(jnp.float32)
    large = max_exact + (jnp.log(nf / max_exact) / math.log(T5_MAX_DIST / max_exact)
                         * (N_BUCKETS - max_exact)).astype(jnp.int32)
    large = jnp.minimum(large, N_BUCKETS - 1)
    return jnp.where(n < max_exact, n, large)

def to_blocks(a):
    return jnp.moveaxis(a.reshape(a.shape[0], -1, Q_BLOCK, *a.shape[2:]), 1, 0)

def from_blocks(a):
    a = jnp.moveaxis(a, 0, 1)
    return a.reshape(a.shape[0], -1, *a.shape[3:])

def even_mixer(x, w_in, w_uk, w_uv, b_f, w_o, rel_bias):
    bsz, seq, _ = x.shape
    k_sel = min(TOPK_MAX, seq // 4)
    n_blk = seq // Q_BLOCK
    h = x @ w_in
    q_a, c_kv, q_idx, k_idx, w_idx, q_b, k_b, v_b, f_in = _split(h, EVEN_WIDTHS)
    q_a = q_a.reshape(bsz, seq, H_A, HEAD_DIM)
    q_lat = jnp.einsum('bshd,hrd->bshr', q_a, w_uk) * (HEAD_DIM ** -0.5)
    q_idx = q_idx.reshape(bsz, seq, H_IDX, D_IDX) * (D_IDX ** -0.5)
    w_idx = w_idx * (H_IDX ** -0.5)
    q_b = q_b.reshape(bsz, seq, H_B, HEAD_DIM) * (HEAD_DIM ** -0.5)
    k_b = k_b.reshape(bsz, seq, H_B, HEAD_DIM)
    v_b = v_b.reshape(bsz, seq, H_B, HEAD_DIM)
    log_f = jax.nn.log_sigmoid(f_in.astype(jnp.float32) + b_f.astype(jnp.float32))
    cum_f = jnp.cumsum(log_f, axis=1)
    cum_f_keys = jnp.swapaxes(cum_f, 1, 2)

    key_pos = jnp.arange(seq)
    bidx = jnp.arange(bsz)[:, None, None]

    def block(args):
        i, ql, qi, wi, qb, fq = args
        q_pos = i * Q_BLOCK + jnp.arange(Q_BLOCK)
        causal = key_pos[None, :] <= q_pos[:, None]
        idx = jnp.einsum('bthd,bsd->bths', qi, k_idx)
        score = jnp.einsum('bth,bths->bts', wi, jax.nn.relu(idx)).astype(jnp.float32)
        score = jnp.where(causal[None], score, -jnp.inf)
        _, sel = lax.top_k(score, k_sel)
        valid = sel <= q_pos[None, :, None]
        c_sel = c_kv[bidx, sel]
        la = jnp.einsum('bthr,btkr->bhtk', ql, c_sel).astype(jnp.float32)
        bias = rel_bias[t5_bucket(q_pos[None, :, None] - sel)]
        la = la + jnp.moveaxis(bias, -1, 1).astype(jnp.float32)
        la = jnp.where(valid[:, None], la, -jnp.inf)
        pa = jax.nn.softmax(la, axis=-1).astype(c_sel.dtype)
        oa = jnp.einsum('bhtk,btkr->bthr', pa, c_sel)
        lb = jnp.einsum('bthd,bshd->bhts', qb, k_b).astype(jnp.float32)
        lb = lb + jnp.swapaxes(fq, 1, 2)[..., None] - cum_f_keys[:, :, None, :]
        lb = jnp.where(causal[None, None], lb, -jnp.inf)
        pb = jax.nn.softmax(lb, axis=-1).astype(v_b.dtype)
        ob = jnp.einsum('bhts,bshd->bthd', pb, v_b)
        return oa, ob

    oa, ob = lax.map(block, (jnp.arange(n_blk), to_blocks(q_lat), to_blocks(q_idx),
                             to_blocks(w_idx), to_blocks(q_b), to_blocks(cum_f)))
    o_a = jnp.einsum('bshr,hrd->bshd', from_blocks(oa), w_uv).reshape(bsz, seq, H_A * HEAD_DIM)
    o_b = from_blocks(ob).reshape(bsz, seq, H_B * HEAD_DIM)
    return jnp.concatenate([o_a, o_b], axis=-1) @ w_o

def odd_mixer(x, w_in, sgu_g, sgu_w, sgu_b, conv_w, w_o):
    bsz, seq, _ = x.shape
    h = x @ w_in
    u, v, g_b, g_c, z = _split(h, ODD_WIDTHS)
    u = jax.nn.gelu(u)
    v = layer_norm(jax.nn.gelu(v).reshape(bsz, seq, G_C, HEAD_DIM), sgu_g)
    v = v.reshape(bsz, seq // CHUNK, CHUNK, G_C, HEAD_DIM)
    mix = jnp.einsum('gts,bnsgd->bntgd', jnp.tril(sgu_w), v) + jnp.swapaxes(sgu_b, 0, 1)[:, :, None]
    o_c = u * mix.reshape(bsz, seq, C_WIDTH)
    o_d = g_b * causal_dwconv(g_c * z, conv_w)
    return jnp.concatenate([o_c, o_d], axis=-1) @ w_o

def conv_ffn(x, w_up, conv_w, w_down):
    h = causal_dwconv(x @ w_up, conv_w)
    g, v = jnp.split(h, 2, axis=-1)
    return (jax.nn.silu(g) * v) @ w_down

def first_inputs(seed: int = 0) -> dict:
    key = jax.random.key(seed)
    ks = jax.random.split(key, 18)

    def nrm(k, shape, scale):
        return jax.random.normal(k, shape, jnp.float32) * scale

    return {
        "x": nrm(ks[0], (BATCH, SEQ, D_MODEL), 1.0),
        "ln_g": 1.0 + nrm(ks[1], (DEPTH, 2, D_MODEL), 0.02),
        "ln_b": nrm(ks[2], (DEPTH, 2, D_MODEL), 0.02),
        "rel_bias": nrm(ks[3], (N_BUCKETS, H_A), 0.5),
        "ev_w_in": nrm(ks[4], (N_EVEN, D_MODEL, EVEN_PROJ), D_MODEL ** -0.5),
        "ev_w_uk": nrm(ks[5], (N_EVEN, H_A, KV_RANK, HEAD_DIM), KV_RANK ** -0.5),
        "ev_w_uv": nrm(ks[6], (N_EVEN, H_A, KV_RANK, HEAD_DIM), KV_RANK ** -0.5),
        "ev_b_f": jax.random.uniform(ks[7], (N_EVEN, H_B), jnp.float32, 1.0, 4.0),
        "ev_w_o": nrm(ks[8], (N_EVEN, EVEN_MIX, D_MODEL), BETA * EVEN_MIX ** -0.5),
        "od_w_in": nrm(ks[9], (N_ODD, D_MODEL, ODD_PROJ), D_MODEL ** -0.5),
        "od_sgu_g": 1.0 + nrm(ks[10], (N_ODD, G_C, HEAD_DIM), 0.02),
        "od_sgu_w": nrm(ks[11], (N_ODD, G_C, CHUNK, CHUNK), CHUNK ** -0.5),
        "od_sgu_b": 1.0 + nrm(ks[12], (N_ODD, G_C, CHUNK), 0.1),
        "od_conv_w": nrm(ks[13], (N_ODD, CONV_W, D_WIDTH), CONV_W ** -0.5),
        "od_w_o": nrm(ks[14], (N_ODD, ODD_MIX, D_MODEL), BETA * ODD_MIX ** -0.5),
        "ffn_w_up": nrm(ks[15], (DEPTH, D_MODEL, 2 * D_FF), D_MODEL ** -0.5),
        "ffn_conv_w": nrm(ks[16], (DEPTH, CONV_W, 2 * D_FF), CONV_W ** -0.5),
        "ffn_w_down": nrm(ks[17], (DEPTH, D_FF, D_MODEL), BETA * D_FF ** -0.5),
    }

def first_block(x, ln_g, ln_b, rel_bias, ev_w_in, ev_w_uk, ev_w_uv, ev_b_f, ev_w_o,
              od_w_in, od_sgu_g, od_sgu_w, od_sgu_b, od_conv_w, od_w_o,
              ffn_w_up, ffn_conv_w, ffn_w_down):
    for layer in range(DEPTH):
        j = layer // 2
        if layer % 2 == 0:
            m = even_mixer(x, ev_w_in[j], ev_w_uk[j], ev_w_uv[j], ev_b_f[j], ev_w_o[j], rel_bias)
        else:
            m = odd_mixer(x, od_w_in[j], od_sgu_g[j], od_sgu_w[j], od_sgu_b[j], od_conv_w[j], od_w_o[j])
        x = layer_norm(ALPHA * x + m, ln_g[layer, 0], ln_b[layer, 0])
        f = conv_ffn(x, ffn_w_up[layer], ffn_conv_w[layer], ffn_w_down[layer])
        x = layer_norm(ALPHA * x + f, ln_g[layer, 1], ln_b[layer, 1])
    return x


F32 = jnp.float32
N_MIXERS = 4
GRID_W = 64
MEM_LEN = 256
NORM_EPS = 1e-6

ATT_HEADS = 16
ATT_KV_HEADS = 4
ATT_HEAD_DIM = D_MODEL // ATT_HEADS
ATT_Q_W = ATT_HEADS * ATT_HEAD_DIM
ATT_KV_W = ATT_KV_HEADS * ATT_HEAD_DIM
ROPE_THETA = 10000.0
WINDOW = 128
ATT_BLOCK = 128

NA_ROWS_MAX = 8
NA_COLS = 16
NA_QCOLS = 16
NA_KCOLS = NA_QCOLS + NA_COLS

X_HEADS = 4
X_HEAD_DIM = 128
X_W = X_HEADS * X_HEAD_DIM

HG_KEY_DIM = 128
HG_HEADS = D_MODEL // HG_KEY_DIM
HG_VAL_DIM = D_MODEL // HG_HEADS
HG_W = HG_HEADS * HG_KEY_DIM
HG_CHUNK = 16

SSM_INNER = 2 * D_MODEL
SSM_HEAD_DIM = 64
SSM_HEADS = SSM_INNER // SSM_HEAD_DIM
SSM_GROUPS = 8
SSM_HEADS_PER_GROUP = SSM_HEADS // SSM_GROUPS
SSM_STATE = 128
SSM_CONV = 5
SSM_CHUNK = 64
SSM_CONV_DIM = SSM_INNER + 2 * SSM_GROUPS * SSM_STATE

FFN_CONV = 3

A_IN_W = ATT_Q_W + 2 * ATT_KV_W + X_W
B_IN_W = 5 * HG_W + X_W
C_IN_W = SSM_INNER + SSM_CONV_DIM + 2 * SSM_HEADS + X_W
D_IN_W = ATT_Q_W + 2 * ATT_KV_W + X_W


def _layers_of(m):
    return (DEPTH - m + N_MIXERS - 1) // N_MIXERS

def rmsnorm(x, g):
    xf = x.astype(F32)
    y = xf * lax.rsqrt(jnp.mean(xf * xf, axis=-1, keepdims=True) + NORM_EPS)
    return (y * g.astype(F32)).astype(x.dtype)

def flip_t(a):
    return jnp.flip(a, axis=1)

def rope(x, pos):
    half = x.shape[-1] // 2
    inv = ROPE_THETA ** (-jnp.arange(half, dtype=F32) / half)
    ang = pos.astype(F32)[:, None] * inv[None, :]
    cos = jnp.cos(ang)[None, :, None, :]
    sin = jnp.sin(ang)[None, :, None, :]
    xf = x.astype(F32)
    x1, x2 = xf[..., :half], xf[..., half:]
    return jnp.concatenate([x1 * cos - x2 * sin, x2 * cos + x1 * sin], axis=-1).astype(x.dtype)

def dwconv_centred(x, w, b):
    k, c = w.shape
    y = lax.conv_general_dilated(x, w[:, None, :].astype(x.dtype), window_strides=(1,),
                                 padding=[(k // 2, k // 2)],
                                 dimension_numbers=('NWC', 'WIO', 'NWC'),
                                 feature_group_count=c)
    return y + b.astype(x.dtype)

def memory_cross_attn(xq, mem_kv):
    bsz, t, _ = xq.shape
    q = xq.reshape(bsz, t, X_HEADS, X_HEAD_DIM)
    k, v = jnp.split(mem_kv, 2, axis=-1)
    k = k.reshape(bsz, -1, X_HEADS, X_HEAD_DIM)
    v = v.reshape(bsz, -1, X_HEADS, X_HEAD_DIM)
    s = jnp.einsum('bthd,bmhd->bhtm', q, k, preferred_element_type=F32) * (X_HEAD_DIM ** -0.5)
    p = jax.nn.softmax(s, axis=-1)
    o = jnp.einsum('bhtm,bmhd->bthd', p.astype(v.dtype), v)
    return o.reshape(bsz, t, X_W)

def window_gqa_sink(q, k, v, sink):
    bsz, t, hq, d = q.shape
    hkv = k.shape[2]
    grp = hq // hkv
    nb = t // ATT_BLOCK
    band = ATT_BLOCK + 2 * WINDOW
    pad = ((0, 0), (WINDOW, WINDOW), (0, 0), (0, 0))
    idx = np.arange(nb)[:, None] * ATT_BLOCK + np.arange(band)[None, :]
    kb = jnp.pad(k, pad)[:, idx]
    vb = jnp.pad(v, pad)[:, idx]
    qb = q.reshape(bsz, nb, ATT_BLOCK, hkv, grp, d)
    s = jnp.einsum('bnqhgd,bnkhd->bnhgqk', qb, kb, preferred_element_type=F32) * (d ** -0.5)
    qpos = np.arange(nb)[:, None] * ATT_BLOCK + np.arange(ATT_BLOCK)[None, :]
    kpos = idx - WINDOW
    valid = ((np.abs(qpos[:, :, None] - kpos[:, None, :]) <= WINDOW)
             & (kpos >= 0)[:, None, :] & (kpos < t)[:, None, :])
    s = jnp.where(valid[None, :, None, None], s, -jnp.inf)
    sk = sink.astype(F32).reshape(hkv, grp)[None, None, :, :, None, None]
    m = jnp.maximum(jnp.max(s, axis=-1, keepdims=True), sk)
    p = jnp.exp(s - m)
    p = p / (jnp.sum(p, axis=-1, keepdims=True) + jnp.exp(sk - m))
    o = jnp.einsum('bnhgqk,bnkhd->bnqhgd', p.astype(v.dtype), vb)
    return o.reshape(bsz, t, hq, d)

def neighbourhood_attn(q, k, v, rpb):
    bsz, t, hq, d = q.shape
    hkv = k.shape[2]
    grp = hq // hkv
    rows = t // GRID_W
    kr = min(NA_ROWS_MAX, rows)
    ncb = GRID_W // NA_QCOLS
    r = np.arange(rows)
    key_rows = np.clip(r - kr // 2, 0, rows - kr)[:, None] + np.arange(kr)[None, :]
    key_cols = (np.clip(np.arange(ncb) * NA_QCOLS - NA_COLS // 2, 0, GRID_W - NA_KCOLS)[:, None]
                + np.arange(NA_KCOLS)[None, :])
    key_idx = (key_rows[:, None, :, None] * GRID_W + key_cols[None, :, None, :]).reshape(rows, ncb, kr * NA_KCOLS)
    kg = k[:, key_idx]
    vg = v[:, key_idx]
    qb = q.reshape(bsz, rows, ncb, NA_QCOLS, hkv, grp, d)
    s = jnp.einsum('brjqhgd,brjkhd->brjhgqk', qb, kg, preferred_element_type=F32) * (d ** -0.5)
    qcol = np.arange(ncb)[:, None] * NA_QCOLS + np.arange(NA_QCOLS)[None, :]
    col_start = np.clip(qcol - NA_COLS // 2, 0, GRID_W - NA_COLS)
    kcol = np.repeat(key_cols[:, None, :], kr, axis=1).reshape(ncb, -1)
    krow = np.repeat(key_rows[:, :, None], NA_KCOLS, axis=2).reshape(rows, -1)
    in_win = ((kcol[:, None, :] >= col_start[..., None])
              & (kcol[:, None, :] < col_start[..., None] + NA_COLS))
    dr = krow - r[:, None] + NA_ROWS_MAX - 1
    dc = np.clip(kcol[:, None, :] - qcol[..., None] + NA_COLS - 1, 0, 2 * NA_COLS - 2)
    bias = rpb.astype(F32)[:, dr[:, None, None, :], dc[None]]
    bias = jnp.where(in_win[None, None], bias, -jnp.inf)
    bias = bias.reshape(hkv, grp, rows, ncb, NA_QCOLS, -1).transpose(2, 3, 0, 1, 4, 5)
    p = jax.nn.softmax(s + bias[None], axis=-1)
    o = jnp.einsum('brjhgqk,brjkhd->brjqhgd', p.astype(v.dtype), vg)
    return o.reshape(bsz, t, hq, d)

def gla_chunked(q, k, v, log_f):
    bsz, t, h, dk = q.shape
    dv = v.shape[-1]
    n = t // HG_CHUNK
    q, k, log_f = (a.reshape(bsz, n, HG_CHUNK, h, dk) for a in (q, k, log_f))
    v = v.reshape(bsz, n, HG_CHUNK, h, dv)
    b = jnp.cumsum(log_f, axis=2)
    b_end = b[:, :, -1:]
    q_dec = q * jnp.exp(b)
    k_dec = k * jnp.exp(-b)
    k_end = k * jnp.exp(b_end - b)
    causal = np.tril(np.ones((HG_CHUNK, HG_CHUNK), dtype=bool))
    s = jnp.where(causal, jnp.einsum('bcthk,bcshk->bchts', q_dec, k_dec), 0.0)
    o_intra = jnp.einsum('bchts,bcshv->bcthv', s, v)

    def step(state, inp):
        qd, ke, vc, dec = inp
        o = jnp.einsum('bthk,bhkv->bthv', qd, state)
        state = dec[..., None] * state + jnp.einsum('bshk,bshv->bhkv', ke, vc)
        return state, o

    xs = tuple(jnp.moveaxis(a, 1, 0) for a in (q_dec, k_end, v, jnp.exp(b_end[:, :, 0])))
    _, o_inter = lax.scan(step, jnp.zeros((bsz, h, dk, dv), F32), xs)
    return (o_intra + jnp.moveaxis(o_inter, 0, 1)).reshape(bsz, t, h, dv)

def ssd_chunked(x, dt, a, bm, cm):
    bsz, t, g, j, p = x.shape
    nst = bm.shape[-1]
    n = t // SSM_CHUNK
    x = x.reshape(bsz, n, SSM_CHUNK, g, j, p)
    dt = dt.reshape(bsz, n, SSM_CHUNK, g, j)
    bm = bm.reshape(bsz, n, SSM_CHUNK, g, nst)
    cm = cm.reshape(bsz, n, SSM_CHUNK, g, nst)
    cs = jnp.cumsum(dt * a, axis=2)
    xdt = x * dt[..., None]
    cs_t = jnp.moveaxis(cs, 2, -1)
    causal = np.tril(np.ones((SSM_CHUNK, SSM_CHUNK), dtype=bool))
    decay = jnp.exp(jnp.where(causal, cs_t[..., :, None] - cs_t[..., None, :], -jnp.inf))
    cb = jnp.einsum('bctgn,bcsgn->bcgts', cm, bm)
    y_diag = jnp.einsum('bcgjts,bcsgjp->bctgjp', cb[:, :, :, None] * decay, xdt)

    def step(state, inp):
        cq, bk, xd, c = inp
        c_end = c[:, -1]
        y_off = jnp.einsum('btgn,bgjpn->btgjp', cq, state) * jnp.exp(c)[..., None]
        w = jnp.exp(c_end[:, None] - c)[..., None]
        state = jnp.exp(c_end)[..., None, None] * state + jnp.einsum('bsgn,bsgjp->bgjpn', bk, xd * w)
        return state, y_off

    xs = tuple(jnp.moveaxis(arr, 1, 0) for arr in (cm, bm, xdt, cs))
    _, y_off = lax.scan(step, jnp.zeros((bsz, g, j, p, nst), F32), xs)
    return (y_diag + jnp.moveaxis(y_off, 0, 1)).reshape(bsz, t, g, j, p)

def hgrn_lower_bounds(logits):
    p = jax.nn.softmax(logits.astype(F32), axis=1)
    return jnp.cumsum(p, axis=1) - p[:, :1]

def mixer_window_attn(u, mem_kv, w_in, sink, w_out, pos):
    bsz, t, _ = u.shape
    q, k, v, xq = jnp.split(u @ w_in, [ATT_Q_W, ATT_Q_W + ATT_KV_W, ATT_Q_W + 2 * ATT_KV_W], axis=-1)
    q = rope(q.reshape(bsz, t, ATT_HEADS, ATT_HEAD_DIM), pos)
    k = rope(k.reshape(bsz, t, ATT_KV_HEADS, ATT_HEAD_DIM), pos)
    v = v.reshape(bsz, t, ATT_KV_HEADS, ATT_HEAD_DIM)
    o = window_gqa_sink(q, k, v, sink).reshape(bsz, t, ATT_Q_W)
    return jnp.concatenate([o, memory_cross_attn(xq, mem_kv)], axis=-1) @ w_out

def mixer_hgrn2(u, mem_kv, w_in, lb_fwd, lb_bwd, norm_g, w_out):
    bsz, t, _ = u.shape
    q, i, zf, zb, gate, xq = jnp.split(u @ w_in, [HG_W, 2 * HG_W, 3 * HG_W, 4 * HG_W, 5 * HG_W], axis=-1)
    shp = (bsz, t, HG_HEADS, HG_KEY_DIM)
    q = jax.nn.silu(q.astype(F32)).reshape(shp)
    v = i.astype(F32).reshape(bsz, t, HG_HEADS, HG_VAL_DIM)

    def forget(z, lb):
        f = lb + (1.0 - lb) * jax.nn.sigmoid(z.astype(F32))
        return jnp.log(f).reshape(shp), (1.0 - f).reshape(shp)

    lf_f, k_f = forget(zf, lb_fwd)
    lf_b, k_b = forget(zb, lb_bwd)
    o = (gla_chunked(q, k_f, v, lf_f)
         + flip_t(gla_chunked(flip_t(q), flip_t(k_b), flip_t(v), flip_t(lf_b))))
    o = rmsnorm(o, norm_g.reshape(HG_HEADS, HG_VAL_DIM)).reshape(bsz, t, HG_W).astype(u.dtype)
    o = o * jax.nn.silu(gate)
    return jnp.concatenate([o, memory_cross_attn(xq, mem_kv)], axis=-1) @ w_out

def mixer_mamba2(u, mem_kv, w_in, conv_w, conv_b, dt_bias, a_log, d_skip, norm_g, w_out):
    bsz, t, _ = u.shape
    z, xbc, dt_raw, xq = jnp.split(
        u @ w_in, [SSM_INNER, SSM_INNER + SSM_CONV_DIM, SSM_INNER + SSM_CONV_DIM + 2 * SSM_HEADS], axis=-1)
    xbc = jax.nn.silu(dwconv_centred(xbc, conv_w, conv_b)).astype(F32)
    xs, bm, cm = jnp.split(xbc, [SSM_INNER, SSM_INNER + SSM_GROUPS * SSM_STATE], axis=-1)
    xs = xs.reshape(bsz, t, SSM_GROUPS, SSM_HEADS_PER_GROUP, SSM_HEAD_DIM)
    bm = bm.reshape(bsz, t, SSM_GROUPS, SSM_STATE)
    cm = cm.reshape(bsz, t, SSM_GROUPS, SSM_STATE)
    dt = jax.nn.softplus(dt_raw.astype(F32).reshape(bsz, t, 2, SSM_HEADS) + dt_bias.astype(F32))
    dt = dt.reshape(bsz, t, 2, SSM_GROUPS, SSM_HEADS_PER_GROUP)
    a = -jnp.exp(a_log.astype(F32)).reshape(2, SSM_GROUPS, SSM_HEADS_PER_GROUP)
    y = (ssd_chunked(xs, dt[:, :, 0], a[0], bm, cm)
         + flip_t(ssd_chunked(flip_t(xs), flip_t(dt[:, :, 1]), a[1], flip_t(bm), flip_t(cm))))
    y = y + d_skip.astype(F32).reshape(SSM_GROUPS, SSM_HEADS_PER_GROUP, 1) * xs
    y = y.reshape(bsz, t, SSM_INNER) * jax.nn.silu(z.astype(F32))
    y = rmsnorm(y.reshape(bsz, t, SSM_GROUPS, -1), norm_g.reshape(SSM_GROUPS, -1))
    y = y.reshape(bsz, t, SSM_INNER).astype(u.dtype)
    return jnp.concatenate([y, memory_cross_attn(xq, mem_kv)], axis=-1) @ w_out

def mixer_neighbourhood(u, mem_kv, w_in, rpb, w_out):
    bsz, t, _ = u.shape
    q, k, v, xq = jnp.split(u @ w_in, [ATT_Q_W, ATT_Q_W + ATT_KV_W, ATT_Q_W + 2 * ATT_KV_W], axis=-1)
    q = q.reshape(bsz, t, ATT_HEADS, ATT_HEAD_DIM)
    k = k.reshape(bsz, t, ATT_KV_HEADS, ATT_HEAD_DIM)
    v = v.reshape(bsz, t, ATT_KV_HEADS, ATT_HEAD_DIM)
    o = neighbourhood_attn(q, k, v, rpb).reshape(bsz, t, ATT_Q_W)
    return jnp.concatenate([o, memory_cross_attn(xq, mem_kv)], axis=-1) @ w_out

def conv_ffn_2(v, w_in, conv_w, conv_b, w_out):
    gate, up = jnp.split(v @ w_in, 2, axis=-1)
    hid = jax.nn.gelu(dwconv_centred(gate, conv_w, conv_b)) * up
    return hid @ w_out

def second_inputs(seed: int = 0) -> dict:
    key = jax.random.key(seed)
    ks = jax.random.split(key, 32)
    n_a, n_b, n_c, n_d = (_layers_of(m) for m in range(N_MIXERS))

    def nrm(k, shape, scale):
        return jax.random.normal(k, shape, F32) * scale

    def gain(k, shape):
        return 1.0 + 0.05 * jax.random.normal(k, shape, F32)

    dt0 = jnp.exp(jax.random.uniform(ks[16], (n_c, 2, SSM_HEADS), F32, math.log(1e-3), math.log(1e-1)))
    return {
        'x': nrm(ks[0], (BATCH, SEQ, D_MODEL), 1.0),
        'mem': nrm(ks[1], (BATCH, MEM_LEN, D_MODEL), 1.0),
        'norm_g': gain(ks[2], (DEPTH, 4, D_MODEL)),
        'mem_norm_g': gain(ks[3], (D_MODEL,)),
        'w_mem_kv': nrm(ks[4], (DEPTH, D_MODEL, 2 * X_W), D_MODEL ** -0.5),
        'a_w_in': nrm(ks[5], (n_a, D_MODEL, A_IN_W), D_MODEL ** -0.5),
        'a_sink': nrm(ks[6], (n_a, ATT_HEADS), 0.5),
        'a_w_out': nrm(ks[7], (n_a, ATT_Q_W + X_W, D_MODEL), (ATT_Q_W + X_W) ** -0.5),
        'b_w_in': nrm(ks[8], (n_b, D_MODEL, B_IN_W), D_MODEL ** -0.5),
        'b_lb_logits': nrm(ks[9], (2, DEPTH, HG_W), 0.1),
        'b_norm_g': gain(ks[10], (n_b, HG_W)),
        'b_w_out': nrm(ks[11], (n_b, HG_W + X_W, D_MODEL), (HG_W + X_W) ** -0.5),
        'c_w_in': nrm(ks[12], (n_c, D_MODEL, C_IN_W), D_MODEL ** -0.5),
        'c_conv_w': nrm(ks[13], (n_c, SSM_CONV, SSM_CONV_DIM), SSM_CONV ** -0.5),
        'c_conv_b': nrm(ks[14], (n_c, SSM_CONV_DIM), 0.02),
        'c_dt_bias': dt0 + jnp.log(-jnp.expm1(-dt0)),
        'c_a_log': jnp.log(jax.random.uniform(ks[15], (n_c, 2, SSM_HEADS), F32, 1.0, 16.0)),
        'c_d': 1.0 + 0.1 * jax.random.normal(ks[17], (n_c, SSM_HEADS), F32),
        'c_norm_g': gain(ks[18], (n_c, SSM_INNER)),
        'c_w_out': nrm(ks[19], (n_c, SSM_INNER + X_W, D_MODEL), (SSM_INNER + X_W) ** -0.5),
        'd_w_in': nrm(ks[20], (n_d, D_MODEL, D_IN_W), D_MODEL ** -0.5),
        'd_rpb': nrm(ks[21], (n_d, ATT_HEADS, 2 * NA_ROWS_MAX - 1, 2 * NA_COLS - 1), 0.1),
        'd_w_out': nrm(ks[22], (n_d, ATT_Q_W + X_W, D_MODEL), (ATT_Q_W + X_W) ** -0.5),
        'ffn_w_in': nrm(ks[23], (DEPTH, D_MODEL, 2 * D_FF), D_MODEL ** -0.5),
        'ffn_conv_w': nrm(ks[24], (DEPTH, FFN_CONV, D_FF), FFN_CONV ** -0.5),
        'ffn_conv_b': nrm(ks[25], (DEPTH, D_FF), 0.02),
        'ffn_w_out': nrm(ks[26], (DEPTH, D_FF, D_MODEL), D_FF ** -0.5),
    }

def second_block(x, mem, norm_g, mem_norm_g, w_mem_kv, a_w_in, a_sink, a_w_out,
              b_w_in, b_lb_logits, b_norm_g, b_w_out,
              c_w_in, c_conv_w, c_conv_b, c_dt_bias, c_a_log, c_d, c_norm_g, c_w_out,
              d_w_in, d_rpb, d_w_out, ffn_w_in, ffn_conv_w, ffn_conv_b, ffn_w_out):
    t = x.shape[1]
    pos = jnp.arange(t)
    mem_n = rmsnorm(mem, mem_norm_g)
    lb = hgrn_lower_bounds(b_lb_logits)
    h = x
    for layer in range(DEPTH):
        kind, slot = layer % N_MIXERS, layer // N_MIXERS
        u = rmsnorm(h, norm_g[layer, 0])
        mem_kv = mem_n @ w_mem_kv[layer]
        if kind == 0:
            y = mixer_window_attn(u, mem_kv, a_w_in[slot], a_sink[slot], a_w_out[slot], pos)
        elif kind == 1:
            y = mixer_hgrn2(u, mem_kv, b_w_in[slot], lb[0, layer], lb[1, layer], b_norm_g[slot], b_w_out[slot])
        elif kind == 2:
            y = mixer_mamba2(u, mem_kv, c_w_in[slot], c_conv_w[slot], c_conv_b[slot], c_dt_bias[slot],
                             c_a_log[slot], c_d[slot], c_norm_g[slot], c_w_out[slot])
        else:
            y = mixer_neighbourhood(u, mem_kv, d_w_in[slot], d_rpb[slot], d_w_out[slot])
        h = h + rmsnorm(y, norm_g[layer, 1])
        f = conv_ffn_2(rmsnorm(h, norm_g[layer, 2]), ffn_w_in[layer], ffn_conv_w[layer],
                     ffn_conv_b[layer], ffn_w_out[layer])
        h = h + rmsnorm(f, norm_g[layer, 3])
    return h


def setup_inputs(seed=0):
    out = dict(first_inputs(seed))
    for name, value in second_inputs(seed + 1).items():
        if name != "x":
            out[name + "_2"] = value
    return out


def reference(
    x, ln_g, ln_b, rel_bias, ev_w_in, ev_w_uk, ev_w_uv, ev_b_f, ev_w_o, od_w_in, od_sgu_g,
    od_sgu_w, od_sgu_b, od_conv_w, od_w_o, ffn_w_up, ffn_conv_w, ffn_w_down, mem_2, norm_g_2,
    mem_norm_g_2, w_mem_kv_2, a_w_in_2, a_sink_2, a_w_out_2, b_w_in_2, b_lb_logits_2,
    b_norm_g_2, b_w_out_2, c_w_in_2, c_conv_w_2, c_conv_b_2, c_dt_bias_2, c_a_log_2, c_d_2,
    c_norm_g_2, c_w_out_2, d_w_in_2, d_rpb_2, d_w_out_2, ffn_w_in_2, ffn_conv_w_2, ffn_conv_b_2,
    ffn_w_out_2,
):
    x = first_block(
        x, ln_g, ln_b, rel_bias, ev_w_in, ev_w_uk, ev_w_uv, ev_b_f, ev_w_o, od_w_in, od_sgu_g,
        od_sgu_w, od_sgu_b, od_conv_w, od_w_o, ffn_w_up, ffn_conv_w, ffn_w_down,
    )
    return second_block(
        x, mem_2, norm_g_2, mem_norm_g_2, w_mem_kv_2, a_w_in_2, a_sink_2, a_w_out_2, b_w_in_2,
        b_lb_logits_2, b_norm_g_2, b_w_out_2, c_w_in_2, c_conv_w_2, c_conv_b_2, c_dt_bias_2,
        c_a_log_2, c_d_2, c_norm_g_2, c_w_out_2, d_w_in_2, d_rpb_2, d_w_out_2, ffn_w_in_2,
        ffn_conv_w_2, ffn_conv_b_2, ffn_w_out_2,
    )


_drawn_inputs = setup_inputs


def setup_inputs(seed=0):
    import zlib

    import numpy as np

    out = dict(_drawn_inputs(seed))
    spreads = {}
    factors = {'od_sgu_g': 25.086,
     'a_sink_2': 8.0,
     'b_lb_logits_2': 8.0,
     'ffn_conv_b_2': 3.322,
     'od_sgu_b': 2.695}
    for name, (base, spread) in spreads.items():
        noise = np.random.default_rng([zlib.crc32(name.encode()), seed]).standard_normal(out[name].shape)
        drawn = base * np.exp(spread * noise) if base else spread * noise
        out[name] = jnp.asarray(drawn.astype(out[name].dtype))
    for name, factor in factors.items():
        out[name] = (out[name] * factor).astype(out[name].dtype)
    return out
```

```python
from contextlib import ExitStack

import numpy as np

import concourse.bass as bass
from concourse import mybir

F32 = mybir.dt.float32
F32R = mybir.dt.float32r
BF16 = mybir.dt.bfloat16
ALU = mybir.AluOpType
ACT = mybir.ActivationFunctionType
AX = mybir.AxisListType

ALPHA = 4.0 ** 0.25
LN_EPS = 1e-5
RMS_EPS = 1e-6
NEG = -1e30
TAKEN = -3e38
NRAW = 3
NSPLIT = 3
AHEAD = 2
ARENA = 14300


def schedule():
    s = []

    def add(name, n, w=2048, first=0):
        s.extend((name, i, w) for i in range(first, first + n))

    def ffn(name_up, name_down, layer, single):
        ups = [(name_up, layer * (22 if not single else 22) + j, 2048) for j in range(22)]
        for m in range(11):
            s.extend(ups[2 * m:2 * m + 2])
            if m:
                s.append((name_down, layer * 11 + m - 1, 2048))
        s.append((name_down, layer * 11 + 10, 2048))

    for l in range(2):
        add("mem_k", 2, first=2 * l)
        add("mem_v", 2, first=2 * l)
    add("ev_a", 7)
    add("ev_v", 2)
    add("ev_b", 2)
    add("ev_c", 1, 1024)
    add("ev_o", 4)
    ffn("up1", "down1", 0, False)
    add("od_v", 2)
    add("od_t", 8)
    add("od_o", 4)
    ffn("up1", "down1", 1, False)
    add("wa_k", 1)
    add("wa_v", 1)
    add("wa_q", 4)
    add("wa_x", 2)
    add("wa_o", 6)
    ffn("up2", "down2", 0, False)
    add("hg_v", 4)
    add("hg_t", 16)
    add("hg_x", 2)
    add("hg_o", 6)
    ffn("up2", "down2", 1, False)
    return s


CC = {}
_n = 0
for _name, _w in (("ident", 128), ("cmf", 128), ("tril", 128), ("m64", 256), ("ones", 256), ("m1", 512),
                  ("mbc", 64), ("cos", 256), ("sin", 256), ("rot", 128)):
    CC[_name] = (_n, _n + _w)
    _n += _w
NCC = _n
PC = {}
_n = 0
for _name, _w in (("ln", 64), ("rg", 32), ("memg", 8), ("fc1", 264), ("fc2", 132), ("fb2", 44), ("oc", 12),
                  ("bng", 8), ("lbl", 32), ("bf", 1), ("sink", 16), ("relb", 8)):
    PC[_name] = (_n, _n + _w)
    _n += _w
NPC = _n


class Engine:

    def __init__(self, key, eng, sems):
        self.key, self.eng, self.sems, self.n, self.seen = key, eng, sems, 0, {}

    def __call__(self, *tokens):
        need = {}
        stack = list(tokens)
        while stack:
            t = stack.pop()
            if t is None:
                continue
            if isinstance(t, list):
                stack.extend(t)
            else:
                need[t[0]] = max(need.get(t[0], 0), t[1])
        for key, value in sorted(need.items()):
            if self.seen.get(key, 0) < value:
                self.eng.wait_ge(self.sems[key], value)
                self.seen[key] = value
        return self.eng

    def done(self, instruction):
        self.n += 1
        instruction.then_inc(self.sems[self.key], 1)
        return (self.key, self.n)


class Slot:
    def __init__(self, t):
        self.t, self.free = t, []


class Ring:
    def __init__(self, tiles):
        self.slots, self.i = [x if isinstance(x, Slot) else Slot(x) for x in tiles], 0

    def take(self):
        s = self.slots[self.i % len(self.slots)]
        self.i += 1
        return s


def program(nc, T, out):
    with ExitStack() as ctx:
        sems = {}

        def sem(name):
            sems[name] = ctx.enter_context(nc.semaphore("s_" + name))

        def sb(name, shape, dt=F32):
            return ctx.enter_context(nc.sbuf_tensor(name, shape, dt))

        for k in "vagp":
            sem(k)
        V = Engine("v", nc.vector, sems)
        A = Engine("a", nc.scalar, sems)
        G = Engine("g", nc.gpsimd, sems)
        P = Engine("p", nc.tensor, sems)
        SP = Engine("sp", nc.sync, sems)
        dma_n = {}

        def dma(name, dst, src, *tokens):
            if name not in sems:
                sem(name)
                dma_n[name] = 0
            dma_n[name] += 16
            SP(*tokens).dma_start(dst, src).then_inc(sems[name], 16)
            return (name, dma_n[name])

        raw = [sb(f"raw{i}", [128, 2048]) for i in range(NRAW)]
        whi = [sb(f"whi{i}", [128, 2048], F32R) for i in range(NSPLIT)]
        wlo = [sb(f"wlo{i}", [128, 2048], F32R) for i in range(NSPLIT)]
        XS = sb("XS", [128, 8, 512], F32R)
        MS = sb("MS", [128, 12, 512], F32R)
        xn = sb("xn", [128, 2, 1024])
        yb = sb("yb", [128, 2, 1024])
        gb = sb("gb", [128, 2, 1024])
        cc = sb("cc", [128, NCC])
        pc = sb("pc", [128, NPC])
        cb = sb("cb", [128, 384], BF16)
        st = sb("st", [128, 64])
        lb = sb("lb", [128, 48])
        ar = sb("ar", [128, ARENA])
        banks = [Slot(ctx.enter_context(nc.psum_tensor(f"ps{i}", [128, 512], F32))) for i in range(8)]
        low, high = banks[0:4], Ring(banks[4:8])
        allb = Ring(banks)

        def C(name, rows=128):
            a, b = CC[name]
            return cc[0:rows, a:b]

        def col(name, i=0, rows=128):
            a = PC[name][0] + i
            return pc[0:rows, a:a + 1]

        ident = C("ident")
        identb, cmb, cmb2 = cb[:, 0:128], cb[:, 128:256], cb[:, 256:384]
        mhalf = st[:, 60:61]

        class Arena:
            def __init__(self):
                self.at = 0

            def __call__(self, n):
                a = self.at
                self.at += n
                assert self.at <= ARENA, self.at
                return ar[:, a:a + n]

        def fence():
            return [(e.key, e.n) for e in (V, A, G, P)]

        t_mem = dma("d_mem", xn[:, :, :], T["mem_2"].rearrange("a (t p) d -> p (a t) d", p=128))
        t_cc = dma("d_cc", cc[:, :], T["c_f32"])
        t_pc = dma("d_pc", pc[:, :], T["c_par"])
        t_cb = dma("d_cb", ar[:, 0:384], T["c_mask"])
        t_half = V.done(V().memset(mhalf, -0.5))
        t_cb = V.done(V(t_cb).tensor_copy(cb[:, :], ar[:, 0:384]))

        sched = schedule()

        class Stream:
            def __init__(self):
                self.pos = self.loaded = self.split_n = 0
                self.raw_free = [[] for _ in range(NRAW)]
                self.landed = {}
                self.ready = {}
                self.used = [[] for _ in range(NSPLIT)]

            def load(self):
                m = self.loaded
                if m >= len(sched):
                    return
                name, i, w = sched[m]
                r = m % NRAW
                self.landed[m] = dma(f"d_w{r}", raw[r][:, 0:w], T[name][i], self.raw_free[r])
                self.loaded += 1

            def split(self):
                m = self.split_n
                if m >= len(sched):
                    return
                w = sched[m][2]
                r, s = m % NRAW, m % NSPLIT
                a = w // 4 * 3
                th = A.done(A(self.landed[m], self.used[s]).activation(whi[s][:, 0:w], raw[r][:, 0:w], ACT.Copy))
                tg = G.done(G(th, self.landed[m], self.used[s]).tensor_tensor(
                    wlo[s][:, 0:a], raw[r][:, 0:a], whi[s][:, 0:a].bitcast(F32), ALU.subtract))
                tv = V.done(V(th, self.landed[m], self.used[s]).tensor_tensor(
                    wlo[s][:, a:w], raw[r][:, a:w], whi[s][:, a:w].bitcast(F32), ALU.subtract))
                self.raw_free[r] = [tg, tv]
                self.ready[m] = [th, tg, tv]
                self.split_n += 1
                self.load()

            def get(self, name, ahead=0):
                m = self.pos + ahead
                assert sched[m][0] == name, (sched[m], name)
                return whi[m % NSPLIT], wlo[m % NSPLIT], self.ready[m]

            def done(self, tok):
                self.used[self.pos % NSPLIT] = [tok]
                self.pos += 1
                self.split()

        W = Stream()
        for _ in range(NRAW):
            W.load()
        for _ in range(AHEAD):
            W.split()

        def split_to(hi, lo, src, *tokens):
            th = A.done(A(*tokens).activation(hi, src, ACT.Copy))
            return V.done(V(th, *tokens).tensor_tensor(lo, src, hi.bitcast(F32), ALU.subtract))

        def project_T(name, xs_ready, ring):
            hi, lo, ready = W.get(name)
            tiles = sched[W.pos][2] // 1024
            bank = ring.take()
            P(ready, xs_ready, bank.free)
            for i in range(tiles):
                o = bank.t[:, 256 * i:256 * i + 256]
                for k in range(8):
                    c = slice(1024 * i + 128 * k, 1024 * i + 128 * k + 128)
                    nc.tensor.matmul(o, hi[:, c], XS[:, k, 0:256], start=(k == 0), stop=False)
                    nc.tensor.matmul(o, hi[:, c], XS[:, k, 256:512], start=False, stop=False)
                    last = nc.tensor.matmul(o, lo[:, c], XS[:, k, 0:256], start=False, stop=(k == 7))
            tok = P.done(last)
            W.done(tok)
            return bank, tok

        def accumulate(name, S, ks, ready, n, accs, first, last, count=1):
            per = 2048 // n
            toks = []
            got = [W.get(name, i) for i in range(count)]
            for tt in range(2):
                for i, (hi, lo, wready) in enumerate(got):
                    P(wready)
                    for j in range(per):
                        k = ks[i * per + j]
                        P(ready[k])
                        sh = S[:, k, 128 * tt:128 * tt + 128]
                        sl = S[:, k, 256 + 128 * tt:384 + 128 * tt]
                        begin = first and i == 0 and j == 0
                        end = last and i == count - 1 and j == per - 1
                        for lhs, w in ((sh, hi), (sh, lo), (sl, hi)):
                            for h in range((n + 511) // 512):
                                acc = accs[tt][h]
                                if begin and lhs is sh and w is hi:
                                    P(acc.free)
                                c = min(n, 512)
                                ins = nc.tensor.matmul(acc.t[:, 0:c], lhs, w[:, n * j + c * h:n * j + c * h + c],
                                                       start=(begin and lhs is sh and w is hi),
                                                       stop=(end and lhs is sl))
                toks.append(P.done(ins))
            for _ in range(count):
                W.done(toks[-1])
            return toks

        def natural(name, S, ready, K, n, accs, hold=1):
            per = 2048 // n
            chunks = K // per
            for c in range(chunks - hold):
                accumulate(name, S, list(range(c * per, (c + 1) * per)), ready, n, accs, c == 0, False)
            c = chunks - hold
            return accumulate(name, S, list(range(c * per, K)), ready, n, accs, c == 0, True, hold)

        xf = Ring([sb(f"xf{i}", [128, 512]) for i in range(2)])

        def to_XS(tt, tok, g, b=None):
            toks = []
            for q in range(2):
                bank = high.take()
                P(tok, bank.free)
                for i in range(4):
                    k = 4 * q + i
                    last = nc.tensor.transpose(bank.t[:, 128 * i:128 * i + 128], yb[:, tt, 128 * k:128 * k + 128], ident)
                tp = P.done(last)
                x = xf.take()
                for i in range(4):
                    k = 4 * q + i
                    src, dst = bank.t[:, 128 * i:128 * i + 128], x.t[:, 128 * i:128 * i + 128]
                    if q == 0:
                        te = V.done(V(tp, x.free).tensor_scalar(dst, src, g(k), b(k) if b else None,
                                                                ALU.mult, ALU.add if b else ALU.bypass))
                    else:
                        te = A.done(A(tp, x.free).activation(dst, src, ACT.Identity, scale=g(k),
                                                             bias=b(k) if b else 0.0))
                bank.free = [te]
                xv = x.t[:, :].rearrange("p (k t) -> p k t", k=4)
                hi = XS[:, 4 * q:4 * q + 4, 128 * tt:128 * tt + 128]
                lo = XS[:, 4 * q:4 * q + 4, 256 + 128 * tt:384 + 128 * tt]
                t = split_to(hi, lo, xv, te)
                x.free = [t]
                toks.append(t)
            return toks

        def rstd_of(dst, src, scale, eps, tok):
            n = src.shape[1]
            t = V.done(V(tok).tensor_scalar(dst, src, scale, eps, ALU.mult, ALU.add))
            for i in range(n):
                t2 = G.done(G(t, t_half).tensor_tensor(dst[:, i:i + 1], dst[:, i:i + 1], mhalf, ALU.pow))
            return t2

        state = {"xn": [None, None], "yb": [[], []], "gb": []}

        def load_gb(src, rows):
            n = 1024 * rows
            ap = bass.AP(tensor=src.tensor, offset=src.offset, ap=[[0, 128], [1, n]])
            return dma("d_gb", gb[:, 0:rows, :].rearrange("p a d -> p (a d)"), ap, state["gb"])

        def layer_norm(accs, toks, idx):
            t_gb = load_gb(T["c_ln"][idx], 2)
            ready, users = [], []
            post = []
            for tt in range(2):
                o = 32 * tt
                for h in range(2):
                    c = slice(512 * h, 512 * h + 512)
                    t = V.done(V(toks[tt], state["xn"][tt], state["yb"][tt]).scalar_tensor_tensor(
                        yb[:, tt, c], xn[:, tt, c], ALPHA, accs[tt][h].t[:, :], ALU.mult, ALU.add))
                    accs[tt][h].free = [t]
                    t = V.done(V(t).bn_stats(st[:, o + 6 * h:o + 6 * h + 6], yb[:, tt, c]))
                t = V.done(V(t).bn_aggr(st[:, o + 12:o + 14], st[:, o:o + 12]))
                t = rstd_of(st[:, o + 14:o + 15], st[:, o + 13:o + 14], 1.0, LN_EPS, t)
                t = V.done(V(t).tensor_scalar(yb[:, tt, :], yb[:, tt, :], st[:, o + 12:o + 13], st[:, o + 14:o + 15],
                                              ALU.subtract, ALU.mult))
                ready += to_XS(tt, t, lambda k: col("ln", 16 * idx + k), lambda k: col("ln", 16 * idx + 8 + k))
                post.append(t)
            for tt in range(2):
                t = G.done(G(post[tt], t_gb).tensor_tensor(xn[:, tt, :], yb[:, tt, :], gb[:, 0, :], ALU.mult))
                t = G.done(G(t).tensor_tensor(xn[:, tt, :], xn[:, tt, :], gb[:, 1, :], ALU.add))
                state["xn"][tt] = t
                state["yb"][tt] = [t, ready[2 * tt:2 * tt + 2]]
                users.append(t)
            state["gb"] = users
            return ready

        def rms_to_XS(tt, tok, gain):
            o = 32 * tt
            t = A.done(A(tok, state["yb"][tt]).activation(yb[:, tt, :], xn[:, tt, :], ACT.Square,
                                                          accum_out=st[:, o + 20:o + 21]))
            t = rstd_of(st[:, o + 21:o + 22], st[:, o + 20:o + 21], 1.0 / 1024, RMS_EPS, t)
            t = V.done(V(t).tensor_scalar(yb[:, tt, :], xn[:, tt, :], st[:, o + 21:o + 22], None, ALU.mult))
            r = to_XS(tt, t, gain)
            state["yb"][tt] = [r]
            return r

        def residual_rms(accs, toks, idx, gain):
            t_gb = load_gb(T["c_rg"][idx], 1)
            ready, users = [], []
            for tt in range(2):
                o = 32 * tt
                sums = []
                for h in range(2):
                    sums.append(A.done(A(toks[tt], state["yb"][tt]).activation(
                        yb[:, tt, 512 * h:512 * h + 512], accs[tt][h].t[:, :], ACT.Square,
                        accum_out=st[:, o + 22 + h:o + 23 + h])))
                t = V.done(V(sums).tensor_tensor(st[:, o + 24:o + 25], st[:, o + 22:o + 23], st[:, o + 23:o + 24], ALU.add))
                t = rstd_of(st[:, o + 25:o + 26], st[:, o + 24:o + 25], 1.0 / 1024, RMS_EPS, t)
                for h in range(2):
                    c = slice(512 * h, 512 * h + 512)
                    t2 = V.done(V(t, t_gb, sums[h]).scalar_tensor_tensor(
                        yb[:, tt, c], accs[tt][h].t[:, :], st[:, o + 25:o + 26], gb[:, 0, c], ALU.mult, ALU.mult))
                    accs[tt][h].free = [t2]
                users.append(t2)
                t = V.done(V(t2, state["xn"][tt]).tensor_tensor(xn[:, tt, :], xn[:, tt, :], yb[:, tt, :], ALU.add))
                state["xn"][tt] = t
                state["yb"][tt] = [t]
                if gain:
                    ready += rms_to_XS(tt, t, gain)
            state["gb"] = users
            return ready

        def finish():
            t = dma("d_out", out.rearrange("a (t p) d -> p (a t) d", p=128), xn[:, :, :], state["xn"][0], state["xn"][1])
            SP(t)

        accs = [[low[0], low[1]], [low[2], low[3]]]

        def attend(heads, causal, Pr, PTr, nmr, ring):
            n = 384 if causal else 512
            segs = [(0, 128), (128, 384)] if causal else [(0, 256), (256, 512)]

            def soft(h):
                score, sink, _ = heads[h]
                bank = ring.take()
                P(bank.free)
                tok = score(bank.t)
                nm = nmr.take()
                V(tok, nm.free)
                if causal:
                    for i, (a, b) in enumerate(segs):
                        t = V.done(nc.vector.tensor_reduce(nm.t[:, i:i + 1], bank.t[:, a:b], AX.X, ALU.max, negate=True))
                else:
                    t = V.done(nc.vector.tensor_reduce(nm.t[:, 0:2], bank.t[:, :].rearrange("p (t s) -> p t s", t=2),
                                                       AX.X, ALU.max, negate=True))
                if sink is not None:
                    t = V.done(V(t).tensor_scalar(nm.t[:, 0:2], nm.t[:, 0:2], sink[1], None, ALU.min))
                p = Pr.take()
                A(t, p.free)
                ta = []
                for i, (a, b) in enumerate(segs):
                    ta.append(A.done(nc.scalar.activation(p.t[:, a:b], bank.t[:, a:b], ACT.Exp, bias=nm.t[:, i:i + 1],
                                                          accum_out=nm.t[:, 2 + i:3 + i])))
                bank.free = [ta[1]]
                if sink is not None:
                    te = A.done(A(t).activation(nm.t[:, 6:8], nm.t[:, 0:2], ACT.Exp, bias=sink[0]))
                    ta.append(V.done(V(te, ta).tensor_tensor(nm.t[:, 2:4], nm.t[:, 2:4], nm.t[:, 6:8], ALU.add)))
                t = V.done(V(ta).reciprocal(nm.t[:, 4:6], nm.t[:, 2:4]))
                tn = []
                for i, (a, b) in enumerate(segs):
                    tn.append(V.done(V(t, ta).tensor_scalar(p.t[:, a:b], p.t[:, a:b], nm.t[:, 4 + i:5 + i], None, ALU.mult)))
                nm.free = tn
                return p, tn

            def turn(h, p, tn):
                bank = ring.take()
                P(tn, bank.free)
                if causal:
                    pairs = [(0, 0), (128, 128), (256, 256)]
                else:
                    pairs = [(0, 0), (128, 256), (256, 128), (384, 384)]
                for a, b in pairs:
                    last = nc.tensor.transpose(bank.t[:, b:b + 128], p.t[:, a:a + 128], ident)
                tp = P.done(last)
                p.free = [tp]
                pt = PTr.take()
                if h % 2:
                    t = V.done(V(tp, pt.free).tensor_copy(pt.t[:, 0:n], bank.t[:, 0:n]))
                else:
                    t = A.done(A(tp, pt.free).activation(pt.t[:, 0:n], bank.t[:, 0:n], ACT.Copy))
                bank.free = [t]
                return pt, t

            H = len(heads)
            ps, pts = {}, {}
            for i in range(H + 3):
                if i < H:
                    ps[i] = soft(i)
                if 0 <= i - 2 < H:
                    pts[i - 2] = turn(i - 2, *ps[i - 2])
                if 0 <= i - 3 < H:
                    pt, t = pts[i - 3]
                    pt.free = [heads[i - 3][2](pt.t, t)]

        scr = nc.dram_tensor("scr_mem", (4, 128, 1024), F32, kind="Internal").ap()
        state["xn"] = [t_mem, t_mem]
        xs = []
        P(t_cc, t_cb)
        V(t_pc)
        A(t_pc, t_cb)
        for tt in range(2):
            xs += rms_to_XS(tt, t_mem, lambda k: col("memg", k))
        t_x = dma("d_x", xn[:, :, :], T["x"].rearrange("a (t p) d -> p (a t) d", p=128), state["yb"][0], state["yb"][1])
        A_ = Arena()
        kv = [A_(1024) for _ in range(4)]
        t_scr = []
        for l in range(2):
            tk = []
            for j in range(2):
                bank, tok = project_T("mem_k", xs, high)
                t = A.done(A(tok).activation(kv[2 * l][:, 512 * j:512 * j + 512], bank.t[:, :], ACT.Copy))
                bank.free = [t]
                tk.append(t)
            t_scr.append(dma(f"d_scr{2 * l}", scr[2 * l], kv[2 * l], tk))
            acc = [[low[2 * l]], [low[2 * l + 1]]]
            toks = natural("mem_v", XS, [xs] * 8, 8, 512, acc)
            tv = []
            for tt in range(2):
                t = V.done(V(toks[tt]).tensor_copy(kv[2 * l + 1][:, 512 * tt:512 * tt + 512], acc[tt][0].t[:, :]))
                acc[tt][0].free = [t]
                tv.append(t)
            t_scr.append(dma(f"d_scr{2 * l + 1}", scr[2 * l + 1], kv[2 * l + 1], tv))

        fz = [fence(), t_scr]
        A_ = Arena()
        onehot = A_(384)
        rb = A_(3072)
        skew = nc.dram_tensor("scr_bias", (8, 128 * 384), F32, kind="Internal").ap()
        t_oh = dma("d_oh", onehot[0:32, :], T["c_onehot"], fz)
        trb = []
        for h in range(8):
            bank = high.take()
            a = PC["relb"][0] + h
            tp = P.done(P(t_oh, t_pc, bank.free).matmul(bank.t[:, 0:384], pc[0:32, a:a + 1].to_broadcast([32, 128]),
                                                       onehot[0:32, :], start=True, stop=True))
            t = V.done(V(tp, fz).tensor_copy(rb[:, 384 * h:384 * h + 384], bank.t[:, 0:384]))
            bank.free = [t]
            trb.append(t)
        t_w = dma("d_skw", skew.rearrange("h (p n) -> p h n", n=384), rb.rearrange("p (h n) -> p h n", h=8), trb)

        state["xn"] = [t_x, t_x]
        xs = []
        for tt in range(2):
            t = A.done(A(t_x, state["yb"][tt]).activation(yb[:, tt, :], xn[:, tt, :], ACT.Copy))
            for q in range(2):
                bank = high.take()
                P(t, bank.free)
                for i in range(4):
                    k = 4 * q + i
                    last = nc.tensor.transpose(bank.t[:, 128 * i:128 * i + 128], yb[:, tt, 128 * k:128 * k + 128], ident)
                tp = P.done(last)
                bv = bank.t[:, :].rearrange("p (k t) -> p k t", k=4)
                t2 = split_to(XS[:, 4 * q:4 * q + 4, 128 * tt:128 * tt + 128],
                              XS[:, 4 * q:4 * q + 4, 256 + 128 * tt:384 + 128 * tt], bv, tp)
                bank.free = [t2]
                xs.append(t2)
            state["yb"][tt] = [tp]

        def even(xs):
            fz = [t_w, fence()]
            R = Arena()
            Bh, RH = R(2048), gb[:, :, :].rearrange("p a d -> p (a d)")
            L, FW, FZ, CT = R(256), R(256), R(256), R(256)
            QI, KI, QB, KB, QA, VB = R(1024), R(256), R(1024), R(1024), R(1024), R(1024)
            CN, WK, WV = R(256), R(512), R(512)
            S, WI, M8 = R(384), R(32), R(8)
            rr = Ring([R(384) for _ in range(2)])
            MB = R(192).bitcast(BF16)
            Pr = Ring([R(384) for _ in range(3)])
            PTr = Ring([R(384) for _ in range(2)])
            nmr = Ring([R(8) for _ in range(4)])
            QLr = Ring([R(256) for _ in range(2)])
            OAr = Ring([R(256) for _ in range(2)])
            t_bh = dma("d_bh", Bh.rearrange("p (h n) -> p h n", h=8),
                       bass.AP(tensor=skew.tensor, offset=127, ap=[[383, 128], [128 * 384, 8], [1, 256]]), fz)
            t_wk = dma("d_wk", WK, T["w_uk"], fz)
            t_wv = dma("d_wv", WV, T["w_uv"], fz)
            t0 = V.done(V(fz).memset(L, 0.0))
            t0 = V.done(V(t0).memset(L[32:40, :], 1.0))
            t0 = V.done(V(t0).memset(L[96:104, :], 1.0))
            t0 = V.done(V(t0).memset(RH, 0.0))
            ring = allb

            def out_of(bank, i, dst, tok, scale=1.0, rows=128):
                return A.done(A(tok, fz).activation(dst, bank.t[0:rows, 256 * i:256 * i + 256], ACT.Copy, scale=scale))

            bank, tok = project_T("ev_a", xs, ring)
            t_fw = out_of(bank, 0, FW, tok)
            t_ki = out_of(bank, 1, KI, tok)
            bank.free = [t_ki]
            t_qi = []
            for j in range(2):
                bank, tok = project_T("ev_a", xs, ring)
                t = A.done(A(tok, fz).activation(QI[:, 512 * j:512 * j + 512], bank.t[:, :], ACT.Copy, scale=0.125))
                bank.free = [t]
                t_qi.append(t)
            bank = ring.take()
            P(t_fw, bank.free)
            for tt in range(2):
                last = nc.tensor.transpose(bank.t[:, 16 * tt:16 * tt + 16], FW[0:16, 128 * tt:128 * tt + 128], ident[0:16, 0:16])
            t_fwt = P.done(last)
            t_wi = V.done(V(t_fwt, fz).tensor_scalar(WI, bank.t[:, 0:32], float(np.float32(8 ** -0.5)), None, ALU.mult))
            bank.free = [t_wi]
            ts = [None, None]
            segs = [(0, 128), (128, 384)]
            for h in range(8):
                bank = ring.take()
                P(t_qi[h // 4], t_ki, bank.free)
                q = slice(64 * (h % 2), 64 * (h % 2) + 64)
                for tt in range(2):
                    a, b = segs[tt]
                    c = 256 * (h // 2) + 128 * tt
                    last = nc.tensor.matmul(bank.t[:, a:b], QI[q, c:c + 128], KI[q, 0:b - a], start=True, stop=True)
                tp = P.done(last)
                r = rr.take()
                t = A.done(A(tp, r.free).activation(r.t[:, :], bank.t[:, 0:384], ACT.Relu))
                bank.free = [t]
                for tt in range(2):
                    a, b = segs[tt]
                    w = WI[:, 16 * tt + 8 + h:16 * tt + 9 + h]
                    if h == 0:
                        ts[tt] = V.done(V(t, t_wi).tensor_scalar(S[:, a:b], r.t[:, a:b], w, None, ALU.mult))
                    else:
                        ts[tt] = V.done(V(t, ts[tt]).scalar_tensor_tensor(S[:, a:b], r.t[:, a:b], w, S[:, a:b],
                                                                          ALU.mult, ALU.add))
                r.free = [ts[0], ts[1]]
            bank, tok = project_T("ev_a", xs, ring)
            t_ct = out_of(bank, 0, CT, tok)
            t_qb = [out_of(bank, 1, QB[:, 0:256], tok, 0.125)]
            bank.free = [t_qb[0]]
            t_kb = []
            for j in range(3):
                bank, tok = project_T("ev_a", xs, ring)
                t_kb.append(out_of(bank, 0, KB[:, 256 * j:256 * j + 256], tok))
                t_qb.append(out_of(bank, 1, QB[:, 256 * j + 256:256 * j + 512], tok, 0.125))
                bank.free = [t_qb[-1]]
            accv = [[ring.take()], [ring.take()]]
            toks = natural("ev_v", XS, [xs] * 8, 8, 512, accv)
            t_vb = []
            for tt in range(2):
                t = A.done(A(toks[tt]).activation(VB[:, 512 * tt:512 * tt + 512], accv[tt][0].t[:, :], ACT.Copy))
                accv[tt][0].free = [t]
                t_vb.append(t)
            bank, tok = project_T("ev_b", xs, ring)
            t_kb.append(out_of(bank, 0, KB[:, 768:1024], tok))
            t_qa = [out_of(bank, 1, QA[:, 0:256], tok)]
            bank.free = [t_qa[0]]

            z = slice(0, 104)
            tz = V.done(V(t_fw, t_pc).tensor_scalar(FZ[z, :], FW[z, :], col("bf", 0, 104), None, ALU.add))
            nc.scalar.preload_act_table_set("natural_log_exp_and_others")
            t = tab = A.done(A(tz, t_fwt).activation(FW[z, :], FZ[z, :], ACT.Abs))
            t = A.done(A(t).activation(FW[z, :], FW[z, :], ACT.Exp, scale=-1.0))
            t = A.done(A(t).activation(FW[z, :], FW[z, :], ACT.Ln, bias=1.0))
            tz = V.done(V(tab).tensor_scalar(FZ[z, :], FZ[z, :], 0.0, None, ALU.min))
            tz = V.done(V(t, tz).tensor_tensor(FZ[z, :], FZ[z, :], FW[z, :], ALU.subtract))
            tz = V.done(V(tz).tensor_tensor_scan(FW[z, :], C("ones", 104), FZ[z, :], 0.0, ALU.mult, ALU.add))
            rv = RH.rearrange("p (h t) -> p h t", h=8)
            t_cum = []
            for a in (0, 64):
                b = a + 32
                tl = V.done(V(tz, t0).tensor_copy(L[a:a + 8, :], FW[a:a + 8, :]))
                t1 = V.done(V(t0, t_cc).tensor_copy(rv[a:a + 8], ident[a:a + 8, a:a + 8].unsqueeze(2).to_broadcast([8, 8, 256])))
                tn = V.done(V(tz).tensor_scalar(FZ[b:b + 8, :], FW[b:b + 8, :], -1.0, None, ALU.mult))
                t2 = V.done(V(tn, t1).tensor_tensor(rv[b:b + 8], ident[b:b + 8, b:b + 8].unsqueeze(2).to_broadcast([8, 8, 256]),
                                                    FZ[b:b + 8, :].unsqueeze(1).to_broadcast([8, 8, 256]), ALU.mult))
                t_cum += [tl, t1, t2]

            outb = {}

            def b_score(h):
                q = slice(64 * (h % 2), 64 * (h % 2) + 64)
                g = slice(64 * (h % 2), 64 * (h % 2) + 40)

                def go(bt):
                    P(t_qb[h // 2], t_kb[h // 2], t_cum)
                    for tt in range(2):
                        a, b = segs[tt]
                        c = 256 * (h // 2)
                        o = bt[:, a:b]
                        nc.tensor.matmul(o, QB[q, c + 128 * tt:c + 128 * tt + 128], KB[q, c:c + b - a], start=True, stop=False)
                        nc.tensor.matmul(o, L[g, 128 * tt:128 * tt + 128], rv[g, h, 0:b - a], start=False, stop=False)
                        last = nc.tensor.matmul(bt[:, b - 128:b], identb, cmb, start=False, stop=True)
                    return P.done(last)
                return go

            def pair_out(h, chunk):
                if h % 2 == 0:
                    outb[0] = ring.take()
                    P(outb[0].free)
                return outb[0], slice(64 * (h % 2), 64 * (h % 2) + 64)

            def put(h, chunk, bank, tp):
                if h % 2:
                    t = split_to(MS[:, chunk, 0:256], MS[:, chunk, 256:512], bank.t[:, 0:256], tp)
                    bank.free = [t]
                    ms[chunk] = t

            def b_value(h):
                def go(pt, t):
                    bank, q = pair_out(h, 4 + h // 2)
                    P(t, t_vb)
                    v = slice(64 * h, 64 * h + 64)
                    nc.tensor.matmul(bank.t[q, 0:256], VB[:, v], pt[:, 0:256], start=True, stop=False)
                    tp = P.done(nc.tensor.matmul(bank.t[q, 128:256], VB[:, 512 + 64 * h:576 + 64 * h], pt[:, 256:384],
                                                 start=False, stop=True))
                    put(h, 4 + h // 2, bank, tp)
                    return tp
                return go

            ms = {}
            attend([(b_score(h), None, b_value(h)) for h in range(8)], True, Pr, PTr, nmr, ring)

            state["gb"] = [("p", P.n)]

            cmf = C("cmf")
            ts[0] = V.done(V(ts[0], t_cc).tensor_tensor(S[:, 0:128], S[:, 0:128], cmf, ALU.add))
            ts[1] = V.done(V(ts[1], t_cc).tensor_tensor(S[:, 256:384], S[:, 256:384], cmf, ALU.add))
            tm = ts[1]
            for tt in range(2):
                a, b = segs[tt]
                t = ts[tt]
                for _ in range(8):
                    tm = V.done(V(t, tm).max(M8, S[:, a:b]))
                    t = tm = V.done(V(tm).match_replace(S[:, a:b], M8, S[:, a:b], TAKEN))
            t = V.done(V(tm).tensor_scalar(S, S, -2e38, 1e30, ALU.is_lt, ALU.mult))
            t1 = V.done(V(t).tensor_scalar(MB[:, 128:256], S[:, 128:256], NEG, None, ALU.add))
            for a in (0, 256):
                t1 = V.done(V(t, fz).scalar_tensor_tensor(MB[:, a:a + 128], S[:, a:a + 128], NEG, cmb, ALU.add, ALU.add))
            t_mb = t1

            bank, tok = project_T("ev_b", xs, ring)
            t = A.done(A(tok).activation(QA[:, 256:768], bank.t[:, :], ACT.Copy))
            bank.free = [t]
            t_qa += [t, t]
            bank, tok = project_T("ev_c", xs, ring)
            t_qa.append(out_of(bank, 0, QA[:, 768:1024], tok))
            bank.free = [t_qa[-1]]
            bank = ring.take()
            P(t_ct, bank.free)
            for tt in range(2):
                last = nc.tensor.transpose(bank.t[:, 128 * tt:128 * tt + 128], CT[:, 128 * tt:128 * tt + 128], ident)
            tp = P.done(last)
            t_cn = V.done(V(tp).tensor_copy(CN, bank.t[:, 0:256]))
            bank.free = [t_cn]

            def a_score(h):
                q = slice(64 * (h % 2), 64 * (h % 2) + 64)

                def go(bt):
                    bank = ring.take()
                    c = 256 * (h // 2)
                    tp = P.done(P(t_qa[h // 2], t_wk, bank.free).matmul(
                        bank.t[:, 0:256], WK[q, 128 * (h // 2):128 * (h // 2) + 128], QA[q, c:c + 256], start=True, stop=True))
                    ql = QLr.take()
                    t = A.done(A(tp, ql.free).activation(ql.t, bank.t[:, 0:256], ACT.Copy, scale=0.125))
                    bank.free = [t]
                    P(t, t_ct, t_bh, t_mb)
                    for tt in range(2):
                        a, b = segs[tt]
                        o = bt[:, a:b]
                        nc.tensor.matmul(o, ql.t[:, 128 * tt:128 * tt + 128], CT[:, 0:b - a], start=True, stop=False)
                        nc.tensor.matmul(o, ident, Bh[:, 256 * h + 128 - 128 * tt:256 * h + 256], start=False, stop=False)
                        last = nc.tensor.matmul(o, identb, MB[:, a:b], start=False, stop=True)
                    tp = P.done(last)
                    ql.free = [tp]
                    return tp
                return go

            def a_value(h):
                def go(pt, t):
                    bank = ring.take()
                    P(t, t_cn, bank.free)
                    nc.tensor.matmul(bank.t[:, 0:256], CN[:, 0:128], pt[:, 0:256], start=True, stop=False)
                    tp = P.done(nc.tensor.matmul(bank.t[:, 128:256], CN[:, 128:256], pt[:, 256:384], start=False, stop=True))
                    oa = OAr.take()
                    t = V.done(V(tp, oa.free).tensor_copy(oa.t, bank.t[:, 0:256]))
                    bank.free = [t]
                    b2, q = pair_out(h, h // 2)
                    t2 = P.done(P(t, t_wv).matmul(b2.t[q, 0:256], WV[:, 64 * h:64 * h + 64], oa.t, start=True, stop=True))
                    oa.free = [t2]
                    put(h, h // 2, b2, t2)
                    return tp
                return go

            attend([(a_score(h), None, a_value(h)) for h in range(8)], True, Pr, PTr, nmr, ring)
            return natural("ev_o", MS, ms, 8, 1024, accs, 2)

        def ffn(xs, layer, kind):
            fz = fence()
            R = Arena()
            hbr = [Slot(R(520)) for _ in range(2)]
            gr = Ring([R(512) for _ in range(3)])
            hr = Ring([R(256) for _ in range(3)])
            for s in hbr:
                t = V.done(V(fz).memset(s.t[:, 0:2], 0.0))
                t = V.done(V(fz).memset(s.t[:, 258:262], 0.0))
                s.free = [t]
            hbr = Ring(hbr)
            up, down = ("up1", "down1") if kind == 1 else ("up2", "down2")
            hs = {}

            def one(j):
                bank, tok = project_T(up, xs, high)
                hb, g, h = hbr.take(), gr.take(), hr.take()
                if kind == 1:
                    v = hb.t.rearrange("p (a n) -> p a n", a=2)
                    w = [[col("fc1", 132 * layer + 66 * a + 3 * j + i) for i in range(3)] for a in range(2)]
                    tc = A.done(A(tok, hb.free, fz).activation(
                        v[:, :, 2:258], bank.t[:, :].rearrange("p (a n) -> p a n", a=2), ACT.Copy))
                    ts = []
                    for a in range(2):
                        o = g.t[:, 256 * a:256 * a + 256]
                        t = A.done(A(tc, g.free).activation(o, bank.t[:, 256 * a:256 * a + 256], ACT.Copy, scale=w[a][2]))
                        bank.free = [t]
                        t = V.done(V(t, tc).scalar_tensor_tensor(o, v[:, a, 1:257], w[a][1], o, ALU.mult, ALU.add))
                        t = V.done(V(t).scalar_tensor_tensor(o, v[:, a, 0:256], w[a][0], o, ALU.mult, ALU.add))
                        ts.append(t)
                    hb.free = [ts[1]]
                    t = A.done(A(ts[0], h.free).activation(h.t, g.t[:, 0:256], ACT.Silu))
                    t = V.done(V(t, ts[1]).tensor_tensor(h.t, h.t, g.t[:, 256:512], ALU.mult))
                    g.free = [t]
                else:
                    w = [col("fc2", 66 * layer + 3 * j + i) for i in range(3)]
                    o = g.t[:, 0:256]
                    tc = A.done(A(tok, hb.free, fz).activation(hb.t[:, 2:258], bank.t[:, 0:256], ACT.Copy))
                    t = A.done(A(tc, g.free).activation(o, bank.t[:, 0:256], ACT.Identity, scale=w[1],
                                                        bias=col("fb2", 22 * layer + j)))
                    tg = t
                    t = V.done(V(t, tc).scalar_tensor_tensor(o, hb.t[:, 1:257], w[0], o, ALU.mult, ALU.add))
                    t = V.done(V(t).scalar_tensor_tensor(o, hb.t[:, 3:259], w[2], o, ALU.mult, ALU.add))
                    hb.free = [t]
                    t = A.done(A(t, h.free).activation(h.t, o, ACT.Gelu_apprx_tanh))
                    g.free = [t]
                    t = V.done(V(t, tg).tensor_tensor(h.t, h.t, bank.t[:, 256:512], ALU.mult))
                    bank.free = [t]
                k = j % 6
                hs[j] = split_to(MS[:, k, 0:256], MS[:, k, 256:512], h.t, t, fz)
                h.free = [hs[j]]

            def down_of(m, last=False):
                ready = {2 * m % 6: hs[2 * m], (2 * m + 1) % 6: hs[2 * m + 1]}
                ks = [2 * m % 6, (2 * m + 1) % 6]
                return accumulate(down, MS, ks, ready, 1024, accs, m == 0, last)

            for m in range(11):
                one(2 * m)
                one(2 * m + 1)
                if m:
                    down_of(m - 1)
            return down_of(10, True)

        def odd(xs):
            fz = fence()
            R = Arena()
            VG, XC = R(1024), R(1024)
            GN, SW, SB = R(512), R(1024), R(128)
            S1, S2 = R(16), R(16)
            U = R(1024)
            gcr = Ring([R(256) for _ in range(2)])
            zr = [Slot(R(260)) for _ in range(4)]
            yr = [R(256) for _ in range(4)]
            xr = Ring([R(256) for _ in range(2)])
            t_gn = dma("d_gn", GN, bass.AP(tensor=T["od_sgu_g"].tensor, offset=0, ap=[[0, 128], [1, 512]]), fz)
            t_sw = dma("d_sw", SW, T["sgu_w"], fz)
            t_sb = dma("d_sb", SB[0:8, :], T["od_sgu_b"][0], fz)
            tm = V.done(V(t_sw).tensor_tensor(SW.rearrange("p (g t) -> p g t", g=8), SW.rearrange("p (g t) -> p g t", g=8),
                                              C("tril").unsqueeze(1).to_broadcast([128, 8, 128]), ALU.mult))
            tz = []
            for s in zr:
                tz.append(V.done(V(fz).memset(s.t[:, 0:2], 0.0)))
            acc = [[low[0]], [low[1]]]
            toks = natural("od_v", XS, [xs] * 8, 8, 512, acc)
            tg = []
            for tt in range(2):
                t = A.done(A(toks[tt], fz).activation(VG[:, 512 * tt:512 * tt + 512], acc[tt][0].t[:, :], ACT.Gelu_apprx_tanh))
                acc[tt][0].free = [t]
                tg.append(t)
            v3 = VG.rearrange("p (g d) -> p g d", d=64)
            x3 = XC.rearrange("p (g d) -> p g d", d=64)
            t = V.done(V(tg).tensor_reduce(S1, v3, AX.X, ALU.add))
            t = V.done(V(t).tensor_scalar(S1, S1, 1.0 / 64, None, ALU.mult))
            t = V.done(V(t).tensor_tensor(v3, v3, S1.unsqueeze(2).to_broadcast([128, 16, 64]), ALU.subtract))
            ta = A.done(A(t, fz).activation(XC, VG, ACT.Square))
            t = V.done(V(ta).tensor_reduce(S2, x3, AX.X, ALU.add))
            t = V.done(V(t).tensor_scalar(S2, S2, 1.0 / 64, LN_EPS, ALU.mult, ALU.add))
            t = G.done(G(t, t_half).tensor_tensor(S2, S2, mhalf.to_broadcast([128, 16]), ALU.pow))
            t = V.done(V(t).tensor_tensor(x3, v3, S2.unsqueeze(2).to_broadcast([128, 16, 64]), ALU.mult))
            t_vn = V.done(V(t, t_gn).tensor_tensor(XC.rearrange("p (t d) -> p t d", t=2), XC.rearrange("p (t d) -> p t d", t=2),
                                                   GN.unsqueeze(1).to_broadcast([128, 2, 512]), ALU.mult))
            tu = []
            for j in range(2):
                bank, tok = project_T("od_t", xs, high)
                t = A.done(A(tok, fz).activation(U[:, 512 * j:512 * j + 512], bank.t[:, :], ACT.Gelu_apprx_tanh))
                bank.free = [t]
                tu += [t, t]
            ty = []
            for i in range(4):
                bank, tok = project_T("od_t", xs, high)
                gc = gcr.take()
                w = [col("oc", 3 * i + k) for k in range(3)]
                t = A.done(A(tok, gc.free, fz).activation(gc.t, bank.t[:, 0:256], ACT.Copy))
                zb, y = zr[i].t, yr[i]
                t = V.done(V(t, tz[i]).tensor_tensor(zb[:, 2:258], gc.t, bank.t[:, 256:512], ALU.mult))
                bank.free = gc.free = [t]
                t = V.done(V(t, fz).tensor_scalar(y, zb[:, 2:258], w[2], None, ALU.mult))
                t = V.done(V(t).scalar_tensor_tensor(y, zb[:, 1:257], w[1], y, ALU.mult, ALU.add))
                t = V.done(V(t).scalar_tensor_tensor(y, zb[:, 0:256], w[0], y, ALU.mult, ALU.add))
                ty.append(t)
            ms = {}
            for c in range(4):
                bank = high.take()
                P(t_vn, tm, t_sb, t_cc, bank.free)
                for g in (2 * c, 2 * c + 1):
                    q = slice(64 * (g % 2), 64 * (g % 2) + 64)
                    for tt in range(2):
                        o = bank.t[q, 128 * tt:128 * tt + 128]
                        nc.tensor.matmul(o, XC[:, 512 * tt + 64 * g:512 * tt + 64 * g + 64], SW[:, 128 * g:128 * g + 128],
                                         start=True, stop=False)
                        last = nc.tensor.matmul(o, ident[0:8, g:g + 1].to_broadcast([8, 64]), SB[0:8, :], start=False, stop=True)
                tp = P.done(last)
                x = xr.take()
                t = V.done(V(tp, tu[c], x.free).tensor_tensor(x.t, U[:, 256 * c:256 * c + 256], bank.t[:, 0:256], ALU.mult))
                bank.free = [t]
                ms[c] = split_to(MS[:, c, 0:256], MS[:, c, 256:512], x.t, t)
                x.free = [ms[c]]
            for j in range(2):
                bank, tok = project_T("od_t", xs, high)
                for i in range(2):
                    c = 2 * j + i
                    x = xr.take()
                    t = V.done(V(tok, ty[c], x.free).tensor_tensor(x.t, yr[c], bank.t[:, 256 * i:256 * i + 256], ALU.mult))
                    bank.free = [t]
                    ms[4 + c] = split_to(MS[:, 4 + c, 0:256], MS[:, 4 + c, 256:512], x.t, t)
                    x.free = [ms[4 + c]]
            return natural("od_o", MS, ms, 8, 1024, accs, 2)

        def cross_heads(R, name, xs, layer, fz, ring, ms):
            MK, MV, XQ = R(1024), R(1024), R(1024)
            t_mk = dma(f"d_mk{layer}", MK, scr[2 * layer], fz, t_scr)
            t_mv = dma(f"d_mv{layer}", MV, scr[2 * layer + 1], fz, t_scr)
            tq = []
            for j in range(2):
                bank, tok = project_T(name, xs, ring)
                t = A.done(A(tok, fz).activation(XQ[:, 512 * j:512 * j + 512], bank.t[:, :], ACT.Copy,
                                                 scale=float(np.float32(128 ** -0.5))))
                bank.free = [t]
                tq.append(t)

            def score(h):
                def go(bt):
                    P(tq[h // 2], t_mk)
                    for tt in range(2):
                        c = 256 * h + 128 * tt
                        last = nc.tensor.matmul(bt[:, 256 * tt:256 * tt + 256], XQ[:, c:c + 128], MK[:, 256 * h:256 * h + 256],
                                                start=True, stop=True)
                    return P.done(last)
                return go

            def value(h):
                def go(pt, t):
                    bank = ring.take()
                    P(t, t_mv, bank.free)
                    for s in range(2):
                        last = nc.tensor.matmul(bank.t[:, 0:256], MV[:, 512 * s + 128 * h:512 * s + 128 * h + 128],
                                                pt[:, 256 * s:256 * s + 256], start=(s == 0), stop=(s == 1))
                    tp = P.done(last)
                    t = split_to(MS[:, 8 + h, 0:256], MS[:, 8 + h, 256:512], bank.t[:, 0:256], tp)
                    bank.free = [t]
                    ms[8 + h] = t
                    return tp
                return go

            return [(score(h), None, value(h)) for h in range(4)]

        def window(xs):
            fz = fence()
            R = Arena()
            KR, QR, VN = R(512), R(2048), R(512)
            qr = Ring([R(512) for _ in range(2)])
            tr = Ring([R(512) for _ in range(2)])
            Pr = Ring([R(512) for _ in range(3)])
            PTr = Ring([R(512) for _ in range(2)])
            nmr = Ring([R(8) for _ in range(4)])
            NS = R(16)
            ring = allb
            a, b = PC["sink"]
            t_ns = V.done(V(t_pc, fz).tensor_scalar(NS, pc[:, a:b], -1.0, None, ALU.mult))

            def rope(dst, bank, tok, scale):
                q = qr.take()
                t = A.done(A(tok, q.free, fz).activation(q.t, bank.t[:, :], ACT.Copy, scale=scale))
                bank.free = [t]
                rb = ring.take()
                tp = P.done(P(t, rb.free).matmul(rb.t[:, :], C("rot"), q.t, start=True, stop=True))
                x = tr.take()
                v2 = lambda ap: ap.rearrange("p (a n) -> p a n", a=2)
                bc = lambda name: C(name).unsqueeze(1).to_broadcast([128, 2, 256])
                t1 = V.done(V(tp, x.free, fz).tensor_tensor(v2(x.t), v2(rb.t[:, :]), bc("sin"), ALU.mult))
                rb.free = [t1]
                t2 = V.done(V(t, fz).tensor_tensor(v2(dst), v2(q.t), bc("cos"), ALU.mult))
                t3 = V.done(V(t1, t2).tensor_tensor(dst, dst, x.t, ALU.add))
                x.free = [t3]
                q.free = [t3]
                return t3

            bank, tok = project_T("wa_k", xs, ring)
            tk = rope(KR, bank, tok, 1.0)
            accv = [[ring.take()], [ring.take()]]
            toks = natural("wa_v", XS, [xs] * 8, 8, 256, accv)
            tv = []
            for tt in range(2):
                t = A.done(A(toks[tt], fz).activation(VN[:, 256 * tt:256 * tt + 256], accv[tt][0].t[:, 0:256], ACT.Copy))
                accv[tt][0].free = [t]
                tv.append(t)
            tq = []
            for j in range(4):
                bank, tok = project_T("wa_q", xs, ring)
                t = rope(QR[:, 512 * j:512 * j + 512], bank, tok, 0.125)
                tq += [t, t]
            ms = {}
            outb = {}

            def score(c, r):
                q = slice(64 * r, 64 * r + 64)

                def go(bt):
                    P(tq[c], tk, t_cb)
                    kc = 256 * (c // 4)
                    for tt in range(2):
                        nc.tensor.matmul(bt[:, 256 * tt:256 * tt + 256], QR[q, 256 * c + 128 * tt:256 * c + 128 * tt + 128],
                                         KR[q, kc:kc + 256], start=True, stop=False)
                        o = bt[:, 128:256] if tt == 0 else bt[:, 256:384]
                        last = nc.tensor.matmul(o, identb, cmb if tt == 0 else cmb2, start=False, stop=True)
                    return P.done(last)
                return go

            def value(c, r):
                kvh = 2 * (c // 4) + r

                def go(pt, t):
                    if r == 0:
                        outb[0] = ring.take()
                        P(outb[0].free)
                    bank = outb[0]
                    q = slice(64 * r, 64 * r + 64)
                    P(t, tv)
                    for s in range(2):
                        last = nc.tensor.matmul(bank.t[q, 0:256], VN[:, 256 * s + 64 * kvh:256 * s + 64 * kvh + 64],
                                                pt[:, 256 * s:256 * s + 256], start=(s == 0), stop=(s == 1))
                    tp = P.done(last)
                    if r:
                        t = split_to(MS[:, c, 0:256], MS[:, c, 256:512], bank.t[:, 0:256], tp)
                        bank.free = [t]
                        ms[c] = t
                    return tp
                return go

            V(t_ns)
            A(t_ns)
            heads = []
            for c in range(8):
                for r in range(2):
                    h = (c % 4) + 4 * r + 8 * (c // 4)
                    heads.append((score(c, r), (col("sink", h), NS[:, h:h + 1]), value(c, r)))
            attend(heads, False, Pr, PTr, nmr, ring)
            heads = cross_heads(R, "wa_x", xs, 0, fz, ring, ms)
            attend(heads, False, Pr, PTr, nmr, ring)
            return natural("wa_o", MS, ms, 12, 1024, accs, 2)

        def hgrn(xs):
            fz = fence()
            R = Arena()
            VN = yb
            SGr = Ring([R(1024) for _ in range(2)])
            FF, KK, LF, CS = R(512), R(512), R(514), R(1024)
            E0 = R(512)
            QQ = R(256)
            GTr = Ring([R(256) for _ in range(2)])
            X0r = Ring([R(1024) for _ in range(2)])
            X1r = Ring([R(1536) for _ in range(2)])
            STr = Ring([R(512) for _ in range(2)])
            ONr = Ring([R(256) for _ in range(2)])
            UD = R(64)
            DD = gb[:, :, :].rearrange("p a d -> p (a d)")
            base = R.at
            stat = Ring([st[:, 32 * i:32 * i + 8] for i in range(2)])
            t = V.done(V(fz).memset(LF[:, 0:1], 0.0))
            t_lf = V.done(V(fz).memset(LF[:, 257:258], 0.0))
            lo0 = PC["lbl"][0]
            l0, l1 = pc[:, lo0:lo0 + 16], pc[:, lo0 + 16:lo0 + 32]
            m, e0, e1 = lb[:, 0:16], lb[:, 16:32], lb[:, 32:48]
            t = V.done(V(t_pc, fz).tensor_tensor(m, l0, l1, ALU.max))
            t1 = V.done(V(t).tensor_tensor(e0, l0, m, ALU.subtract))
            t2 = V.done(V(t).tensor_tensor(e1, l1, m, ALU.subtract))
            t = A.done(A(t1, t2).activation(lb[:, 16:48], lb[:, 16:48], ACT.Exp))
            t = V.done(V(t).tensor_tensor(m, e0, e1, ALU.add))
            t = V.done(V(t).reciprocal(m, m))
            t1 = V.done(V(t).tensor_tensor(e0, e0, m, ALU.mult))
            t2 = V.done(V(t).tensor_tensor(e1, e1, m, ALU.mult))
            t = V.done(V(t1, t2).tensor_tensor(m, e0, e1, ALU.add))
            t = V.done(V(t).tensor_tensor(m, m, e0, ALU.subtract))
            t_lb = V.done(V(t).tensor_scalar(e0, m, -1.0, 1.0, ALU.mult, ALU.add))
            vacc = [[low[0], low[1]], [low[2], low[3]]]
            toks = natural("hg_v", XS, [xs] * 8, 8, 1024, vacc)
            tv = []
            for tt in range(2):
                for h in range(2):
                    t = A.done(A(toks[tt], fz, state["yb"][tt]).activation(
                        VN[:, tt, 512 * h:512 * h + 512], vacc[tt][h].t[:, :], ACT.Copy))
                    vacc[tt][h].free = [t]
                    tv.append(t)
            ring = allb
            free = {"FF": [], "KK": [], "LF": [t_lf], "CS": [], "E0": [], "QQ": [], "DD": [state["gb"]], "UD": []}
            D4 = DD.rearrange("p (l d t) -> p l d t", l=4, d=2)
            C3 = CS.rearrange("p (k d t) -> p k d t", k=2, d=2)
            ms = {}

            def gates(h):
                bz, tz = project_T("hg_t", xs, ring)
                bq, tq = project_T("hg_t", xs, ring)
                sg, gt = SGr.take(), GTr.take()
                ta = A.done(A(tz, sg.free, fz).activation(sg.t[:, 0:512], bz.t[:, :], ACT.Sigmoid))
                bz.free = [ta]
                tb = A.done(A(tq).activation(sg.t[:, 512:1024], bq.t[:, :], ACT.Sigmoid))
                t_q = V.done(V(tb, free["QQ"]).tensor_tensor(QQ, sg.t[:, 512:768], bq.t[:, 0:256], ALU.mult))
                t_g = V.done(V(tb, gt.free).tensor_tensor(gt.t, sg.t[:, 768:1024], bq.t[:, 256:512], ALU.mult))
                bq.free = [t_g]
                for d in range(2):
                    o = 8 * d + h
                    tf = V.done(V(ta, t_lb, free["FF"]).tensor_scalar(
                        FF[:, 256 * d:256 * d + 256], sg.t[:, 256 * d:256 * d + 256], e0[:, o:o + 1], m[:, o:o + 1],
                        ALU.mult, ALU.add))
                sg.free = [tf, t_g]
                tk = V.done(V(tf, free["KK"]).tensor_scalar(KK, FF, -1.0, 1.0, ALU.mult, ALU.add))
                lf = LF.rearrange("p (d t) -> p d t", d=2)
                tl = A.done(A(tf, free["LF"]).activation(lf[:, :, 1:257], FF.rearrange("p (d t) -> p d t", d=2), ACT.Ln))
                free["FF"] = [tl, tk]
                V(tl, free["CS"], fz)
                for k, mask in ((0, C("m64")), (1, C("ones"))):
                    nc_v = nc.vector
                    tc = V.done(nc_v.tensor_tensor_scan(C3[:, k, 0, :], mask, lf[:, 0, 1:257], 0.0, ALU.mult, ALU.add))
                    tc = V.done(nc_v.tensor_tensor_scan(C3[:, k, 1, :], lf[:, 1, 0:256], mask, 0.0, ALU.add, ALU.mult))
                free["LF"] = [tc]
                V(tc, free["DD"])
                for lev in range(4):
                    n = 32 << lev
                    nb = 256 // n
                    for d in range(2):
                        src = C3[:, lev // 2, d, :].rearrange("p (b n) -> p b n", n=n)
                        dst = D4[:, lev, d, :].rearrange("p (b n) -> p b n", n=n)
                        mid = n // 2 - 1 + d
                        td = V.done(nc.vector.tensor_tensor(dst, src, src[:, :, mid:mid + 1].to_broadcast([128, nb, n]),
                                                            ALU.subtract))
                free["CS"] = [td]
                tn = A.done(A(td).activation(DD[:, 512:2048], DD[:, 512:2048], ACT.Abs))
                te1 = A.done(A(td, free["E0"]).activation(E0, DD[:, 0:512], ACT.Exp, scale=-1.0))
                te2 = A.done(A(te1).activation(DD[:, 0:512], DD[:, 0:512], ACT.Exp))
                te3 = A.done(A(tn).activation(DD[:, 512:2048], DD[:, 512:2048], ACT.Exp, scale=-1.0))
                x0, x1 = X0r.take(), X1r.take()
                V(te2, t_q, tk, x0.free, fz)
                nc_v = nc.vector
                V.done(nc_v.tensor_tensor(x0.t[:, 0:256], QQ, DD[:, 0:256], ALU.mult))
                V.done(nc_v.tensor_tensor(x0.t[:, 256:512], KK[:, 0:256], E0[:, 0:256], ALU.mult))
                V.done(nc_v.tensor_tensor(x0.t[:, 512:768], QQ, E0[:, 256:512], ALU.mult))
                t0 = V.done(nc_v.tensor_tensor(x0.t[:, 768:1024], KK[:, 256:512], DD[:, 256:512], ALU.mult))
                free["E0"] = [t0]
                V(te3, x1.free)
                for lev in range(1, 4):
                    half = 16 << lev
                    for d in range(2):
                        v = lambda ap: ap.rearrange("p (b s n) -> p b s n", s=2, n=half)
                        dst = v(x1.t[:, 512 * (lev - 1) + 256 * d:512 * (lev - 1) + 256 * d + 256])
                        e = v(D4[:, lev, d, :])
                        kk, qq = v(KK[:, 256 * d:256 * d + 256]), v(QQ)
                        V.done(nc_v.tensor_tensor(dst[:, :, d, :], kk[:, :, d, :], e[:, :, d, :], ALU.mult))
                        t1 = V.done(nc_v.tensor_tensor(dst[:, :, 1 - d, :], qq[:, :, 1 - d, :], e[:, :, 1 - d, :], ALU.mult))
                free["DD"] = free["KK"] = free["QQ"] = [t1]
                return x0, x1, gt, t1

            def mix(h, x0, x1, gt, tx):
                main, diag = ring.take(), ring.take()
                P(tx, main.free, diag.free)
                mm = nc.tensor.matmul
                qf, kf, qb, kb = (x0.t[:, 256 * i:256 * i + 256] for i in range(4))
                for tile in range(2):
                    for i in range(4):
                        o = 128 * tile + 32 * i
                        r = slice(32 * i, 32 * i + 32)
                        mm(main.t[r, 256 * tile + o:256 * tile + o + 32], kf[:, o:o + 32], qf[:, o:o + 32], start=True, stop=True)
                        mm(diag.t[r, 32 * tile:32 * tile + 32], kb[:, o:o + 32], qb[:, o:o + 32], start=True, stop=True)
                for lev in range(1, 4):
                    half = 16 << lev
                    xf_ = x1.t[:, 512 * (lev - 1):512 * (lev - 1) + 256]
                    xb_ = x1.t[:, 512 * (lev - 1) + 256:512 * lev]
                    for o in range(0, 256, 2 * half):
                        L_, R_ = slice(o, o + half), slice(o + half, o + 2 * half)
                        for x, ks, qs in ((xf_, L_, R_), (xb_, R_, L_)):
                            tile, r = ks.start // 128, ks.start % 128
                            last = mm(main.t[r:r + half, 256 * tile + qs.start:256 * tile + qs.stop], x[:, ks], x[:, qs],
                                      start=True, stop=True)
                tp = P.done(last)
                x0.free = [tp]
                x1.free = [tp]
                s = STr.take()
                t1 = V.done(V(tp, s.free, fz).tensor_tensor(s.t, main.t[:, :], C("m1"), ALU.mult))
                main.free = [t1]
                t2 = V.done(V(tp, free["UD"]).tensor_tensor(UD, diag.t[:, 0:64], C("mbc"), ALU.mult))
                diag.free = [t2]
                V(t1, t2)
                for i in range(4):
                    sv = s.t[32 * i:32 * i + 32, :]
                    ap = bass.AP(tensor=sv.tensor, offset=sv.offset + 32 * i, ap=[list(sv.ap[0]), [384, 2], [1, 32]])
                    uv = UD[32 * i:32 * i + 32, :].rearrange("p (a n) -> p a n", a=2)
                    ts = V.done(nc.vector.tensor_tensor(ap, ap, uv, ALU.add))
                free["UD"] = [ts]
                bank = ring.take()
                P(ts, tv, bank.free)
                for tt in range(2):
                    for sb_ in range(2):
                        last = mm(bank.t[:, 128 * tt:128 * tt + 128], s.t[:, 256 * sb_ + 128 * tt:256 * sb_ + 128 * tt + 128],
                                  VN[:, sb_, 128 * h:128 * h + 128], start=(sb_ == 0), stop=(sb_ == 1))
                tp = P.done(last)
                s.free = [tp]
                on, sc = ONr.take(), stat.take()
                tq = []
                for tt in range(2):
                    tq.append(A.done(A(tp, on.free, sc.free, fz).activation(
                        on.t[:, 128 * tt:128 * tt + 128], bank.t[:, 128 * tt:128 * tt + 128], ACT.Square,
                        accum_out=sc.t[:, tt:tt + 1])))
                t = rstd_of(sc.t[:, 2:4], sc.t[:, 0:2], 1.0 / 128, RMS_EPS, tq)
                for tt in range(2):
                    to = V.done(V(t, tq).tensor_scalar(on.t[:, 128 * tt:128 * tt + 128], bank.t[:, 128 * tt:128 * tt + 128],
                                                       sc.t[:, 2 + tt:3 + tt], None, ALU.mult))
                sc.free = [to]
                bank.free = [to]
                b2 = ring.take()
                P(to, b2.free)
                for tt in range(2):
                    last = nc.tensor.transpose(b2.t[:, 128 * tt:128 * tt + 128], on.t[:, 128 * tt:128 * tt + 128], ident)
                tp = P.done(last)
                t = V.done(V(tp).scalar_tensor_tensor(on.t, b2.t[:, 0:256], col("bng", h), gt.t, ALU.mult, ALU.mult))
                b2.free = [t]
                gt.free = [t]
                ms[h] = split_to(MS[:, h, 0:256], MS[:, h, 256:512], on.t, t)
                on.free = [ms[h]]

            g = gates(0)
            for h in range(8):
                nxt = gates(h + 1) if h < 7 else None
                mix(h, *g)
                g = nxt
            state["gb"] = [free["DD"]]
            last_p = ("p", P.n)
            state["yb"] = [[last_p], [last_p]]
            fz2 = fence()
            R2 = Arena()
            Pr = Ring([R2(512) for _ in range(3)])
            PTr = Ring([R2(512) for _ in range(2)])
            nmr = Ring([R2(8) for _ in range(4)])
            for ring_ in (Pr, PTr, nmr):
                for s in ring_.slots:
                    s.free = [fz2]
            heads = cross_heads(R2, "hg_x", xs, 1, fz2, ring, ms)
            attend(heads, False, Pr, PTr, nmr, ring)
            return natural("hg_o", MS, ms, 12, 1024, accs, 2)

        steps = [
            lambda xs: layer_norm(accs, even(xs), 0),
            lambda xs: layer_norm(accs, ffn(xs, 0, 1), 1),
            lambda xs: layer_norm(accs, odd(xs), 2),
            lambda xs: layer_norm(accs, ffn(xs, 1, 1), 3),
            lambda xs: [rms_to_XS(tt, state["xn"][tt], lambda k: col("rg", k)) for tt in range(2)],
            lambda xs: residual_rms(accs, window(xs), 0, lambda k: col("rg", 8 + k)),
            lambda xs: residual_rms(accs, ffn(xs, 0, 2), 1, lambda k: col("rg", 16 + k)),
            lambda xs: residual_rms(accs, hgrn(xs), 2, lambda k: col("rg", 24 + k)),
            lambda xs: residual_rms(accs, ffn(xs, 1, 2), 3, None),
        ]
        for step in steps:
            xs = step(xs)
        finish()


def constants():
    f = np.float32
    cc = np.zeros((128, NCC), f)
    p, j = np.arange(128)[:, None], np.arange(128)[None, :]

    def put(name, a):
        lo, hi = CC[name]
        cc[:, lo:hi] = a

    put("ident", p == j)
    put("cmf", np.where(j <= p, 0.0, -1e37))
    put("tril", p <= j)
    t = np.arange(256)
    put("m64", (t % 64 != 0)[None])
    put("ones", 1.0)
    m1 = np.ones((128, 2, 256))
    mb = np.zeros((128, 2, 32))
    for tile in range(2):
        for s in range(128):
            b = s // 32
            lo = 128 * tile + 32 * b
            m1[s, tile, lo:lo + 32] = (np.arange(lo, lo + 32) >= 128 * tile + s)
            mb[s, tile] = (np.arange(lo, lo + 32) <= 128 * tile + s)
    put("m1", m1.reshape(128, 512))
    put("mbc", mb.reshape(128, 64))
    inv = f(10000.0) ** (-np.arange(32, dtype=f) / f(32))
    ang = np.arange(256, dtype=f)[None, :] * inv[:, None].astype(f)
    put("cos", np.tile(np.cos(ang), (4, 1)))
    put("sin", np.tile(np.sin(ang), (4, 1)))
    rot = np.zeros((128, 128))
    for b in (0, 64):
        for i in range(32):
            rot[b + i + 32, b + i] = -1.0
            rot[b + i, b + i + 32] = 1.0
    put("rot", rot)
    cb = np.zeros((128, 384), f)
    cb[:, 0:128] = p == j
    cb[:, 128:256] = np.where(j <= p, 0.0, NEG)
    cb[:, 256:384] = np.where(j >= p, 0.0, NEG)
    n = np.maximum(255 - np.arange(384), 0)
    large = 16 + (np.log(np.maximum(n, 1).astype(f) / f(16)) / f(np.log(8.0)) * f(16)).astype(np.int32)
    bucket = np.where(n < 16, n, np.minimum(large, 31))
    onehot = (np.arange(32)[:, None] == bucket[None, :]).astype(f)
    return cc, cb, onehot


def layouts(d):
    a = {k: np.ascontiguousarray(np.asarray(v)) for k, v in d.items()}

    def tiles(w, cols):
        k = w.shape[0] // 128
        t = np.stack([w[:, c] for c in cols]).reshape(len(cols) // 2, 2, k, 128, 128)
        return np.ascontiguousarray(t.transpose(0, 3, 1, 2, 4)).reshape(len(cols) // 2, 128, -1)

    def rows(w):
        per = 2048 // w.shape[1]
        t = w.reshape(-1, per, 128, w.shape[1]).transpose(0, 2, 1, 3)
        return np.ascontiguousarray(t).reshape(-1, 128, 2048)

    def span(lo, n=1):
        return [np.arange(lo + 128 * i, lo + 128 * i + 128) for i in range(n)]

    r = {"x": a["x"], "mem_2": a["mem_2"], "od_sgu_g": a["od_sgu_g"], "od_sgu_b": a["od_sgu_b"]}
    mk = a["w_mem_kv_2"]
    r["mem_k"] = np.concatenate([tiles(mk[l], span(0, 4)) for l in range(2)])
    r["mem_v"] = np.concatenate([rows(mk[l][:, 512:]) for l in range(2)])
    w = a["ev_w_in"][0]
    fw = np.zeros((1024, 128), w.dtype)
    fw[:, 0:8] = fw[:, 32:40] = fw[:, 64:72] = fw[:, 96:104] = w[:, 2760:2768]
    fw[:, 8:16] = w[:, 1216:1224]
    wx = np.concatenate([w, fw], axis=1)
    kd = np.concatenate([np.arange(1152, 1216)] * 2)
    qa, ck, qi = span(0, 4), span(512), span(640, 4)
    qb, kb = span(1224, 4), span(1736, 4)
    r["ev_a"] = tiles(wx, span(2768) + [kd] + qi + ck + [qb[0], kb[0], qb[1], kb[1], qb[2], kb[2], qb[3]])
    r["ev_a"] = r["ev_a"][:7]
    ev_b = tiles(wx, [kb[3], qa[0], qa[1], qa[2]])
    r["ev_b"] = ev_b
    r["ev_c"] = tiles(wx, [qa[3], qa[3]])[:, :, 0:1024].copy()
    r["ev_v"] = rows(w[:, 2248:2760])
    r["ev_o"] = rows(a["ev_w_o"][0])
    r["w_uk"] = np.ascontiguousarray(a["ev_w_uk"][0].reshape(4, 2, 128, 64).transpose(1, 3, 0, 2)).reshape(128, 512)
    r["w_uv"] = np.ascontiguousarray(a["ev_w_uv"][0].transpose(1, 0, 2)).reshape(128, 512)
    for name, src, dn in (("1", "ffn_w_up", "ffn_w_down"), ("2", "ffn_w_in_2", "ffn_w_out_2")):
        r["up" + name] = np.concatenate([
            tiles(a[src][l], [c for j in range(22) for c in (span(128 * j)[0], span(2816 + 128 * j)[0])]) for l in range(2)])
        r["down" + name] = np.concatenate([rows(a[dn][l]) for l in range(2)])
    w = a["od_w_in"][0]
    u, gb_, gc, z = span(0, 4), span(1024, 4), span(1536, 4), span(2048, 4)
    r["od_v"] = rows(w[:, 512:1024])
    r["od_t"] = tiles(w, u + [c for i in range(4) for c in (gc[i], z[i])] + gb_)
    r["od_o"] = rows(a["od_w_o"][0])
    r["sgu_w"] = np.ascontiguousarray(a["od_sgu_w"][0].transpose(2, 0, 1)).reshape(128, 1024)
    w = a["a_w_in_2"][0]
    pair = [np.concatenate([np.arange(64 * (8 * (c // 4) + c % 4), 64 * (8 * (c // 4) + c % 4) + 64),
                            np.arange(64 * (8 * (c // 4) + c % 4 + 4), 64 * (8 * (c // 4) + c % 4 + 4) + 64)])
            for c in range(8)]
    r["wa_k"] = tiles(w, span(1024, 2))
    r["wa_v"] = rows(w[:, 1280:1536])
    r["wa_q"] = tiles(w, pair)
    r["wa_x"] = tiles(w, span(1536, 4))
    order = np.concatenate(pair + [np.arange(1024, 1536)])
    r["wa_o"] = rows(a["a_w_out_2"][0][order])
    w = a["b_w_in_2"][0]
    r["hg_v"] = rows(w[:, 1024:2048])
    r["hg_t"] = tiles(w, [c for h in range(8) for c in (
        span(2048 + 128 * h)[0], span(3072 + 128 * h)[0], span(128 * h)[0], span(4096 + 128 * h)[0])])
    r["hg_x"] = tiles(w, span(5120, 4))
    r["hg_o"] = rows(a["b_w_out_2"][0])
    r["c_ln"] = np.stack([a["ln_g"].reshape(4, 1024), a["ln_b"].reshape(4, 1024)], axis=1).reshape(4, 1, 2048)
    ng = a["norm_g_2"]
    r["c_rg"] = np.stack([ng[0, 1], ng[0, 3], ng[1, 1], ng[1, 3]]).reshape(4, 1, 1024)
    cc, cb, onehot = constants()
    par = np.zeros((128, NPC), np.float32)

    def put(name, v):
        lo, hi = PC[name]
        par[:v.shape[0], lo:hi] = v

    def cols(v):
        v = v.reshape(-1, v.shape[-1] // 128, 128)
        return v.transpose(2, 0, 1).reshape(128, -1)

    put("ln", cols(r["c_ln"].reshape(4, 2, 1024)))
    put("rg", cols(np.stack([ng[0, 0], ng[0, 2], ng[1, 0], ng[1, 2]])))
    put("memg", cols(a["mem_norm_g_2"][None]))
    put("fc1", a["ffn_conv_w"].reshape(2, 3, 44, 128).transpose(3, 0, 2, 1).reshape(128, -1))
    put("fc2", a["ffn_conv_w_2"].reshape(2, 3, 22, 128).transpose(3, 0, 2, 1).reshape(128, -1))
    put("fb2", cols(a["ffn_conv_b_2"]))
    put("oc", a["od_conv_w"].reshape(3, 4, 128).transpose(2, 1, 0).reshape(128, -1))
    put("bng", cols(a["b_norm_g_2"]))
    put("lbl", a["b_lb_logits_2"].reshape(2, 2, 8, 128).transpose(3, 1, 0, 2).reshape(128, -1))
    bf = np.zeros((104, 1), np.float32)
    bf[0:8, 0] = bf[32:40, 0] = bf[64:72, 0] = bf[96:104, 0] = a["ev_b_f"][0]
    put("bf", bf)
    put("sink", np.tile(a["a_sink_2"], (128, 1)))
    put("relb", a["rel_bias"])
    r["c_f32"], r["c_par"], r["c_onehot"], r["c_mask"] = cc, par, onehot, cb
    return r


def kernel(**inputs):
    import concourse.bacc as bacc
    from concourse.bass_utils import run_bass_kernel_spmd as run

    r = layouts(inputs)
    nc = bacc.Bacc("TRN2", target_bir_lowering=False, num_devices=1)
    T = {k: nc.dram_tensor(f"in_{k}", v.shape, mybir.dt.from_np(v.dtype), kind="ExternalInput").ap() for k, v in r.items()}
    out = nc.dram_tensor("out_0", (1, 256, 1024), F32, kind="ExternalOutput").ap()
    program(nc, T, out)
    res = run(nc, [{f"in_{k}": v for k, v in r.items()}], core_ids=[0])
    return res.results[0]["out_0"]
```

```python
from contextlib import ExitStack

import numpy as np

import concourse.bass as bass
from concourse import mybir

F32 = mybir.dt.float32
F32R = mybir.dt.float32r
BF16 = mybir.dt.bfloat16
I32 = mybir.dt.int32
ALU = mybir.AluOpType
ACT = mybir.ActivationFunctionType
AX = mybir.AxisListType

ALPHA = 4.0 ** 0.25
LN_EPS = 1e-5
RMS_EPS = 1e-6
NEG = -1e30
TAKEN = -3e38
NRAW = 3
NSPLIT = 3
AHEAD = 2
ARENA = 14280


def schedule():
    s = []

    def add(name, n, w=2048, first=0):
        s.extend((name, i, w) for i in range(first, first + n))

    def ffn(name_up, name_down, layer):
        ups = [(name_up, layer * 22 + j, 2048) for j in range(22)]
        for m in range(11):
            s.extend(ups[2 * m:2 * m + 2])
            if 0 < m < 10:
                s.append((name_down, layer * 11 + m - 1, 2048))
        s.extend((name_down, layer * 11 + m, 2048) for m in (9, 10))

    for l in range(2):
        add("mem_k", 2, first=2 * l)
        add("mem_v", 2, first=2 * l)
    add("ev_a", 7)
    add("ev_v", 2)
    add("ev_b", 2)
    add("ev_c", 1, 1024)
    add("ev_o", 4)
    ffn("up1", "down1", 0)
    add("od_v", 2)
    add("od_t", 8)
    add("od_o", 4)
    ffn("up1", "down1", 1)
    add("wa_k", 1)
    add("wa_v", 1)
    add("wa_q", 4)
    add("wa_x", 2)
    add("wa_o", 6)
    ffn("up2", "down2", 0)
    add("hg_v", 4)
    add("hg_t", 16)
    add("hg_x", 2)
    add("hg_o", 6)
    ffn("up2", "down2", 1)
    return s


CC = {}
_n = 0
for _name, _w in (("ident", 128), ("cmf", 128), ("tril", 128), ("m64", 256), ("ones", 256), ("m1", 512),
                  ("mbc", 64), ("cos", 256), ("sin", 256), ("rot", 128)):
    CC[_name] = (_n, _n + _w)
    _n += _w
NCC = _n
PC = {}
_n = 0
for _name, _w in (("ln", 64), ("rg", 32), ("memg", 8), ("fc1", 264), ("fc2", 132), ("fb2", 44), ("oc", 12),
                  ("bng", 8), ("lbl", 32), ("bf", 1), ("sink", 16), ("relb", 8)):
    PC[_name] = (_n, _n + _w)
    _n += _w
NPC = _n


class Engine:

    def __init__(self, key, eng, sems):
        self.key, self.eng, self.sems, self.n, self.seen = key, eng, sems, 0, {}

    def __call__(self, *tokens):
        need = {}
        stack = list(tokens)
        while stack:
            t = stack.pop()
            if t is None:
                continue
            if isinstance(t, list):
                stack.extend(t)
            else:
                need[t[0]] = max(need.get(t[0], 0), t[1])
        for key, value in sorted(need.items()):
            if self.seen.get(key, 0) < value:
                self.eng.wait_ge(self.sems[key], value)
                self.seen[key] = value
        return self.eng

    def done(self, instruction):
        self.n += 1
        instruction.then_inc(self.sems[self.key], 1)
        return (self.key, self.n)


class Slot:
    def __init__(self, t):
        self.t, self.free = t, []


class Ring:
    def __init__(self, tiles):
        self.slots, self.i = [x if isinstance(x, Slot) else Slot(x) for x in tiles], 0

    def take(self):
        s = self.slots[self.i % len(self.slots)]
        self.i += 1
        return s


def program(nc, T, out):
    with ExitStack() as ctx:
        sems = {}

        def sem(name):
            sems[name] = ctx.enter_context(nc.semaphore("s_" + name))

        def sb(name, shape, dt=F32):
            return ctx.enter_context(nc.sbuf_tensor(name, shape, dt))

        for k in "vagp":
            sem(k)
        V = Engine("v", nc.vector, sems)
        A = Engine("a", nc.scalar, sems)
        G = Engine("g", nc.gpsimd, sems)
        P = Engine("p", nc.tensor, sems)
        SP = Engine("sp", nc.sync, sems)
        dma_n = {}

        def dma(name, dst, src, *tokens):
            if name not in sems:
                sem(name)
                dma_n[name] = 0
            dma_n[name] += 16
            SP(*tokens).dma_start(dst, src).then_inc(sems[name], 16)
            return (name, dma_n[name])

        raw = [sb(f"raw{i}", [128, 2048]) for i in range(NRAW)]
        whi = [sb(f"whi{i}", [128, 2048], F32R) for i in range(NSPLIT)]
        wlo = [sb(f"wlo{i}", [128, 2048], F32R) for i in range(NSPLIT)]
        XS = sb("XS", [128, 8, 512], F32R)
        MS = sb("MS", [128, 12, 512], F32R)
        xn = sb("xn", [128, 2, 1024])
        yb = sb("yb", [128, 2, 1024])
        gb = sb("gb", [128, 2, 1024])
        cc = sb("cc", [128, NCC])
        pc = sb("pc", [128, NPC])
        cb = sb("cb", [128, 384], BF16)
        st = sb("st", [128, 64])
        nw = sb("nw", [128, 32])
        lb = sb("lb", [128, 48])
        ar = sb("ar", [128, ARENA])
        banks = [Slot(ctx.enter_context(nc.psum_tensor(f"ps{i}", [128, 512], F32))) for i in range(8)]
        low, high = banks[0:4], Ring(banks[4:8])
        allb = Ring(banks)

        def C(name, rows=128):
            a, b = CC[name]
            return cc[0:rows, a:b]

        def col(name, i=0, rows=128):
            a = PC[name][0] + i
            return pc[0:rows, a:a + 1]

        ident = C("ident")
        identb, cmb, cmb2 = cb[:, 0:128], cb[:, 128:256], cb[:, 256:384]

        class Arena:
            def __init__(self):
                self.at = 0

            def __call__(self, n):
                a = self.at
                self.at += n
                assert self.at <= ARENA, self.at
                return ar[:, a:a + n]

        def fence():
            return [(e.key, e.n) for e in (V, A, G, P)]

        t_pc = dma("d_pc", pc[:, :], T["c_par"])
        t_oh = dma("d_oh", ar[0:32, 5000:5384], T["c_onehot"])
        t_mem = [dma(f"d_mem{i}", gb[:, i, :], T["mem_2"][0, 128 * i:128 * i + 128]) for i in range(2)]
        t_id = dma("d_id", cc[:, 0:128], T["c_f32"][:, 0:128])

        sched = schedule()

        class Stream:
            def __init__(self):
                self.pos = self.loaded = self.split_n = 0
                self.raw_free = [[] for _ in range(NRAW)]
                self.landed = {}
                self.ready = {}
                self.used = [[] for _ in range(NSPLIT)]

            def load(self):
                m = self.loaded
                if m >= len(sched):
                    return
                name, i, w = sched[m]
                r = m % NRAW
                self.landed[m] = dma(f"d_w{r}", raw[r][:, 0:w], T[name][i], self.raw_free[r])
                self.loaded += 1

            def split(self, share=3):
                m = self.split_n
                if m >= len(sched):
                    return
                w = sched[m][2]
                r, s = m % NRAW, m % NSPLIT
                a = w // 4 * share
                th = A.done(A(self.landed[m], self.used[s]).activation(whi[s][:, 0:w], raw[r][:, 0:w], ACT.Copy))
                tg = G.done(G(th, self.landed[m], self.used[s]).tensor_tensor(
                    wlo[s][:, 0:a], raw[r][:, 0:a], whi[s][:, 0:a].bitcast(F32), ALU.subtract))
                tv = V.done(V(th, self.landed[m], self.used[s]).tensor_tensor(
                    wlo[s][:, a:w], raw[r][:, a:w], whi[s][:, a:w].bitcast(F32), ALU.subtract)) if a < w else None
                self.raw_free[r] = [tg, tv]
                self.ready[m] = [th, tg, tv]
                self.split_n += 1
                self.load()

            def get(self, name, ahead=0):
                m = self.pos + ahead
                assert sched[m][0] == name, (sched[m], name)
                return whi[m % NSPLIT], wlo[m % NSPLIT], self.ready[m]

            def fill(self, ahead=AHEAD, share=3):
                while self.split_n < self.pos + ahead and self.split_n < len(sched):
                    self.split(share)

            def done(self, tok, fill=True):
                self.used[self.pos % NSPLIT] = [tok]
                self.pos += 1
                if fill:
                    self.fill()
                if later and self.pos % 2:
                    later.pop(0)()

        later = []
        W = Stream()
        for _ in range(NRAW):
            W.load()
        for _ in range(AHEAD):
            W.split()

        def split_to(hi, lo, src, *tokens):
            th = A.done(A(*tokens).activation(hi, src, ACT.Copy))
            return V.done(V(th, *tokens).tensor_tensor(lo, src, hi.bitcast(F32), ALU.subtract))

        def at(xs, k):
            return [x[k * len(x) // 8] for x in xs]

        def project_T(name, xs_ready, ring, XS=XS):
            hi, lo, ready = W.get(name)
            tiles = sched[W.pos][2] // 1024
            bank = ring.take()
            P(ready, bank.free)
            for i in range(tiles):
                o = bank.t[:, 256 * i:256 * i + 256]
                for k in range(8):
                    P(at(xs_ready, k))
                    c = slice(1024 * i + 128 * k, 1024 * i + 128 * k + 128)
                    nc.tensor.matmul(o, hi[:, c], XS[:, k, 0:256], start=(k == 0), stop=False)
                    nc.tensor.matmul(o, hi[:, c], XS[:, k, 256:512], start=False, stop=False)
                    last = nc.tensor.matmul(o, lo[:, c], XS[:, k, 0:256], start=False, stop=(k == 7))
            tok = P.done(last)
            W.done(tok)
            return bank, tok

        def accumulate(name, S, ks, ready, n, accs, first, last, count=1, by_tile=False, held=False):
            per = 2048 // n
            toks = []
            if held:
                W.fill(NSPLIT)
            got = [W.get(name, i) for i in range(count)]
            for tt in range(2):
                for i, (hi, lo, wready) in enumerate(got):
                    P(wready)
                    for j in range(per):
                        k = ks[i * per + j]
                        P(ready[k][tt] if by_tile else ready[k])
                        sh = S[:, k, 128 * tt:128 * tt + 128]
                        sl = S[:, k, 256 + 128 * tt:384 + 128 * tt]
                        begin = first and i == 0 and j == 0
                        end = last and i == count - 1 and j == per - 1
                        for lhs, w in ((sh, hi), (sh, lo), (sl, hi)):
                            for h in range((n + 511) // 512):
                                acc = accs[tt][h]
                                if begin and lhs is sh and w is hi:
                                    P(acc.free)
                                c = min(n, 512)
                                ins = nc.tensor.matmul(acc.t[:, 0:c], lhs, w[:, n * j + c * h:n * j + c * h + c],
                                                       start=(begin and lhs is sh and w is hi),
                                                       stop=(end and lhs is sl))
                toks.append(P.done(ins))
            for _ in range(count):
                W.done(toks[-1], not held)
            return toks

        def natural(name, S, ready, K, n, accs, hold=1, lead=1):
            per = 2048 // n
            chunks = K // per
            if lead > 1:
                groups = [lead] + [1] * (chunks - lead - hold) + [hold] * (chunks > lead)
            else:
                groups = [1] * (chunks - hold) + [hold]
            c = 0
            for g in groups:
                t = accumulate(name, S, list(range(c * per, (c + g) * per)), ready, n, accs, c == 0, c + g == chunks, g, lead > 1, hold > 1 and c + g == chunks)
                c += g
            return t

        xf = Ring([sb(f"xf{i}", [128, 256]) for i in range(4)])

        def to_XS(tt, tok, src, rhs, g, b, aside, XS=XS):
            toks = []
            for q in range(4):
                bank = high.take()
                P(tok, bank.free)
                for i in range(2):
                    k = 2 * q + i
                    o, x = bank.t[:, 128 * i:128 * i + 128], src[:, tt, 128 * k:128 * k + 128]
                    last = nc.tensor.transpose(o, x, ident) if rhs is ident else \
                        nc.tensor.matmul(o, x, rhs, start=True, stop=True)
                tp = P.done(last)
                hi = XS[:, 2 * q:2 * q + 2, 128 * tt:128 * tt + 128]
                lo = XS[:, 2 * q:2 * q + 2, 256 + 128 * tt:384 + 128 * tt]
                if b is None and not aside:
                    for i in range(2):
                        th = A.done(A(tp).activation(hi[:, i, :], bank.t[:, 128 * i:128 * i + 128], ACT.Identity,
                                                     scale=g(2 * q + i)))
                    for i in range(2):
                        t = V.done(V(th).scalar_tensor_tensor(lo[:, i, :], bank.t[:, 128 * i:128 * i + 128], g(2 * q + i),
                                                              hi[:, i, :].bitcast(F32), ALU.mult, ALU.subtract))
                    bank.free = [t]
                    toks.append(t)
                    continue
                x = xf.take()
                for i in range(2):
                    k = 2 * q + i
                    o, dst = bank.t[:, 128 * i:128 * i + 128], x.t[:, 128 * i:128 * i + 128]
                    if q % 2 or aside:
                        te = A.done(A(tp, x.free).activation(dst, o, ACT.Identity, scale=g(k), bias=b(k) if b else 0.0))
                    else:
                        te = V.done(V(tp, x.free).tensor_scalar(dst, o, g(k), b(k) if b else None,
                                                                ALU.mult, ALU.add if b else ALU.bypass))
                bank.free = [te]
                xv = x.t[:, :].rearrange("p (k t) -> p k t", k=2)
                th = A.done(A(te).activation(hi, xv, ACT.Copy))
                E = G if aside else V
                t = E.done(E(th, te).tensor_tensor(lo, xv, hi.bitcast(F32), ALU.subtract))
                x.free = [t]
                toks.append(t)
            return toks

        def rstd_of(dst, src, scale, eps, tok):
            n = src.shape[1]
            a, b, y = nw[:, 0:n], nw[:, 16:16 + n], dst
            t = V.done(V(tok).tensor_scalar(a, src, scale, eps, ALU.mult, ALU.add))
            ty = V.done(V(t).tensor_scalar(y.bitcast(I32), a.bitcast(I32), -0.5, 1597463007.0, ALU.mult, ALU.add))
            t = V.done(V(ty).tensor_scalar(a, a, -0.5, None, ALU.mult))
            for _ in range(3):
                if n == 1:
                    t = V.done(V(t).tensor_scalar(b, y, a, y, ALU.mult, ALU.mult))
                else:
                    t = V.done(V(t).tensor_tensor(b, y, y, ALU.mult))
                    t = V.done(V(t).tensor_tensor(b, b, a, ALU.mult))
                t = V.done(V(t).scalar_tensor_tensor(y, b, 1.5, y, ALU.add, ALU.mult))
            return t

        state = {"xn": [None, None], "yb": [[], []], "gb": []}

        def flush():
            while later:
                later.pop(0)()

        def load_gb(src, rows):
            n = 1024 * rows
            ap = bass.AP(tensor=src.tensor, offset=src.offset, ap=[[0, 128], [1, n]])
            return dma("d_gb", gb[:, 0:rows, :].rearrange("p a d -> p (a d)"), ap, state["gb"])

        def weave(steps, order):
            for i in order:
                if i is None:
                    W.fill(2, 4)
                else:
                    next(steps[i])

        def layer_norm(accs, toks, idx):
            t_gb = load_gb(T["c_ln"][idx], 2)
            ready, post = [None, None], [None, None]

            def tile(tt):
                o = 32 * tt
                for h in range(2):
                    c = slice(512 * h, 512 * h + 512)
                    t = V.done(V(toks[tt], state["xn"][tt], state["yb"][tt]).scalar_tensor_tensor(
                        yb[:, tt, c], xn[:, tt, c], ALPHA, accs[tt][h].t[:, :], ALU.mult, ALU.add))
                    accs[tt][h].free = [t]
                    t = V.done(V(t).bn_stats(st[:, o + 6 * h:o + 6 * h + 6], yb[:, tt, c]))
                t = V.done(V(t).bn_aggr(st[:, o + 12:o + 14], st[:, o:o + 12]))
                t = rstd_of(st[:, o + 14:o + 15], st[:, o + 13:o + 14], 1.0, LN_EPS, t)
                t = V.done(V(t).tensor_scalar(yb[:, tt, :], yb[:, tt, :], st[:, o + 12:o + 13], st[:, o + 14:o + 15],
                                              ALU.subtract, ALU.mult))
                post[tt] = t
                yield
                ready[tt] = to_XS(tt, t, yb, ident, lambda k: col("ln", 16 * idx + k), lambda k: col("ln", 16 * idx + 8 + k),
                                  tt == 0)
                yield

            weave([tile(0), tile(1)], [0, 0, None, 1, 1])

            def scaled(tt):
                t = G.done(G(post[tt], t_gb).tensor_tensor(xn[:, tt, :], yb[:, tt, :], gb[:, 0, :], ALU.mult))
                state["xn"][tt] = t
                state["yb"][tt] = [t, ready[tt]]

            def shifted(tt):
                t = G.done(G(state["xn"][tt]).tensor_tensor(xn[:, tt, :], xn[:, tt, :], gb[:, 1, :], ALU.add))
                state["xn"][tt] = t
                state["gb"] = [state["gb"], t]

            for tt in range(2):
                later.append(lambda tt=tt: scaled(tt))
                later.append(lambda tt=tt: shifted(tt))
            if idx == 3:
                flush()
            return ready

        def rms_steps(tt, toks, gain, out, XS=XS, xn=xn):
            o = 32 * tt
            for h in range(2):
                t = A.done(A(toks[h], state["yb"][tt]).activation(
                    yb[:, tt, 512 * h:512 * h + 512], xn[:, tt, 512 * h:512 * h + 512], ACT.Square,
                    accum_out=st[:, o + 16 + h:o + 17 + h]))
            yield
            t = V.done(V(t).tensor_tensor(st[:, o + 20:o + 21], st[:, o + 16:o + 17], st[:, o + 17:o + 18], ALU.add))
            t = rstd_of(st[:, o + 21:o + 22], st[:, o + 20:o + 21], 1.0 / 1024, RMS_EPS, t)
            diag = yb[:, tt, 0:128]
            t = V.done(V(t).tensor_scalar(diag, ident, st[:, o + 21:o + 22], None, ALU.mult))
            yield
            out[tt] = to_XS(tt, t, xn, diag, gain, None, tt == 0, XS)
            state["yb"][tt] = [out[tt]]
            yield

        def rms_to_XS(toks, gain, XS=XS, xn=xn):
            out = [None, None]
            weave([rms_steps(tt, [toks[tt]] * 2, gain, out, XS, xn) for tt in range(2)], [0, 1, 0, 1, 0, 1])
            return out

        def residual_rms(accs, toks, idx, gain):
            t_gb = load_gb(T["c_rg"][idx], 1)
            ready, users = [None, None], []

            def tile(tt):
                o = 32 * tt
                sums = []
                for h in range(2):
                    sums.append(A.done(A(toks[tt], state["yb"][tt]).activation(
                        yb[:, tt, 512 * h:512 * h + 512], accs[tt][h].t[:, :], ACT.Square,
                        accum_out=st[:, o + 22 + h:o + 23 + h])))
                yield
                t = V.done(V(sums).tensor_tensor(st[:, o + 24:o + 25], st[:, o + 22:o + 23], st[:, o + 23:o + 24], ALU.add))
                t = rstd_of(st[:, o + 25:o + 26], st[:, o + 24:o + 25], 1.0 / 1024, RMS_EPS, t)
                halves = []
                for h in range(2):
                    c = slice(512 * h, 512 * h + 512)
                    t2 = V.done(V(t, t_gb, sums[h]).scalar_tensor_tensor(
                        yb[:, tt, c], accs[tt][h].t[:, :], st[:, o + 25:o + 26], gb[:, 0, c], ALU.mult, ALU.mult))
                    accs[tt][h].free = [t2]
                    halves.append(V.done(V(t2, state["xn"][tt]).tensor_tensor(xn[:, tt, c], xn[:, tt, c], yb[:, tt, c],
                                                                              ALU.add)))
                users.append(t2)
                state["xn"][tt] = halves
                state["yb"][tt] = halves
                if gain:
                    yield from rms_steps(tt, halves, gain, ready)
                yield

            weave([tile(0), tile(1)], [0, 0, 1, 0, 0, 1, None, 1, 1] if gain else [0, 0, 1, 1])
            state["gb"] = users
            return ready

        def finish():
            t = dma("d_out", out.rearrange("a (t p) d -> p (a t) d", p=128), xn[:, :, :], state["xn"][0], state["xn"][1])
            SP(t)

        accs = [[low[0], low[1]], [low[2], low[3]]]

        def attend(heads, causal, Pr, PTr, nmr, ring):
            n = 384 if causal else 512
            segs = [(0, 128), (128, 384)] if causal else [(0, 256), (256, 512)]

            def soft(h):
                head = heads[h]
                sink = head.get("sink")
                bank = ring.take()
                P(bank.free)
                tok = head["score"](bank.t)
                nm = nmr.take()
                V(tok, nm.free)
                if causal:
                    for i, (a, b) in enumerate(segs):
                        t = V.done(nc.vector.tensor_reduce(nm.t[:, i:i + 1], bank.t[:, a:b], AX.X, ALU.max, negate=True))
                else:
                    t = V.done(nc.vector.tensor_reduce(nm.t[:, 0:2], bank.t[:, :].rearrange("p (t s) -> p t s", t=2),
                                                       AX.X, ALU.max, negate=True))
                if sink is not None:
                    t = V.done(V(t).tensor_scalar(nm.t[:, 0:2], nm.t[:, 0:2], sink[1], None, ALU.min))
                p = Pr.take()
                A(t, p.free)
                ta = []
                for i, (a, b) in enumerate(segs):
                    ta.append(A.done(nc.scalar.activation(p.t[:, a:b], bank.t[:, a:b], ACT.Exp, bias=nm.t[:, i:i + 1],
                                                          accum_out=nm.t[:, 2 + i:3 + i])))
                bank.free = [ta[1]]
                if sink is not None:
                    ta.append(A.done(A(t).activation(nm.t[:, 6:8], nm.t[:, 0:2], ACT.Exp, bias=sink[0])))
                return p, nm, ta

            def normalise(h, p, nm, ta):
                if heads[h].get("sink") is not None:
                    ta = [V.done(V(ta).tensor_tensor(nm.t[:, 2:4], nm.t[:, 2:4], nm.t[:, 6:8], ALU.add)), ta]
                t = V.done(V(ta).reciprocal(nm.t[:, 4:6], nm.t[:, 2:4]))
                tn = []
                for i, (a, b) in enumerate(segs):
                    tn.append(V.done(V(t, ta).tensor_scalar(p.t[:, a:b], p.t[:, a:b], nm.t[:, 4 + i:5 + i], None, ALU.mult)))
                nm.free = tn
                return p, tn

            def turn(h, p, tn):
                bank = ring.take()
                P(tn, bank.free)
                if causal:
                    pairs = [(0, 0), (128, 128), (256, 256)]
                else:
                    pairs = [(0, 0), (128, 256), (256, 128), (384, 384)]
                for a, b in pairs:
                    last = nc.tensor.transpose(bank.t[:, b:b + 128], p.t[:, a:a + 128], ident)
                tp = P.done(last)
                p.free = [tp]
                pt = PTr.take()
                if h % 2:
                    t = V.done(V(tp, pt.free).tensor_copy(pt.t[:, 0:n], bank.t[:, 0:n]))
                else:
                    t = A.done(A(tp, pt.free).activation(pt.t[:, 0:n], bank.t[:, 0:n], ACT.Copy))
                bank.free = [t]
                return pt, t

            H = len(heads)
            ex, ps, pts = {}, {}, {}
            for i in range(-1, H + 5):
                if 0 <= i - 1 < H:
                    ps[i - 1] = normalise(i - 1, *ex[i - 1])
                if 0 <= i - 2 < H:
                    pts[i - 2] = turn(i - 2, *ps[i - 2])
                if 0 <= i - 3 < H:
                    pt, t = pts[i - 3]
                    pt.free = [heads[i - 3]["value"](pt.t, t)]
                if 0 <= i - 4 < H and "post" in heads[i - 4]:
                    heads[i - 4]["post"]()
                if i + 1 < H and "prep" in heads[i + 1]:
                    heads[i + 1]["prep"]()
                if 0 <= i < H:
                    ex[i] = soft(i)

        V(t_pc)
        A(t_pc)
        kv = [ar[:, 1024 * i:1024 * i + 1024] for i in range(4)]
        onehot, rb = ar[:, 5000:5384], ar[:, 5400:8472]
        skew = nc.dram_tensor("scr_bias", (8, 128 * 384), F32, kind="Internal").ap()
        trb = []
        for h in range(8):
            bank = high.take()
            a = PC["relb"][0] + h
            tp = P.done(P(t_oh, t_pc, bank.free).matmul(bank.t[:, 0:384], pc[0:32, a:a + 1].to_broadcast([32, 128]),
                                                       onehot[0:32, :], start=True, stop=True))
            t = V.done(V(tp).tensor_copy(rb[:, 384 * h:384 * h + 384], bank.t[:, 0:384]))
            bank.free = [t]
            trb.append(t)

        scr = nc.dram_tensor("scr_mem", (4, 128, 1024), F32, kind="Internal").ap()
        P(t_id)
        xm = rms_to_XS(t_mem, lambda k: col("memg", k), MS, gb)
        state["gb"] = fence()[0:2]
        t_x = [dma(f"d_x{i}", xn[:, i, :], T["x"][0, 128 * i:128 * i + 128]) for i in range(2)]
        t_w = dma("d_skw", skew.rearrange("h (p n) -> p h n", n=384), rb.rearrange("p (h n) -> p h n", h=8), trb)
        t_cc = dma("d_cc", cc[:, 128:], T["c_f32"][:, 128:])
        t_cb = dma("d_cb", ar[:, 8500:8884], T["c_mask"])
        t_scr = []
        xs = []
        state["xn"] = list(t_x)
        for l in range(2):
            tk = []
            for j in range(2):
                bank, tok = project_T("mem_k", xm, high, MS)
                t = A.done(A(tok).activation(kv[2 * l][:, 512 * j:512 * j + 512], bank.t[:, :], ACT.Copy))
                bank.free = [t]
                tk.append(t)
            t_scr.append(dma(f"d_scr{2 * l}", scr[2 * l], kv[2 * l], tk))
            acc = [[low[2 * l]], [low[2 * l + 1]]]
            toks = natural("mem_v", MS, [at(xm, k) for k in range(8)], 8, 512, acc)
            tv = []
            for tt in range(2):
                t = V.done(V(toks[tt]).tensor_copy(kv[2 * l + 1][:, 512 * tt:512 * tt + 512], acc[tt][0].t[:, :]))
                acc[tt][0].free = [t]
                tv.append(t)
            t_scr.append(dma(f"d_scr{2 * l + 1}", scr[2 * l + 1], kv[2 * l + 1], tv))
            if l == 0:
                t_cb = V.done(V(t_cb).tensor_copy(cb[:, :], ar[:, 8500:8884]))
                P(t_cc, t_cb)
                for tt in range(2):
                    r = []
                    for q in range(2):
                        bank = high.take()
                        P(t_x[tt], bank.free)
                        for i in range(4):
                            k = 4 * q + i
                            last = nc.tensor.transpose(bank.t[:, 128 * i:128 * i + 128], xn[:, tt, 128 * k:128 * k + 128],
                                                       ident)
                        tp = P.done(last)
                        bv = bank.t[:, :].rearrange("p (k t) -> p k t", k=4)
                        t2 = split_to(XS[:, 4 * q:4 * q + 4, 128 * tt:128 * tt + 128],
                                      XS[:, 4 * q:4 * q + 4, 256 + 128 * tt:384 + 128 * tt], bv, tp)
                        bank.free = [t2]
                        r.append(t2)
                    xs.append(r)

        def even(xs):
            fz = [t_w, fence(), t_scr]
            R = Arena()
            Bh, RH = R(2048), gb[:, :, :].rearrange("p a d -> p (a d)")
            L, FW, FZ, CT = R(256), R(256), R(256), R(256)
            QI, KI, QB, KB, QA, VB = R(1024), R(256), R(1024), R(1024), R(1024), R(1024)
            CN, WK, WV = R(256), R(512), R(512)
            S, WI, M8 = R(384), R(32), R(16)
            rr = Ring([R(384) for _ in range(2)])
            MB = R(192).bitcast(BF16)
            Pr = Ring([R(384) for _ in range(3)])
            PTr = Ring([R(384) for _ in range(2)])
            nmr = Ring([R(8) for _ in range(4)])
            QLr = Ring([R(256) for _ in range(2)])
            OAr = Ring([R(256) for _ in range(2)])
            t_bh = dma("d_bh", Bh.rearrange("p (h n) -> p h n", h=8),
                       bass.AP(tensor=skew.tensor, offset=127, ap=[[383, 128], [128 * 384, 8], [1, 256]]), fz)
            t_wk = dma("d_wk", WK, T["w_uk"], fz)
            t_wv = dma("d_wv", WV, T["w_uv"], fz)
            t0 = V.done(V(fz).memset(L, 0.0))
            t0 = V.done(V(t0).memset(L[32:40, :], 1.0))
            t0 = V.done(V(t0).memset(L[96:104, :], 1.0))
            t0 = V.done(V(t0).memset(RH, 0.0))
            ring = allb

            def out_of(bank, i, dst, tok, scale=1.0, rows=128):
                return A.done(A(tok, fz).activation(dst, bank.t[0:rows, 256 * i:256 * i + 256], ACT.Copy, scale=scale))

            bank, tok = project_T("ev_a", xs, ring)
            t_fw = out_of(bank, 0, FW, tok)
            t_ki = out_of(bank, 1, KI, tok)
            bank.free = [t_ki]
            t_qi = []
            for j in range(2):
                bank, tok = project_T("ev_a", xs, ring)
                t = A.done(A(tok, fz).activation(QI[:, 512 * j:512 * j + 512], bank.t[:, :], ACT.Copy, scale=0.125))
                bank.free = [t]
                t_qi.append(t)
            bank = ring.take()
            P(t_fw, bank.free)
            for tt in range(2):
                last = nc.tensor.transpose(bank.t[:, 16 * tt:16 * tt + 16], FW[0:16, 128 * tt:128 * tt + 128], ident[0:16, 0:16])
            t_fwt = P.done(last)
            t_wi = V.done(V(t_fwt, fz).tensor_scalar(WI, bank.t[:, 0:32], float(np.float32(8 ** -0.5)), None, ALU.mult))
            bank.free = [t_wi]
            ts = [None, None]
            segs = [(0, 128), (128, 384)]
            for h in range(8):
                bank = ring.take()
                P(t_qi[h // 4], t_ki, bank.free)
                q = slice(64 * (h % 2), 64 * (h % 2) + 64)
                for tt in range(2):
                    a, b = segs[tt]
                    c = 256 * (h // 2) + 128 * tt
                    last = nc.tensor.matmul(bank.t[:, a:b], QI[q, c:c + 128], KI[q, 0:b - a], start=True, stop=True)
                tp = P.done(last)
                r = rr.take()
                t = A.done(A(tp, r.free).activation(r.t[:, :], bank.t[:, 0:384], ACT.Relu))
                bank.free = [t]
                for tt in range(2):
                    a, b = segs[tt]
                    w = WI[:, 16 * tt + 8 + h:16 * tt + 9 + h]
                    if h == 0:
                        ts[tt] = V.done(V(t, t_wi).tensor_scalar(S[:, a:b], r.t[:, a:b], w, None, ALU.mult))
                    else:
                        ts[tt] = V.done(V(t, ts[tt]).scalar_tensor_tensor(S[:, a:b], r.t[:, a:b], w, S[:, a:b],
                                                                          ALU.mult, ALU.add))
                r.free = [ts[0], ts[1]]
            cmf = C("cmf")
            ts[0] = V.done(V(ts[0], t_cc).tensor_tensor(S[:, 0:128], S[:, 0:128], cmf, ALU.add))
            ts[1] = V.done(V(ts[1], t_cc).tensor_tensor(S[:, 256:384], S[:, 256:384], cmf, ALU.add))
            rounds = [0, 1] * 8

            def select(n):
                for _ in range(n):
                    tt = rounds.pop(0)
                    a, b = segs[tt]
                    m8 = M8[:, 8 * tt:8 * tt + 8]
                    t = V.done(V(ts[tt]).max(m8, S[:, a:b]))
                    ts[tt] = V.done(V(t).match_replace(S[:, a:b], m8, S[:, a:b], TAKEN))

            select(2)
            bank, tok = project_T("ev_a", xs, ring)
            t_ct = out_of(bank, 0, CT, tok)
            t_qb = [out_of(bank, 1, QB[:, 0:256], tok, 0.125)]
            bank.free = [t_qb[0]]
            t_kb = []
            for j in range(3):
                select(2)
                bank, tok = project_T("ev_a", xs, ring)
                t_kb.append(out_of(bank, 0, KB[:, 256 * j:256 * j + 256], tok))
                t_qb.append(out_of(bank, 1, QB[:, 256 * j + 256:256 * j + 512], tok, 0.125))
                bank.free = [t_qb[-1]]
            select(2)
            accv = [[ring.take()], [ring.take()]]
            toks = natural("ev_v", XS, [at(xs, k) for k in range(8)], 8, 512, accv)
            select(4)
            t_vb = []
            for tt in range(2):
                t = A.done(A(toks[tt]).activation(VB[:, 512 * tt:512 * tt + 512], accv[tt][0].t[:, :], ACT.Copy))
                accv[tt][0].free = [t]
                t_vb.append(t)
            bank, tok = project_T("ev_b", xs, ring)
            t_kb.append(out_of(bank, 0, KB[:, 768:1024], tok))
            t_qa = [out_of(bank, 1, QA[:, 0:256], tok)]
            bank.free = [t_qa[0]]

            select(2)
            t = V.done(V(ts).tensor_scalar(S, S, -2e38, 1e30, ALU.is_lt, ALU.mult))
            t_mb = [V.done(V(t, fz).tensor_scalar(MB[:, 128:256], S[:, 128:256], NEG, None, ALU.add))]
            for a in (0, 256):
                t_mb.append(V.done(V(t, fz).scalar_tensor_tensor(MB[:, a:a + 128], S[:, a:a + 128], NEG, cmb, ALU.add, ALU.add)))

            z = slice(0, 104)
            tz = V.done(V(t_fw, t_pc).tensor_scalar(FZ[z, :], FW[z, :], col("bf", 0, 104), None, ALU.add))
            nc.scalar.preload_act_table_set("natural_log_exp_and_others")
            t = tab = A.done(A(tz, t_fwt).activation(FW[z, :], FZ[z, :], ACT.Abs))
            t = A.done(A(t).activation(FW[z, :], FW[z, :], ACT.Exp, scale=-1.0))
            t = A.done(A(t).activation(FW[z, :], FW[z, :], ACT.Ln, bias=1.0))
            tz = V.done(V(tab).tensor_scalar(FZ[z, :], FZ[z, :], 0.0, None, ALU.min))
            tz = V.done(V(t, tz).tensor_tensor(FZ[z, :], FZ[z, :], FW[z, :], ALU.subtract))
            tz = V.done(V(tz).tensor_tensor_scan(FW[z, :], C("ones", 104), FZ[z, :], 0.0, ALU.mult, ALU.add))
            rv = RH.rearrange("p (h t) -> p h t", h=8)
            t_cum = []
            for a in (0, 64):
                b = a + 32
                tl = V.done(V(tz, t0).tensor_copy(L[a:a + 8, :], FW[a:a + 8, :]))
                t1 = V.done(V(t0, t_cc).tensor_copy(rv[a:a + 8], ident[a:a + 8, a:a + 8].unsqueeze(2).to_broadcast([8, 8, 256])))
                tn = V.done(V(tz).tensor_scalar(FZ[b:b + 8, :], FW[b:b + 8, :], -1.0, None, ALU.mult))
                t2 = V.done(V(tn, t1).tensor_tensor(rv[b:b + 8], ident[b:b + 8, b:b + 8].unsqueeze(2).to_broadcast([8, 8, 256]),
                                                    FZ[b:b + 8, :].unsqueeze(1).to_broadcast([8, 8, 256]), ALU.mult))
                t_cum += [tl, t1, t2]

            outb = {}

            def b_score(h):
                q = slice(64 * (h % 2), 64 * (h % 2) + 64)
                g = slice(64 * (h % 2), 64 * (h % 2) + 40)

                def go(bt):
                    P(t_qb[h // 2], t_kb[h // 2], t_cum)
                    for tt in range(2):
                        a, b = segs[tt]
                        c = 256 * (h // 2)
                        o = bt[:, a:b]
                        nc.tensor.matmul(o, QB[q, c + 128 * tt:c + 128 * tt + 128], KB[q, c:c + b - a], start=True, stop=False)
                        nc.tensor.matmul(o, L[g, 128 * tt:128 * tt + 128], rv[g, h, 0:b - a], start=False, stop=False)
                        last = nc.tensor.matmul(bt[:, b - 128:b], identb, cmb, start=False, stop=True)
                    return P.done(last)
                return go

            def pair_out(h, chunk):
                if h % 2 == 0:
                    outb[0] = ring.take()
                    P(outb[0].free)
                return outb[0], slice(64 * (h % 2), 64 * (h % 2) + 64)

            def put(h, chunk, bank, tp):
                if h % 2:
                    t = split_to(MS[:, chunk, 0:256], MS[:, chunk, 256:512], bank.t[:, 0:256], tp)
                    bank.free = [t]
                    ms[chunk] = t

            def b_value(h):
                def go(pt, t):
                    bank, q = pair_out(h, 4 + h // 2)
                    P(t, t_vb)
                    v = slice(64 * h, 64 * h + 64)
                    nc.tensor.matmul(bank.t[q, 0:256], VB[:, v], pt[:, 0:256], start=True, stop=False)
                    tp = P.done(nc.tensor.matmul(bank.t[q, 128:256], VB[:, 512 + 64 * h:576 + 64 * h], pt[:, 256:384],
                                                 start=False, stop=True))
                    put(h, 4 + h // 2, bank, tp)
                    return tp
                return go

            ms = {}
            attend([{"score": b_score(h), "value": b_value(h)} for h in range(8)], True, Pr, PTr, nmr, ring)
            state["gb"] = [("p", P.n)]

            state["gb"] = [("p", P.n)]

            bank, tok = project_T("ev_b", xs, ring)
            t = A.done(A(tok).activation(QA[:, 256:768], bank.t[:, :], ACT.Copy))
            bank.free = [t]
            t_qa += [t, t]
            bank, tok = project_T("ev_c", xs, ring)
            t_qa.append(out_of(bank, 0, QA[:, 768:1024], tok))
            bank.free = [t_qa[-1]]
            bank = ring.take()
            P(t_ct, bank.free)
            for tt in range(2):
                last = nc.tensor.transpose(bank.t[:, 128 * tt:128 * tt + 128], CT[:, 128 * tt:128 * tt + 128], ident)
            tp = P.done(last)
            t_cn = V.done(V(tp).tensor_copy(CN, bank.t[:, 0:256]))
            bank.free = [t_cn]

            lat, mixed = {}, {}

            def a_prep(h):
                q = slice(64 * (h % 2), 64 * (h % 2) + 64)

                def go():
                    bank = ring.take()
                    c = 256 * (h // 2)
                    tp = P.done(P(t_qa[h // 2], t_wk, bank.free).matmul(
                        bank.t[:, 0:256], WK[q, 128 * (h // 2):128 * (h // 2) + 128], QA[q, c:c + 256], start=True, stop=True))
                    ql = QLr.take()
                    t = A.done(A(tp, ql.free).activation(ql.t, bank.t[:, 0:256], ACT.Copy, scale=0.125))
                    bank.free = [t]
                    lat[h] = ql, t
                return go

            def a_score(h):
                def go(bt):
                    ql, t = lat[h]
                    P(t, t_ct, t_bh, t_mb)
                    for tt in range(2):
                        a, b = segs[tt]
                        o = bt[:, a:b]
                        nc.tensor.matmul(o, ql.t[:, 128 * tt:128 * tt + 128], CT[:, 0:b - a], start=True, stop=False)
                        nc.tensor.matmul(o, ident, Bh[:, 256 * h + 128 - 128 * tt:256 * h + 256], start=False, stop=False)
                        last = nc.tensor.matmul(o, identb, MB[:, a:b], start=False, stop=True)
                    tp = P.done(last)
                    ql.free = [tp]
                    return tp
                return go

            def a_value(h):
                def go(pt, t):
                    bank = ring.take()
                    P(t, t_cn, bank.free)
                    nc.tensor.matmul(bank.t[:, 0:256], CN[:, 0:128], pt[:, 0:256], start=True, stop=False)
                    tp = P.done(nc.tensor.matmul(bank.t[:, 128:256], CN[:, 128:256], pt[:, 256:384], start=False, stop=True))
                    oa = OAr.take()
                    t = V.done(V(tp, oa.free).tensor_copy(oa.t, bank.t[:, 0:256]))
                    bank.free = [t]
                    mixed[h] = oa, t
                    return tp
                return go

            def a_post(h):
                def go():
                    oa, t = mixed[h]
                    b2, q = pair_out(h, h // 2)
                    t2 = P.done(P(t, t_wv).matmul(b2.t[q, 0:256], WV[:, 64 * h:64 * h + 64], oa.t, start=True, stop=True))
                    oa.free = [t2]
                    put(h, h // 2, b2, t2)
                return go

            attend([{"prep": a_prep(h), "score": a_score(h), "value": a_value(h), "post": a_post(h)} for h in range(8)],
                   True, Pr, PTr, nmr, ring)
            return natural("ev_o", MS, ms, 8, 1024, accs, 2)

        def ffn(xs, layer, kind):
            fz = fence()
            R = Arena()
            hbr = [Slot(R(520)) for _ in range(2)]
            gr = Ring([R(512) for _ in range(3)])
            hr = Ring([R(256) for _ in range(3)])
            for s in hbr:
                t = V.done(V(fz).memset(s.t[:, 0:2], 0.0))
                t = V.done(V(fz).memset(s.t[:, 258:262], 0.0))
                s.free = [t]
            hbr = Ring(hbr)
            up, down = ("up1", "down1") if kind == 1 else ("up2", "down2")
            hs = {}

            def one(j):
                bank, tok = project_T(up, xs, high)
                hb, g, h = hbr.take(), gr.take(), hr.take()
                if kind == 1:
                    v = hb.t.rearrange("p (a n) -> p a n", a=2)
                    w = [[col("fc1", 132 * layer + 66 * a + 3 * j + i) for i in range(3)] for a in range(2)]
                    tc = A.done(A(tok, hb.free, fz).activation(
                        v[:, :, 2:258], bank.t[:, :].rearrange("p (a n) -> p a n", a=2), ACT.Copy))
                    ts = []
                    for a in range(2):
                        o = g.t[:, 256 * a:256 * a + 256]
                        t = A.done(A(tc, g.free).activation(o, bank.t[:, 256 * a:256 * a + 256], ACT.Copy, scale=w[a][2]))
                        bank.free = [t]
                        t = V.done(V(t, tc).scalar_tensor_tensor(o, v[:, a, 1:257], w[a][1], o, ALU.mult, ALU.add))
                        t = V.done(V(t).scalar_tensor_tensor(o, v[:, a, 0:256], w[a][0], o, ALU.mult, ALU.add))
                        ts.append(t)
                    hb.free = [ts[1]]
                    t = A.done(A(ts[0], h.free).activation(h.t, g.t[:, 0:256], ACT.Silu))
                    t = V.done(V(t, ts[1]).tensor_tensor(h.t, h.t, g.t[:, 256:512], ALU.mult))
                    g.free = [t]
                else:
                    w = [col("fc2", 66 * layer + 3 * j + i) for i in range(3)]
                    o = g.t[:, 0:256]
                    tc = A.done(A(tok, hb.free, fz).activation(hb.t[:, 2:258], bank.t[:, 0:256], ACT.Copy))
                    t = A.done(A(tc, g.free).activation(o, bank.t[:, 0:256], ACT.Identity, scale=w[1],
                                                        bias=col("fb2", 22 * layer + j)))
                    tg = t
                    t = V.done(V(t, tc).scalar_tensor_tensor(o, hb.t[:, 1:257], w[0], o, ALU.mult, ALU.add))
                    t = V.done(V(t).scalar_tensor_tensor(o, hb.t[:, 3:259], w[2], o, ALU.mult, ALU.add))
                    hb.free = [t]
                    t = A.done(A(t, h.free).activation(h.t, o, ACT.Gelu_apprx_tanh))
                    g.free = [t]
                    t = V.done(V(t, tg).tensor_tensor(h.t, h.t, bank.t[:, 256:512], ALU.mult))
                    bank.free = [t]
                k = j % 6
                hs[j] = split_to(MS[:, k, 0:256], MS[:, k, 256:512], h.t, t, fz)
                h.free = [hs[j]]

            def down_of(m, last=False):
                js = range(2 * m, 2 * m + (4 if last else 2))
                return accumulate(down, MS, [j % 6 for j in js], {j % 6: hs[j] for j in js}, 1024, accs, m == 0, last,
                                  2 if last else 1, False, last)

            for m in range(11):
                one(2 * m)
                one(2 * m + 1)
                if 0 < m < 10:
                    down_of(m - 1)
            return down_of(9, True)

        def odd(xs):
            fz = fence()
            R = Arena()
            VG, XC = R(1024), R(1024)
            GN, SW, SB = R(512), R(1024), R(128)
            S1, S2, S3 = R(16), R(16), R(16)
            U = R(1024)
            gcr = Ring([R(256) for _ in range(2)])
            zr = [Slot(R(260)) for _ in range(4)]
            yr = [R(256) for _ in range(4)]
            xr = Ring([R(256) for _ in range(2)])
            t_gn = dma("d_gn", GN, bass.AP(tensor=T["od_sgu_g"].tensor, offset=0, ap=[[0, 128], [1, 512]]), fz)
            t_sw = dma("d_sw", SW, T["sgu_w"], fz)
            t_sb = dma("d_sb", SB[0:8, :], T["od_sgu_b"][0], fz)
            tm = V.done(V(t_sw).tensor_tensor(SW.rearrange("p (g t) -> p g t", g=8), SW.rearrange("p (g t) -> p g t", g=8),
                                              C("tril").unsqueeze(1).to_broadcast([128, 8, 128]), ALU.mult))
            tz = []
            for s in zr:
                tz.append(V.done(V(fz).memset(s.t[:, 0:2], 0.0)))
            acc = [[low[0]], [low[1]]]
            toks = natural("od_v", XS, [at(xs, k) for k in range(8)], 8, 512, acc, 1, 2)
            tg = []
            for tt in range(2):
                t = A.done(A(toks[tt], fz).activation(VG[:, 512 * tt:512 * tt + 512], acc[tt][0].t[:, :], ACT.Gelu_apprx_tanh))
                acc[tt][0].free = [t]
                tg.append(t)
            v3 = VG.rearrange("p (g d) -> p g d", d=64)
            x3 = XC.rearrange("p (g d) -> p g d", d=64)
            t = V.done(V(tg).tensor_reduce(S1, v3, AX.X, ALU.add))
            t = V.done(V(t).tensor_scalar(S1, S1, 1.0 / 64, None, ALU.mult))
            t = V.done(V(t).tensor_tensor(v3, v3, S1.unsqueeze(2).to_broadcast([128, 16, 64]), ALU.subtract))
            ta = A.done(A(t, fz).activation(XC, VG, ACT.Square))
            t = V.done(V(ta).tensor_reduce(S2, x3, AX.X, ALU.add))
            t = rstd_of(S3, S2, 1.0 / 64, LN_EPS, t)
            t = V.done(V(t).tensor_tensor(x3, v3, S3.unsqueeze(2).to_broadcast([128, 16, 64]), ALU.mult))
            t_vn = V.done(V(t, t_gn).tensor_tensor(XC.rearrange("p (t d) -> p t d", t=2), XC.rearrange("p (t d) -> p t d", t=2),
                                                   GN.unsqueeze(1).to_broadcast([128, 2, 512]), ALU.mult))
            tu = []
            for j in range(2):
                bank, tok = project_T("od_t", xs, high)
                t = A.done(A(tok, fz).activation(U[:, 512 * j:512 * j + 512], bank.t[:, :], ACT.Gelu_apprx_tanh))
                bank.free = [t]
                tu += [t, t]
            ty = []
            for i in range(4):
                bank, tok = project_T("od_t", xs, high)
                gc = gcr.take()
                w = [col("oc", 3 * i + k) for k in range(3)]
                t = A.done(A(tok, gc.free, fz).activation(gc.t, bank.t[:, 0:256], ACT.Copy))
                zb, y = zr[i].t, yr[i]
                t = V.done(V(t, tz[i]).tensor_tensor(zb[:, 2:258], gc.t, bank.t[:, 256:512], ALU.mult))
                bank.free = gc.free = [t]
                t = V.done(V(t, fz).tensor_scalar(y, zb[:, 2:258], w[2], None, ALU.mult))
                t = V.done(V(t).scalar_tensor_tensor(y, zb[:, 1:257], w[1], y, ALU.mult, ALU.add))
                t = V.done(V(t).scalar_tensor_tensor(y, zb[:, 0:256], w[0], y, ALU.mult, ALU.add))
                ty.append(t)
            ms = {}
            for c in range(4):
                bank = high.take()
                P(t_vn, tm, t_sb, t_cc, bank.free)
                for g in (2 * c, 2 * c + 1):
                    q = slice(64 * (g % 2), 64 * (g % 2) + 64)
                    for tt in range(2):
                        o = bank.t[q, 128 * tt:128 * tt + 128]
                        nc.tensor.matmul(o, XC[:, 512 * tt + 64 * g:512 * tt + 64 * g + 64], SW[:, 128 * g:128 * g + 128],
                                         start=True, stop=False)
                        last = nc.tensor.matmul(o, ident[0:8, g:g + 1].to_broadcast([8, 64]), SB[0:8, :], start=False, stop=True)
                tp = P.done(last)
                x = xr.take()
                t = V.done(V(tp, tu[c], x.free).tensor_tensor(x.t, U[:, 256 * c:256 * c + 256], bank.t[:, 0:256], ALU.mult))
                bank.free = [t]
                ms[c] = split_to(MS[:, c, 0:256], MS[:, c, 256:512], x.t, t)
                x.free = [ms[c]]
            for j in range(2):
                bank, tok = project_T("od_t", xs, high)
                for i in range(2):
                    c = 2 * j + i
                    x = xr.take()
                    t = V.done(V(tok, ty[c], x.free).tensor_tensor(x.t, yr[c], bank.t[:, 256 * i:256 * i + 256], ALU.mult))
                    bank.free = [t]
                    ms[4 + c] = split_to(MS[:, 4 + c, 0:256], MS[:, 4 + c, 256:512], x.t, t)
                    x.free = [ms[4 + c]]
            return natural("od_o", MS, ms, 8, 1024, accs, 2)

        def cross_heads(R, name, xs, layer, fz, ring, ms):
            MK, MV, XQ = R(1024), R(1024), R(1024)
            t_mk = dma(f"d_mk{layer}", MK, scr[2 * layer], fz, t_scr)
            t_mv = dma(f"d_mv{layer}", MV, scr[2 * layer + 1], fz, t_scr)
            tq = []
            for j in range(2):
                bank, tok = project_T(name, xs, ring)
                t = A.done(A(tok, fz).activation(XQ[:, 512 * j:512 * j + 512], bank.t[:, :], ACT.Copy,
                                                 scale=float(np.float32(128 ** -0.5))))
                bank.free = [t]
                tq.append(t)

            def score(h):
                def go(bt):
                    P(tq[h // 2], t_mk)
                    for tt in range(2):
                        c = 256 * h + 128 * tt
                        last = nc.tensor.matmul(bt[:, 256 * tt:256 * tt + 256], XQ[:, c:c + 128], MK[:, 256 * h:256 * h + 256],
                                                start=True, stop=True)
                    return P.done(last)
                return go

            def value(h):
                def go(pt, t):
                    bank = ring.take()
                    P(t, t_mv, bank.free)
                    for s in range(2):
                        last = nc.tensor.matmul(bank.t[:, 0:256], MV[:, 512 * s + 128 * h:512 * s + 128 * h + 128],
                                                pt[:, 256 * s:256 * s + 256], start=(s == 0), stop=(s == 1))
                    tp = P.done(last)
                    t = split_to(MS[:, 8 + h, 0:256], MS[:, 8 + h, 256:512], bank.t[:, 0:256], tp)
                    bank.free = [t]
                    ms[8 + h] = t
                    return tp
                return go

            return [{"score": score(h), "value": value(h)} for h in range(4)]

        def window(xs):
            fz = fence()
            R = Arena()
            KR, QR, VN = R(512), R(2048), R(512)
            qr = Ring([R(512) for _ in range(2)])
            tr = Ring([R(512) for _ in range(2)])
            Pr = Ring([R(512) for _ in range(3)])
            PTr = Ring([R(512) for _ in range(2)])
            nmr = Ring([R(8) for _ in range(4)])
            NS = R(16)
            ring = allb
            a, b = PC["sink"]
            t_ns = V.done(V(t_pc, fz).tensor_scalar(NS, pc[:, a:b], -1.0, None, ALU.mult))

            def rope(dst, bank, tok, scale):
                q = qr.take()
                t = A.done(A(tok, q.free, fz).activation(q.t, bank.t[:, :], ACT.Copy, scale=scale))
                bank.free = [t]
                rb = ring.take()
                tp = P.done(P(t, rb.free).matmul(rb.t[:, :], C("rot"), q.t, start=True, stop=True))
                x = tr.take()
                v2 = lambda ap: ap.rearrange("p (a n) -> p a n", a=2)
                bc = lambda name: C(name).unsqueeze(1).to_broadcast([128, 2, 256])
                t1 = V.done(V(tp, x.free, fz).tensor_tensor(v2(x.t), v2(rb.t[:, :]), bc("sin"), ALU.mult))
                rb.free = [t1]
                t2 = V.done(V(t, fz).tensor_tensor(v2(dst), v2(q.t), bc("cos"), ALU.mult))
                t3 = V.done(V(t1, t2).tensor_tensor(dst, dst, x.t, ALU.add))
                x.free = [t3]
                q.free = [t3]
                return t3

            bank, tok = project_T("wa_k", xs, ring)
            tk = rope(KR, bank, tok, 1.0)
            accv = [[ring.take()], [ring.take()]]
            toks = natural("wa_v", XS, [at(xs, k) for k in range(8)], 8, 256, accv)
            tv = []
            for tt in range(2):
                t = A.done(A(toks[tt], fz).activation(VN[:, 256 * tt:256 * tt + 256], accv[tt][0].t[:, 0:256], ACT.Copy))
                accv[tt][0].free = [t]
                tv.append(t)
            tq = []
            for j in range(4):
                bank, tok = project_T("wa_q", xs, ring)
                t = rope(QR[:, 512 * j:512 * j + 512], bank, tok, 0.125)
                tq += [t, t]
            ms = {}
            outb = {}

            def score(c, r):
                q = slice(64 * r, 64 * r + 64)

                def go(bt):
                    P(tq[c], tk, t_cb)
                    kc = 256 * (c // 4)
                    for tt in range(2):
                        nc.tensor.matmul(bt[:, 256 * tt:256 * tt + 256], QR[q, 256 * c + 128 * tt:256 * c + 128 * tt + 128],
                                         KR[q, kc:kc + 256], start=True, stop=False)
                        o = bt[:, 128:256] if tt == 0 else bt[:, 256:384]
                        last = nc.tensor.matmul(o, identb, cmb if tt == 0 else cmb2, start=False, stop=True)
                    return P.done(last)
                return go

            def value(c, r):
                kvh = 2 * (c // 4) + r

                def go(pt, t):
                    if r == 0:
                        outb[0] = ring.take()
                        P(outb[0].free)
                    bank = outb[0]
                    q = slice(64 * r, 64 * r + 64)
                    P(t, tv)
                    for s in range(2):
                        last = nc.tensor.matmul(bank.t[q, 0:256], VN[:, 256 * s + 64 * kvh:256 * s + 64 * kvh + 64],
                                                pt[:, 256 * s:256 * s + 256], start=(s == 0), stop=(s == 1))
                    tp = P.done(last)
                    if r:
                        t = split_to(MS[:, c, 0:256], MS[:, c, 256:512], bank.t[:, 0:256], tp)
                        bank.free = [t]
                        ms[c] = t
                    return tp
                return go

            V(t_ns)
            A(t_ns)
            heads = []
            for c in range(8):
                for r in range(2):
                    h = (c % 4) + 4 * r + 8 * (c // 4)
                    heads.append({"score": score(c, r), "sink": (col("sink", h), NS[:, h:h + 1]), "value": value(c, r)})
            attend(heads, False, Pr, PTr, nmr, ring)
            heads = cross_heads(R, "wa_x", xs, 0, fz, ring, ms)
            attend(heads, False, Pr, PTr, nmr, ring)
            return natural("wa_o", MS, ms, 12, 1024, accs, 2)

        def hgrn(xs):
            fz = fence()
            R = Arena()
            VN = yb
            SGr = Ring([R(1024) for _ in range(2)])
            FF, KK, LF, CS = R(512), R(512), R(514), R(1024)
            E0 = R(512)
            QQ = R(256)
            GTr = Ring([R(256) for _ in range(2)])
            X0r = Ring([R(1024) for _ in range(2)])
            X1r = Ring([R(1536) for _ in range(2)])
            STr = Ring([R(512) for _ in range(2)])
            ONr = Ring([R(256) for _ in range(2)])
            UD = R(64)
            DD = gb[:, :, :].rearrange("p a d -> p (a d)")
            base = R.at
            stat = Ring([st[:, 32 * i:32 * i + 8] for i in range(2)])
            t = V.done(V(fz).memset(LF[:, 0:1], 0.0))
            t_lf = V.done(V(fz).memset(LF[:, 257:258], 0.0))
            lo0 = PC["lbl"][0]
            l0, l1 = pc[:, lo0:lo0 + 16], pc[:, lo0 + 16:lo0 + 32]
            m, e0, e1 = lb[:, 0:16], lb[:, 16:32], lb[:, 32:48]
            t = V.done(V(t_pc, fz).tensor_tensor(m, l0, l1, ALU.max))
            t1 = V.done(V(t).tensor_tensor(e0, l0, m, ALU.subtract))
            t2 = V.done(V(t).tensor_tensor(e1, l1, m, ALU.subtract))
            t = A.done(A(t1, t2).activation(lb[:, 16:48], lb[:, 16:48], ACT.Exp))
            t = V.done(V(t).tensor_tensor(m, e0, e1, ALU.add))
            t = V.done(V(t).reciprocal(m, m))
            t1 = V.done(V(t).tensor_tensor(e0, e0, m, ALU.mult))
            t2 = V.done(V(t).tensor_tensor(e1, e1, m, ALU.mult))
            t = V.done(V(t1, t2).tensor_tensor(m, e0, e1, ALU.add))
            t = V.done(V(t).tensor_tensor(m, m, e0, ALU.subtract))
            t_lb = V.done(V(t).tensor_scalar(e0, m, -1.0, 1.0, ALU.mult, ALU.add))
            vacc = [[low[0], low[1]], [low[2], low[3]]]
            toks = natural("hg_v", XS, [at(xs, k) for k in range(8)], 8, 1024, vacc, 1, 2)
            tv = []
            for tt in range(2):
                for h in range(2):
                    t = A.done(A(toks[tt], fz, state["yb"][tt]).activation(
                        VN[:, tt, 512 * h:512 * h + 512], vacc[tt][h].t[:, :], ACT.Copy))
                    vacc[tt][h].free = [t]
                    tv.append(t)
            ring = allb
            free = {"FF": [], "KK": [], "LF": [t_lf], "CS": [], "E0": [], "QQ": [], "DD": [state["gb"]], "UD": []}
            D4 = DD.rearrange("p (l d t) -> p l d t", l=4, d=2)
            C3 = CS.rearrange("p (k d t) -> p k d t", k=2, d=2)
            ms = {}

            def gates(h):
                bz, tz = project_T("hg_t", xs, ring)
                bq, tq = project_T("hg_t", xs, ring)
                sg, gt = SGr.take(), GTr.take()
                ta = A.done(A(tz, sg.free, fz).activation(sg.t[:, 0:512], bz.t[:, :], ACT.Sigmoid))
                bz.free = [ta]
                tb = A.done(A(tq).activation(sg.t[:, 512:1024], bq.t[:, :], ACT.Sigmoid))
                t_q = V.done(V(tb, free["QQ"]).tensor_tensor(QQ, sg.t[:, 512:768], bq.t[:, 0:256], ALU.mult))
                t_g = V.done(V(tb, gt.free).tensor_tensor(gt.t, sg.t[:, 768:1024], bq.t[:, 256:512], ALU.mult))
                bq.free = [t_g]
                for d in range(2):
                    o = 8 * d + h
                    tf = V.done(V(ta, t_lb, free["FF"]).tensor_scalar(
                        FF[:, 256 * d:256 * d + 256], sg.t[:, 256 * d:256 * d + 256], e0[:, o:o + 1], m[:, o:o + 1],
                        ALU.mult, ALU.add))
                sg.free = [tf, t_g]
                tk = V.done(V(tf, free["KK"]).tensor_scalar(KK, FF, -1.0, 1.0, ALU.mult, ALU.add))
                lf = LF.rearrange("p (d t) -> p d t", d=2)
                tl = A.done(A(tf, free["LF"]).activation(lf[:, :, 1:257], FF.rearrange("p (d t) -> p d t", d=2), ACT.Ln))
                free["FF"] = [tl, tk]
                V(tl, free["CS"], fz)
                for k, mask in ((0, C("m64")), (1, C("ones"))):
                    nc_v = nc.vector
                    tc = V.done(nc_v.tensor_tensor_scan(C3[:, k, 0, :], mask, lf[:, 0, 1:257], 0.0, ALU.mult, ALU.add))
                    tc = V.done(nc_v.tensor_tensor_scan(C3[:, k, 1, :], lf[:, 1, 0:256], mask, 0.0, ALU.add, ALU.mult))
                free["LF"] = [tc]
                V(tc, free["DD"])
                for lev in range(4):
                    n = 32 << lev
                    nb = 256 // n
                    for d in range(2):
                        src = C3[:, lev // 2, d, :].rearrange("p (b n) -> p b n", n=n)
                        dst = D4[:, lev, d, :].rearrange("p (b n) -> p b n", n=n)
                        mid = n // 2 - 1 + d
                        td = V.done(nc.vector.tensor_tensor(dst, src, src[:, :, mid:mid + 1].to_broadcast([128, nb, n]),
                                                            ALU.subtract))
                free["CS"] = [td]
                tn = A.done(A(td).activation(DD[:, 512:2048], DD[:, 512:2048], ACT.Abs))
                te1 = A.done(A(td, free["E0"]).activation(E0, DD[:, 0:512], ACT.Exp, scale=-1.0))
                te2 = A.done(A(te1).activation(DD[:, 0:512], DD[:, 0:512], ACT.Exp))
                te3 = A.done(A(tn).activation(DD[:, 512:2048], DD[:, 512:2048], ACT.Exp, scale=-1.0))
                x0, x1 = X0r.take(), X1r.take()
                V(te2, t_q, tk, x0.free, fz)
                nc_v = nc.vector
                V.done(nc_v.tensor_tensor(x0.t[:, 0:256], QQ, DD[:, 0:256], ALU.mult))
                V.done(nc_v.tensor_tensor(x0.t[:, 256:512], KK[:, 0:256], E0[:, 0:256], ALU.mult))
                V.done(nc_v.tensor_tensor(x0.t[:, 512:768], QQ, E0[:, 256:512], ALU.mult))
                t0 = V.done(nc_v.tensor_tensor(x0.t[:, 768:1024], KK[:, 256:512], DD[:, 256:512], ALU.mult))
                free["E0"] = [t0]
                V(te3, x1.free)
                for lev in range(1, 4):
                    half = 16 << lev
                    for d in range(2):
                        v = lambda ap: ap.rearrange("p (b s n) -> p b s n", s=2, n=half)
                        dst = v(x1.t[:, 512 * (lev - 1) + 256 * d:512 * (lev - 1) + 256 * d + 256])
                        e = v(D4[:, lev, d, :])
                        kk, qq = v(KK[:, 256 * d:256 * d + 256]), v(QQ)
                        V.done(nc_v.tensor_tensor(dst[:, :, d, :], kk[:, :, d, :], e[:, :, d, :], ALU.mult))
                        t1 = V.done(nc_v.tensor_tensor(dst[:, :, 1 - d, :], qq[:, :, 1 - d, :], e[:, :, 1 - d, :], ALU.mult))
                free["DD"] = free["KK"] = free["QQ"] = [t1]
                return x0, x1, gt, t1

            def mix(h, x0, x1, gt, tx):
                main, diag = ring.take(), ring.take()
                P(tx, main.free, diag.free)
                mm = nc.tensor.matmul
                qf, kf, qb, kb = (x0.t[:, 256 * i:256 * i + 256] for i in range(4))
                for tile in range(2):
                    for i in range(4):
                        o = 128 * tile + 32 * i
                        r = slice(32 * i, 32 * i + 32)
                        mm(main.t[r, 256 * tile + o:256 * tile + o + 32], kf[:, o:o + 32], qf[:, o:o + 32], start=True, stop=True)
                        mm(diag.t[r, 32 * tile:32 * tile + 32], kb[:, o:o + 32], qb[:, o:o + 32], start=True, stop=True)
                for lev in range(1, 4):
                    half = 16 << lev
                    xf_ = x1.t[:, 512 * (lev - 1):512 * (lev - 1) + 256]
                    xb_ = x1.t[:, 512 * (lev - 1) + 256:512 * lev]
                    for o in range(0, 256, 2 * half):
                        L_, R_ = slice(o, o + half), slice(o + half, o + 2 * half)
                        for x, ks, qs in ((xf_, L_, R_), (xb_, R_, L_)):
                            tile, r = ks.start // 128, ks.start % 128
                            last = mm(main.t[r:r + half, 256 * tile + qs.start:256 * tile + qs.stop], x[:, ks], x[:, qs],
                                      start=True, stop=True)
                tp = P.done(last)
                x0.free = [tp]
                x1.free = [tp]
                s = STr.take()
                t1 = V.done(V(tp, s.free, fz).tensor_tensor(s.t, main.t[:, :], C("m1"), ALU.mult))
                main.free = [t1]
                t2 = V.done(V(tp, free["UD"]).tensor_tensor(UD, diag.t[:, 0:64], C("mbc"), ALU.mult))
                diag.free = [t2]
                V(t1, t2)
                for i in range(4):
                    sv = s.t[32 * i:32 * i + 32, :]
                    ap = bass.AP(tensor=sv.tensor, offset=sv.offset + 32 * i, ap=[list(sv.ap[0]), [384, 2], [1, 32]])
                    uv = UD[32 * i:32 * i + 32, :].rearrange("p (a n) -> p a n", a=2)
                    ts = V.done(nc.vector.tensor_tensor(ap, ap, uv, ALU.add))
                free["UD"] = [ts]
                bank = ring.take()
                P(ts, tv, bank.free)
                for tt in range(2):
                    for sb_ in range(2):
                        last = mm(bank.t[:, 128 * tt:128 * tt + 128], s.t[:, 256 * sb_ + 128 * tt:256 * sb_ + 128 * tt + 128],
                                  VN[:, sb_, 128 * h:128 * h + 128], start=(sb_ == 0), stop=(sb_ == 1))
                tp = P.done(last)
                s.free = [tp]
                on, sc = ONr.take(), stat.take()
                tq = []
                for tt in range(2):
                    tq.append(A.done(A(tp, on.free, sc.free, fz).activation(
                        on.t[:, 128 * tt:128 * tt + 128], bank.t[:, 128 * tt:128 * tt + 128], ACT.Square,
                        accum_out=sc.t[:, tt:tt + 1])))
                t = rstd_of(sc.t[:, 2:4], sc.t[:, 0:2], 1.0 / 128, RMS_EPS, tq)
                for tt in range(2):
                    to = V.done(V(t, tq).tensor_scalar(on.t[:, 128 * tt:128 * tt + 128], bank.t[:, 128 * tt:128 * tt + 128],
                                                       sc.t[:, 2 + tt:3 + tt], None, ALU.mult))
                sc.free = [to]
                bank.free = [to]
                b2 = ring.take()
                P(to, b2.free)
                for tt in range(2):
                    last = nc.tensor.transpose(b2.t[:, 128 * tt:128 * tt + 128], on.t[:, 128 * tt:128 * tt + 128], ident)
                tp = P.done(last)
                t = V.done(V(tp).scalar_tensor_tensor(on.t, b2.t[:, 0:256], col("bng", h), gt.t, ALU.mult, ALU.mult))
                b2.free = [t]
                gt.free = [t]
                ms[h] = split_to(MS[:, h, 0:256], MS[:, h, 256:512], on.t, t)
                on.free = [ms[h]]

            g = gates(0)
            for h in range(8):
                nxt = gates(h + 1) if h < 7 else None
                mix(h, *g)
                g = nxt
            state["gb"] = [free["DD"]]
            last_p = ("p", P.n)
            state["yb"] = [[last_p], [last_p]]
            fz2 = fence()
            R2 = Arena()
            Pr = Ring([R2(512) for _ in range(3)])
            PTr = Ring([R2(512) for _ in range(2)])
            nmr = Ring([R2(8) for _ in range(4)])
            for ring_ in (Pr, PTr, nmr):
                for s in ring_.slots:
                    s.free = [fz2]
            heads = cross_heads(R2, "hg_x", xs, 1, fz2, ring, ms)
            attend(heads, False, Pr, PTr, nmr, ring)
            return natural("hg_o", MS, ms, 12, 1024, accs, 2)

        steps = [
            lambda xs: layer_norm(accs, even(xs), 0),
            lambda xs: layer_norm(accs, ffn(xs, 0, 1), 1),
            lambda xs: layer_norm(accs, odd(xs), 2),
            lambda xs: layer_norm(accs, ffn(xs, 1, 1), 3),
            lambda xs: rms_to_XS(state["xn"], lambda k: col("rg", k)),
            lambda xs: residual_rms(accs, window(xs), 0, lambda k: col("rg", 8 + k)),
            lambda xs: residual_rms(accs, ffn(xs, 0, 2), 1, lambda k: col("rg", 16 + k)),
            lambda xs: residual_rms(accs, hgrn(xs), 2, lambda k: col("rg", 24 + k)),
            lambda xs: residual_rms(accs, ffn(xs, 1, 2), 3, None),
        ]
        for step in steps:
            xs = step(xs)
        finish()


def constants():
    f = np.float32
    cc = np.zeros((128, NCC), f)
    p, j = np.arange(128)[:, None], np.arange(128)[None, :]

    def put(name, a):
        lo, hi = CC[name]
        cc[:, lo:hi] = a

    put("ident", p == j)
    put("cmf", np.where(j <= p, 0.0, -1e37))
    put("tril", p <= j)
    t = np.arange(256)
    put("m64", (t % 64 != 0)[None])
    put("ones", 1.0)
    m1 = np.ones((128, 2, 256))
    mb = np.zeros((128, 2, 32))
    for tile in range(2):
        for s in range(128):
            b = s // 32
            lo = 128 * tile + 32 * b
            m1[s, tile, lo:lo + 32] = (np.arange(lo, lo + 32) >= 128 * tile + s)
            mb[s, tile] = (np.arange(lo, lo + 32) <= 128 * tile + s)
    put("m1", m1.reshape(128, 512))
    put("mbc", mb.reshape(128, 64))
    inv = f(10000.0) ** (-np.arange(32, dtype=f) / f(32))
    ang = np.arange(256, dtype=f)[None, :] * inv[:, None].astype(f)
    put("cos", np.tile(np.cos(ang), (4, 1)))
    put("sin", np.tile(np.sin(ang), (4, 1)))
    rot = np.zeros((128, 128))
    for b in (0, 64):
        for i in range(32):
            rot[b + i + 32, b + i] = -1.0
            rot[b + i, b + i + 32] = 1.0
    put("rot", rot)
    cb = np.zeros((128, 384), f)
    cb[:, 0:128] = p == j
    cb[:, 128:256] = np.where(j <= p, 0.0, NEG)
    cb[:, 256:384] = np.where(j >= p, 0.0, NEG)
    n = np.maximum(255 - np.arange(384), 0)
    large = 16 + (np.log(np.maximum(n, 1).astype(f) / f(16)) / f(np.log(8.0)) * f(16)).astype(np.int32)
    bucket = np.where(n < 16, n, np.minimum(large, 31))
    onehot = (np.arange(32)[:, None] == bucket[None, :]).astype(f)
    return cc, cb, onehot


def layouts(d):
    a = {k: np.ascontiguousarray(np.asarray(v)) for k, v in d.items()}

    def tiles(w, cols):
        k = w.shape[0] // 128
        t = np.stack([w[:, c] for c in cols]).reshape(len(cols) // 2, 2, k, 128, 128)
        return np.ascontiguousarray(t.transpose(0, 3, 1, 2, 4)).reshape(len(cols) // 2, 128, -1)

    def rows(w):
        per = 2048 // w.shape[1]
        t = w.reshape(-1, per, 128, w.shape[1]).transpose(0, 2, 1, 3)
        return np.ascontiguousarray(t).reshape(-1, 128, 2048)

    def span(lo, n=1):
        return [np.arange(lo + 128 * i, lo + 128 * i + 128) for i in range(n)]

    r = {"x": a["x"], "mem_2": a["mem_2"], "od_sgu_g": a["od_sgu_g"], "od_sgu_b": a["od_sgu_b"]}
    mk = a["w_mem_kv_2"]
    r["mem_k"] = np.concatenate([tiles(mk[l], span(0, 4)) for l in range(2)])
    r["mem_v"] = np.concatenate([rows(mk[l][:, 512:]) for l in range(2)])
    w = a["ev_w_in"][0]
    fw = np.zeros((1024, 128), w.dtype)
    fw[:, 0:8] = fw[:, 32:40] = fw[:, 64:72] = fw[:, 96:104] = w[:, 2760:2768]
    fw[:, 8:16] = w[:, 1216:1224]
    wx = np.concatenate([w, fw], axis=1)
    kd = np.concatenate([np.arange(1152, 1216)] * 2)
    qa, ck, qi = span(0, 4), span(512), span(640, 4)
    qb, kb = span(1224, 4), span(1736, 4)
    r["ev_a"] = tiles(wx, span(2768) + [kd] + qi + ck + [qb[0], kb[0], qb[1], kb[1], qb[2], kb[2], qb[3]])
    r["ev_a"] = r["ev_a"][:7]
    ev_b = tiles(wx, [kb[3], qa[0], qa[1], qa[2]])
    r["ev_b"] = ev_b
    r["ev_c"] = tiles(wx, [qa[3], qa[3]])[:, :, 0:1024].copy()
    r["ev_v"] = rows(w[:, 2248:2760])
    r["ev_o"] = rows(a["ev_w_o"][0])
    r["w_uk"] = np.ascontiguousarray(a["ev_w_uk"][0].reshape(4, 2, 128, 64).transpose(1, 3, 0, 2)).reshape(128, 512)
    r["w_uv"] = np.ascontiguousarray(a["ev_w_uv"][0].transpose(1, 0, 2)).reshape(128, 512)
    for name, src, dn in (("1", "ffn_w_up", "ffn_w_down"), ("2", "ffn_w_in_2", "ffn_w_out_2")):
        r["up" + name] = np.concatenate([
            tiles(a[src][l], [c for j in range(22) for c in (span(128 * j)[0], span(2816 + 128 * j)[0])]) for l in range(2)])
        r["down" + name] = np.concatenate([rows(a[dn][l]) for l in range(2)])
    w = a["od_w_in"][0]
    u, gb_, gc, z = span(0, 4), span(1024, 4), span(1536, 4), span(2048, 4)
    r["od_v"] = rows(w[:, 512:1024])
    r["od_t"] = tiles(w, u + [c for i in range(4) for c in (gc[i], z[i])] + gb_)
    r["od_o"] = rows(a["od_w_o"][0])
    r["sgu_w"] = np.ascontiguousarray(a["od_sgu_w"][0].transpose(2, 0, 1)).reshape(128, 1024)
    w = a["a_w_in_2"][0]
    pair = [np.concatenate([np.arange(64 * (8 * (c // 4) + c % 4), 64 * (8 * (c // 4) + c % 4) + 64),
                            np.arange(64 * (8 * (c // 4) + c % 4 + 4), 64 * (8 * (c // 4) + c % 4 + 4) + 64)])
            for c in range(8)]
    r["wa_k"] = tiles(w, span(1024, 2))
    r["wa_v"] = rows(w[:, 1280:1536])
    r["wa_q"] = tiles(w, pair)
    r["wa_x"] = tiles(w, span(1536, 4))
    order = np.concatenate(pair + [np.arange(1024, 1536)])
    r["wa_o"] = rows(a["a_w_out_2"][0][order])
    w = a["b_w_in_2"][0]
    r["hg_v"] = rows(w[:, 1024:2048])
    r["hg_t"] = tiles(w, [c for h in range(8) for c in (
        span(2048 + 128 * h)[0], span(3072 + 128 * h)[0], span(128 * h)[0], span(4096 + 128 * h)[0])])
    r["hg_x"] = tiles(w, span(5120, 4))
    r["hg_o"] = rows(a["b_w_out_2"][0])
    r["c_ln"] = np.stack([a["ln_g"].reshape(4, 1024), a["ln_b"].reshape(4, 1024)], axis=1).reshape(4, 1, 2048)
    ng = a["norm_g_2"]
    r["c_rg"] = np.stack([ng[0, 1], ng[0, 3], ng[1, 1], ng[1, 3]]).reshape(4, 1, 1024)
    cc, cb, onehot = constants()
    par = np.zeros((128, NPC), np.float32)

    def put(name, v):
        lo, hi = PC[name]
        par[:v.shape[0], lo:hi] = v

    def cols(v):
        v = v.reshape(-1, v.shape[-1] // 128, 128)
        return v.transpose(2, 0, 1).reshape(128, -1)

    put("ln", cols(r["c_ln"].reshape(4, 2, 1024)))
    put("rg", cols(np.stack([ng[0, 0], ng[0, 2], ng[1, 0], ng[1, 2]])))
    put("memg", cols(a["mem_norm_g_2"][None]))
    put("fc1", a["ffn_conv_w"].reshape(2, 3, 44, 128).transpose(3, 0, 2, 1).reshape(128, -1))
    put("fc2", a["ffn_conv_w_2"].reshape(2, 3, 22, 128).transpose(3, 0, 2, 1).reshape(128, -1))
    put("fb2", cols(a["ffn_conv_b_2"]))
    put("oc", a["od_conv_w"].reshape(3, 4, 128).transpose(2, 1, 0).reshape(128, -1))
    put("bng", cols(a["b_norm_g_2"]))
    put("lbl", a["b_lb_logits_2"].reshape(2, 2, 8, 128).transpose(3, 1, 0, 2).reshape(128, -1))
    bf = np.zeros((104, 1), np.float32)
    bf[0:8, 0] = bf[32:40, 0] = bf[64:72, 0] = bf[96:104, 0] = a["ev_b_f"][0]
    put("bf", bf)
    put("sink", np.tile(a["a_sink_2"], (128, 1)))
    put("relb", a["rel_bias"])
    r["c_f32"], r["c_par"], r["c_onehot"], r["c_mask"] = cc, par, onehot, cb
    return r


def kernel(**inputs):
    import concourse.bacc as bacc
    from concourse.bass_utils import run_bass_kernel_spmd as run

    r = layouts(inputs)
    nc = bacc.Bacc("TRN2", target_bir_lowering=False, num_devices=1)
    T = {k: nc.dram_tensor(f"in_{k}", v.shape, mybir.dt.from_np(v.dtype), kind="ExternalInput").ap() for k, v in r.items()}
    out = nc.dram_tensor("out_0", (1, 256, 1024), F32, kind="ExternalOutput").ap()
    program(nc, T, out)
    res = run(nc, [{f"in_{k}": v for k, v in r.items()}], core_ids=[0])
    return res.results[0]["out_0"]
```

```python
from contextlib import ExitStack

import numpy as np

import concourse.bass as bass
from concourse import mybir

F32 = mybir.dt.float32
F32R = mybir.dt.float32r
BF16 = mybir.dt.bfloat16
I32 = mybir.dt.int32
ALU = mybir.AluOpType
ACT = mybir.ActivationFunctionType
AX = mybir.AxisListType

ALPHA = 4.0 ** 0.25
LN_EPS = 1e-5
RMS_EPS = 1e-6
NEG = -1e30
TAKEN = -3e38
NRAW = 3
NSPLIT = 3
AHEAD = 2
ARENA = 14280


def schedule():
    s = []

    def add(name, n, w=2048, first=0):
        s.extend((name, i, w) for i in range(first, first + n))

    def ffn(name_up, name_down, layer):
        ups = [(name_up, layer * 22 + j, 2048) for j in range(22)]
        for m in range(11):
            s.extend(ups[2 * m:2 * m + 2])
            if 0 < m < 10:
                s.append((name_down, layer * 11 + m - 1, 2048))
        s.extend((name_down, layer * 11 + m, 2048) for m in (9, 10))

    for l in range(2):
        add("mem_k", 2, first=2 * l)
        add("mem_v", 2, first=2 * l)
    add("ev_a", 7)
    add("ev_v", 2)
    add("ev_b", 2)
    add("ev_c", 1, 1024)
    add("ev_o", 4)
    ffn("up1", "down1", 0)
    add("od_v", 2)
    add("od_t", 8)
    add("od_o", 4)
    ffn("up1", "down1", 1)
    add("wa_k", 1)
    add("wa_v", 1)
    add("wa_q", 4)
    add("wa_x", 2)
    add("wa_o", 6)
    ffn("up2", "down2", 0)
    add("hg_v", 4)
    add("hg_t", 16)
    add("hg_x", 2)
    add("hg_o", 6)
    ffn("up2", "down2", 1)
    return s


CC = {}
_n = 0
for _name, _w in (("ident", 128), ("cmf", 128), ("tril", 128), ("m64", 256), ("ones", 256), ("m1", 512),
                  ("mbc", 64), ("cos", 256), ("sin", 256), ("rot", 128)):
    CC[_name] = (_n, _n + _w)
    _n += _w
NCC = _n
PC = {}
_n = 0
for _name, _w in (("ln", 64), ("rg", 32), ("memg", 8), ("fc1", 264), ("fc2", 132), ("fb2", 44), ("oc", 12),
                  ("bng", 8), ("lbl", 32), ("bf", 1), ("sink", 16), ("relb", 8)):
    PC[_name] = (_n, _n + _w)
    _n += _w
NPC = _n


class Engine:

    def __init__(self, key, eng, sems):
        self.key, self.eng, self.sems, self.n, self.seen = key, eng, sems, 0, {}

    def __call__(self, *tokens):
        need = {}
        stack = list(tokens)
        while stack:
            t = stack.pop()
            if t is None:
                continue
            if isinstance(t, list):
                stack.extend(t)
            else:
                need[t[0]] = max(need.get(t[0], 0), t[1])
        for key, value in sorted(need.items()):
            if self.seen.get(key, 0) < value:
                self.eng.wait_ge(self.sems[key], value)
                self.seen[key] = value
        return self.eng

    def done(self, instruction):
        self.n += 1
        instruction.then_inc(self.sems[self.key], 1)
        return (self.key, self.n)


class Slot:
    def __init__(self, t):
        self.t, self.free = t, []


class Ring:
    def __init__(self, tiles):
        self.slots, self.i = [x if isinstance(x, Slot) else Slot(x) for x in tiles], 0

    def take(self):
        s = self.slots[self.i % len(self.slots)]
        self.i += 1
        return s


def program(nc, T, out):
    with ExitStack() as ctx:
        sems = {}

        def sem(name):
            sems[name] = ctx.enter_context(nc.semaphore("s_" + name))

        def sb(name, shape, dt=F32):
            return ctx.enter_context(nc.sbuf_tensor(name, shape, dt))

        for k in "vagp":
            sem(k)
        V = Engine("v", nc.vector, sems)
        A = Engine("a", nc.scalar, sems)
        G = Engine("g", nc.gpsimd, sems)
        P = Engine("p", nc.tensor, sems)
        SP = Engine("sp", nc.sync, sems)
        dma_n = {}

        def dma(name, dst, src, *tokens):
            if name not in sems:
                sem(name)
                dma_n[name] = 0
            dma_n[name] += 16
            SP(*tokens).dma_start(dst, src).then_inc(sems[name], 16)
            return (name, dma_n[name])

        raw = [sb(f"raw{i}", [128, 2048]) for i in range(NRAW)]
        whi = [sb(f"whi{i}", [128, 2048], F32R) for i in range(NSPLIT)]
        wlo = [sb(f"wlo{i}", [128, 2048], F32R) for i in range(NSPLIT)]
        XS = sb("XS", [128, 8, 512], F32R)
        MS = sb("MS", [128, 12, 512], F32R)
        xn = sb("xn", [128, 2, 1024])
        yb = sb("yb", [128, 2, 1024])
        gb = sb("gb", [128, 2, 1024])
        cc = sb("cc", [128, NCC])
        pc = sb("pc", [128, NPC])
        cb = sb("cb", [128, 384], BF16)
        st = sb("st", [128, 64])
        nw = sb("nw", [128, 32])
        lb = sb("lb", [128, 48])
        ar = sb("ar", [128, ARENA])
        banks = [Slot(ctx.enter_context(nc.psum_tensor(f"ps{i}", [128, 512], F32))) for i in range(8)]
        low, high = banks[0:4], Ring(banks[4:8])
        allb = Ring(banks)

        def C(name, rows=128):
            a, b = CC[name]
            return cc[0:rows, a:b]

        def col(name, i=0, rows=128):
            a = PC[name][0] + i
            return pc[0:rows, a:a + 1]

        ident = C("ident")
        identb, cmb, cmb2 = cb[:, 0:128], cb[:, 128:256], cb[:, 256:384]

        class Arena:
            def __init__(self):
                self.at = 0

            def __call__(self, n):
                a = self.at
                self.at += n
                assert self.at <= ARENA, self.at
                return ar[:, a:a + n]

        def fence():
            return [(e.key, e.n) for e in (V, A, G, P)]

        mhalf = st[:, 60:61]
        t_half = V.done(V().memset(mhalf, -0.5))
        t_mem = [dma(f"d_mem{i}", gb[:, i, :], T["mem_2"][0, 128 * i:128 * i + 128]) for i in range(2)]
        t_pc = dma("d_pc", pc[:, :], T["c_par"])
        t_id = dma("d_id", cc[:, 0:128], T["c_f32"][:, 0:128])

        sched = schedule()

        class Stream:
            def __init__(self):
                self.pos = self.loaded = self.split_n = 0
                self.share = 3
                self.raw_free = [[] for _ in range(NRAW)]
                self.landed = {}
                self.ready = {}
                self.used = [[] for _ in range(NSPLIT)]

            def load(self):
                m = self.loaded
                if m >= len(sched):
                    return
                name, i, w = sched[m]
                r = m % NRAW
                self.landed[m] = dma(f"d_w{r}", raw[r][:, 0:w], T[name][i], self.raw_free[r])
                self.loaded += 1

            def split(self, share):
                m = self.split_n
                if m >= len(sched):
                    return
                w = sched[m][2]
                r, s = m % NRAW, m % NSPLIT
                a = w // 4 * share
                th = A.done(A(self.landed[m], self.used[s]).activation(whi[s][:, 0:w], raw[r][:, 0:w], ACT.Copy))
                tg = G.done(G(th, self.landed[m], self.used[s]).tensor_tensor(
                    wlo[s][:, 0:a], raw[r][:, 0:a], whi[s][:, 0:a].bitcast(F32), ALU.subtract))
                tv = V.done(V(th, self.landed[m], self.used[s]).tensor_tensor(
                    wlo[s][:, a:w], raw[r][:, a:w], whi[s][:, a:w].bitcast(F32), ALU.subtract)) if a < w else None
                self.raw_free[r] = [tg, tv]
                self.ready[m] = [th, tg, tv]
                self.split_n += 1
                self.load()

            def get(self, name, ahead=0):
                m = self.pos + ahead
                assert sched[m][0] == name, (sched[m], name)
                return whi[m % NSPLIT], wlo[m % NSPLIT], self.ready[m]

            def fill(self, ahead=AHEAD, share=None):
                share = share or self.share
                while self.split_n < self.pos + ahead and self.split_n < len(sched):
                    self.split(share)

            def done(self, tok, fill=True):
                self.used[self.pos % NSPLIT] = [tok]
                self.pos += 1
                if fill:
                    self.fill()
                if later and self.pos % 2:
                    later.pop(0)()

        later = []
        W = Stream()
        W.load()
        t_oh = dma("d_oh", ar[0:32, 5000:5384], T["c_onehot"])
        for _ in range(NRAW - 1):
            W.load()

        def split_to(hi, lo, src, *tokens):
            th = A.done(A(*tokens).activation(hi, src, ACT.Copy))
            return V.done(V(th, *tokens).tensor_tensor(lo, src, hi.bitcast(F32), ALU.subtract))

        def at(xs, k):
            return [x[k * len(x) // 8] for x in xs]

        def project_T(name, xs_ready, ring, XS=XS):
            hi, lo, ready = W.get(name)
            tiles = sched[W.pos][2] // 1024
            bank = ring.take()
            P(ready, bank.free)
            for i in range(tiles):
                o = bank.t[:, 256 * i:256 * i + 256]
                for k in range(8):
                    P(at(xs_ready, k))
                    c = slice(1024 * i + 128 * k, 1024 * i + 128 * k + 128)
                    nc.tensor.matmul(o, hi[:, c], XS[:, k, 0:256], start=(k == 0), stop=False)
                    nc.tensor.matmul(o, hi[:, c], XS[:, k, 256:512], start=False, stop=False)
                    last = nc.tensor.matmul(o, lo[:, c], XS[:, k, 0:256], start=False, stop=(k == 7))
            tok = P.done(last)
            W.done(tok)
            return bank, tok

        def accumulate(name, S, ks, ready, n, accs, first, last, count=1, by_tile=False, held=False):
            per = 2048 // n
            toks = []
            if held:
                W.fill(NSPLIT)
            got = [W.get(name, i) for i in range(count)]
            halves = [[h] for h in range(2)] if held else [list(range((n + 511) // 512))]
            for tt in range(2):
                toks.append([])
                for hs_ in halves:
                    for i, (hi, lo, wready) in enumerate(got):
                        P(wready)
                        for j in range(per):
                            k = ks[i * per + j]
                            P(ready[k][tt] if by_tile else ready[k])
                            sh = S[:, k, 128 * tt:128 * tt + 128]
                            sl = S[:, k, 256 + 128 * tt:384 + 128 * tt]
                            begin = first and i == 0 and j == 0
                            end = last and i == count - 1 and j == per - 1
                            for lhs, w in ((sh, hi), (sh, lo), (sl, hi)):
                                for h in hs_:
                                    acc = accs[tt][h]
                                    if begin and lhs is sh and w is hi:
                                        P(acc.free)
                                    c = min(n, 512)
                                    ins = nc.tensor.matmul(acc.t[:, 0:c], lhs, w[:, n * j + c * h:n * j + c * h + c],
                                                           start=(begin and lhs is sh and w is hi),
                                                           stop=(end and lhs is sl))
                    toks[-1].append(P.done(ins))
            for _ in range(count):
                W.done(toks[-1], not held)
            return toks

        def natural(name, S, ready, K, n, accs, hold=1, lead=1):
            per = 2048 // n
            chunks = K // per
            if hold > 1:
                load_gains()
            if lead > 1:
                groups = [lead] + [1] * (chunks - lead - hold) + [hold] * (chunks > lead)
            else:
                groups = [1] * (chunks - hold) + [hold]
            c = 0
            for g in groups:
                t = accumulate(name, S, list(range(c * per, (c + g) * per)), ready, n, accs, c == 0, c + g == chunks, g, lead > 1, hold > 1 and c + g == chunks)
                c += g
            return t

        xf = Ring([sb(f"xf{i}", [128, 256]) for i in range(4)])

        def to_XS(tt, tok, src, rhs, g, b, aside, XS=XS):
            toks = []
            for q in range(4):
                bank = high.take()
                P(tok, bank.free)
                for i in range(2):
                    k = 2 * q + i
                    o, x = bank.t[:, 128 * i:128 * i + 128], src[:, tt, 128 * k:128 * k + 128]
                    last = nc.tensor.transpose(o, x, ident) if rhs is ident else \
                        nc.tensor.matmul(o, x, rhs, start=True, stop=True)
                tp = P.done(last)
                hi = XS[:, 2 * q:2 * q + 2, 128 * tt:128 * tt + 128]
                lo = XS[:, 2 * q:2 * q + 2, 256 + 128 * tt:384 + 128 * tt]
                if b is None and not aside:
                    for i in range(2):
                        th = A.done(A(tp).activation(hi[:, i, :], bank.t[:, 128 * i:128 * i + 128], ACT.Identity,
                                                     scale=g(2 * q + i)))
                    for i in range(2):
                        t = V.done(V(th).scalar_tensor_tensor(lo[:, i, :], bank.t[:, 128 * i:128 * i + 128], g(2 * q + i),
                                                              hi[:, i, :].bitcast(F32), ALU.mult, ALU.subtract))
                    bank.free = [t]
                    toks.append(t)
                    continue
                x = xf.take()
                for i in range(2):
                    k = 2 * q + i
                    o, dst = bank.t[:, 128 * i:128 * i + 128], x.t[:, 128 * i:128 * i + 128]
                    if q % 2 or aside:
                        te = A.done(A(tp, x.free).activation(dst, o, ACT.Identity, scale=g(k), bias=b(k) if b else 0.0))
                    else:
                        te = V.done(V(tp, x.free).tensor_scalar(dst, o, g(k), b(k) if b else None,
                                                                ALU.mult, ALU.add if b else ALU.bypass))
                bank.free = [te]
                xv = x.t[:, :].rearrange("p (k t) -> p k t", k=2)
                th = A.done(A(te).activation(hi, xv, ACT.Copy))
                E = G if aside else V
                t = E.done(E(th, te).tensor_tensor(lo, xv, hi.bitcast(F32), ALU.subtract))
                x.free = [t]
                toks.append(t)
            return toks

        def rstd_of(dst, src, scale, eps, tok, between=lambda: None):
            n = src.shape[1]
            a, b, y = nw[:, 0:n], nw[:, 16:16 + n], dst
            t = V.done(V(tok).tensor_scalar(a, src, scale, eps, ALU.mult, ALU.add))
            ty = V.done(V(t).tensor_scalar(y.bitcast(I32), a.bitcast(I32), -0.5, 1597463007.0, ALU.mult, ALU.add))
            t = V.done(V(ty).tensor_scalar(a, a, -0.5, None, ALU.mult))
            for _ in range(3):
                between()
                t = V.done(V(t).tensor_tensor(b, y, y, ALU.mult))
                between()
                t = V.done(V(t).tensor_tensor(b, b, a, ALU.mult))
                between()
                t = V.done(V(t).scalar_tensor_tensor(y, b, 1.5, y, ALU.add, ALU.mult))
            return t

        def rstd_one(dst, src, scale, eps, tok):
            t = V.done(V(tok).tensor_scalar(dst, src, scale, eps, ALU.mult, ALU.add))
            return G.done(G(t, t_half).tensor_tensor(dst, dst, mhalf, ALU.pow))

        state = {"xn": [None, None], "yb": [[], []], "gb": []}

        gains = [(T["c_ln"][i], 2) for i in range(4)] + [(T["c_rg"][i], 1) for i in range(4)]

        def load_gains():
            assert not later
            src, rows = gains.pop(0)
            n = 1024 * rows
            ap = bass.AP(tensor=src.tensor, offset=src.offset, ap=[[0, 128], [1, n]])
            state["t_gb"] = dma("d_gb", gb[:, 0:rows, :].rearrange("p a d -> p (a d)"), ap, state["gb"])

        def weave(steps, order):
            for i in order:
                if i is None:
                    W.fill(2, 4)
                else:
                    next(steps[i])

        def layer_norm(accs, toks, idx):
            t_gb = state["t_gb"]
            ready, post = [None, None], [None, None]

            def tile(tt):
                o = 32 * tt
                for h in range(2):
                    c = slice(512 * h, 512 * h + 512)
                    t = V.done(V(toks[tt][h], state["xn"][tt], state["yb"][tt]).scalar_tensor_tensor(
                        yb[:, tt, c], xn[:, tt, c], ALPHA, accs[tt][h].t[:, :], ALU.mult, ALU.add))
                    accs[tt][h].free = [t]
                    t = V.done(V(t).bn_stats(st[:, o + 6 * h:o + 6 * h + 6], yb[:, tt, c]))
                t = V.done(V(t).bn_aggr(st[:, o + 12:o + 14], st[:, o:o + 12]))
                t = rstd_one(st[:, o + 14:o + 15], st[:, o + 13:o + 14], 1.0, LN_EPS, t)
                t = V.done(V(t).tensor_scalar(yb[:, tt, :], yb[:, tt, :], st[:, o + 12:o + 13], st[:, o + 14:o + 15],
                                              ALU.subtract, ALU.mult))
                post[tt] = t
                yield
                if idx == 3:
                    E = V if tt else G
                    cs = [slice(0, 512), slice(512, 1024)]
                    ts = [E.done(E(t, t_gb).tensor_tensor(xn[:, tt, c], yb[:, tt, c], gb[:, 0, c], ALU.mult)) for c in cs]
                    ts = [E.done(E(t).tensor_tensor(xn[:, tt, c], xn[:, tt, c], gb[:, 1, c], ALU.add))
                          for c, t in zip(cs, ts)]
                    state["xn"][tt] = state["yb"][tt] = ts
                    post[tt] = ts
                    yield from rms_steps(tt, ts, lambda k: col("rg", k), ready)
                ready[tt] = to_XS(tt, t, yb, ident, lambda k: col("ln", 16 * idx + k), lambda k: col("ln", 16 * idx + 8 + k),
                                  tt == 0)
                yield

            if idx == 3:
                weave([tile(0), tile(1)], [0, 0, 1, 1, 0, 1, 0, None, 1])
                state["gb"] = post
                return ready
            weave([tile(0), tile(1)], [0, 1, 0, None, 1])

            def scaled(tt):
                t = G.done(G(post[tt], t_gb).tensor_tensor(xn[:, tt, :], yb[:, tt, :], gb[:, 0, :], ALU.mult))
                state["xn"][tt] = t
                state["yb"][tt] = [t, ready[tt]]

            def shifted(tt):
                t = G.done(G(state["xn"][tt]).tensor_tensor(xn[:, tt, :], xn[:, tt, :], gb[:, 1, :], ALU.add))
                state["xn"][tt] = t
                state["gb"] = [state["gb"], t]

            for tt in range(2):
                later.append(lambda tt=tt: scaled(tt))
                later.append(lambda tt=tt: shifted(tt))
            return ready

        def rms_steps(tt, toks, gain, out, XS=XS, xn=xn, aside=True):
            o = 32 * tt
            for h in range(2):
                t = A.done(A(toks[h], state["yb"][tt]).activation(
                    yb[:, tt, 512 * h:512 * h + 512], xn[:, tt, 512 * h:512 * h + 512], ACT.Square,
                    accum_out=st[:, o + 16 + h:o + 17 + h]))
            yield
            t = V.done(V(t).tensor_tensor(st[:, o + 20:o + 21], st[:, o + 16:o + 17], st[:, o + 17:o + 18], ALU.add))
            t = (rstd_one if aside else rstd_of)(st[:, o + 21:o + 22], st[:, o + 20:o + 21], 1.0 / 1024, RMS_EPS, t)
            diag = yb[:, tt, 0:128]
            t = V.done(V(t).tensor_scalar(diag, ident, st[:, o + 21:o + 22], None, ALU.mult))
            yield
            out[tt] = to_XS(tt, t, xn, diag, gain, None, aside and tt == 0, XS)
            state["yb"][tt] = [out[tt]]
            yield

        def residual_rms(accs, toks, idx, gain):
            t_gb = state["t_gb"]
            ready, users = [None, None], []

            def tile(tt):
                o = 32 * tt
                sums = []
                for h in range(2):
                    sums.append(A.done(A(toks[tt][h], state["yb"][tt]).activation(
                        yb[:, tt, 512 * h:512 * h + 512], accs[tt][h].t[:, :], ACT.Square,
                        accum_out=st[:, o + 22 + h:o + 23 + h])))
                yield
                t = V.done(V(sums).tensor_tensor(st[:, o + 24:o + 25], st[:, o + 22:o + 23], st[:, o + 23:o + 24], ALU.add))
                t = rstd_one(st[:, o + 25:o + 26], st[:, o + 24:o + 25], 1.0 / 1024, RMS_EPS, t)
                yield
                halves = []
                for h in range(2):
                    c = slice(512 * h, 512 * h + 512)
                    t2 = V.done(V(t, t_gb, sums[h]).scalar_tensor_tensor(
                        yb[:, tt, c], accs[tt][h].t[:, :], st[:, o + 25:o + 26], gb[:, 0, c], ALU.mult, ALU.mult))
                    accs[tt][h].free = [t2]
                    halves.append(V.done(V(t2, state["xn"][tt]).tensor_tensor(xn[:, tt, c], xn[:, tt, c], yb[:, tt, c],
                                                                              ALU.add)))
                users.append(t2)
                state["xn"][tt] = halves
                state["yb"][tt] = halves
                if gain:
                    yield from rms_steps(tt, halves, gain, ready)
                yield

            weave([tile(0), tile(1)], [0, 0, 0, 1, 0, 1, 0, 1, 1, None, 1] if gain else [0, 0, 1, 1, 0, 1])
            state["gb"] = users
            return ready

        def finish():
            SP([dma(f"d_out{tt}", out[0, 128 * tt:128 * tt + 128], xn[:, tt, :], state["xn"][tt]) for tt in range(2)])

        accs = [[low[0], low[1]], [low[2], low[3]]]

        def attend(*args):
            for _ in attend_steps(*args):
                pass

        def attend_steps(heads, causal, Pr, PTr, nmr, ring):
            n = 384 if causal else 512
            segs = [(0, 128), (128, 384)] if causal else [(0, 256), (256, 512)]

            def top(h):
                head = heads[h]
                sink = head.get("sink")
                bank = ring.take()
                P(bank.free)
                tok = head["score"](bank.t)
                nm = nmr.take()
                V(tok, nm.free)
                if causal:
                    for i, (a, b) in enumerate(segs):
                        t = V.done(nc.vector.tensor_reduce(nm.t[:, i:i + 1], bank.t[:, a:b], AX.X, ALU.max, negate=True))
                else:
                    t = V.done(nc.vector.tensor_reduce(nm.t[:, 0:2], bank.t[:, :].rearrange("p (t s) -> p t s", t=2),
                                                       AX.X, ALU.max, negate=True))
                if sink is not None:
                    t = V.done(V(t).tensor_scalar(nm.t[:, 0:2], nm.t[:, 0:2], sink[1], None, ALU.min))
                return bank, nm, t

            def soft(h, bank, nm, t):
                sink = heads[h].get("sink")
                p = Pr.take()
                A(t, p.free)
                ta = []
                for i, (a, b) in enumerate(segs):
                    ta.append(A.done(nc.scalar.activation(p.t[:, a:b], bank.t[:, a:b], ACT.Exp, bias=nm.t[:, i:i + 1],
                                                          accum_out=nm.t[:, 2 + i:3 + i])))
                bank.free = [ta[1]]
                if sink is not None:
                    ta.append(A.done(A(t).activation(nm.t[:, 6:8], nm.t[:, 0:2], ACT.Exp, bias=sink[0])))
                return p, nm, ta

            def normalise(h, p, nm, ta):
                if heads[h].get("sink") is not None:
                    ta = [V.done(V(ta).tensor_tensor(nm.t[:, 2:4], nm.t[:, 2:4], nm.t[:, 6:8], ALU.add)), ta]
                t = V.done(V(ta).reciprocal(nm.t[:, 4:6], nm.t[:, 2:4]))
                tn = []
                for i, (a, b) in enumerate(segs):
                    tn.append(V.done(V(t, ta).tensor_scalar(p.t[:, a:b], p.t[:, a:b], nm.t[:, 4 + i:5 + i], None, ALU.mult)))
                nm.free = tn
                return p, tn

            def turn(h, p, tn):
                bank = ring.take()
                P(tn, bank.free)
                if causal:
                    pairs = [(0, 0), (128, 128), (256, 256)]
                else:
                    pairs = [(0, 0), (128, 256), (256, 128), (384, 384)]
                for a, b in pairs:
                    last = nc.tensor.transpose(bank.t[:, b:b + 128], p.t[:, a:a + 128], ident)
                tp = P.done(last)
                p.free = [tp]
                pt = PTr.take()
                if h % 2:
                    t = V.done(V(tp, pt.free).tensor_copy(pt.t[:, 0:n], bank.t[:, 0:n]))
                else:
                    t = A.done(A(tp, pt.free).activation(pt.t[:, 0:n], bank.t[:, 0:n], ACT.Copy))
                bank.free = [t]
                return pt, t

            H = len(heads)
            ex, ps, pts = {}, {}, {}
            tops = {}
            for i in range(-2, H + 6):
                if 0 <= i < H:
                    tops[i] = top(i)
                if 0 <= i - 2 < H:
                    ps[i - 2] = normalise(i - 2, *ex[i - 2])
                if 0 <= i - 3 < H:
                    pts[i - 3] = turn(i - 3, *ps[i - 3])
                if 0 <= i - 4 < H:
                    pt, t = pts[i - 4]
                    pt.free = [heads[i - 4]["value"](pt.t, t)]
                if 0 <= i - 5 < H and "post" in heads[i - 5]:
                    heads[i - 5]["post"]()
                if i + 2 < H and "prep" in heads[i + 2]:
                    heads[i + 2]["prep"]()
                if 0 <= i < H:
                    ex[i] = soft(i, *tops[i])
                yield

        kv = [ar[:, 1024 * i:1024 * i + 1024] for i in range(4)]
        onehot, rb = ar[:, 5000:5384], ar[:, 5400:8472]
        skew = nc.dram_tensor("scr_bias", (8, 128 * 384), F32, kind="Internal").ap()
        xm = [None, None]
        steps = [rms_steps(tt, [t_mem[tt]] * 2, lambda k: col("memg", k), xm, MS, gb, False) for tt in range(2)]
        weave(steps, [0, 1])
        A(t_pc)
        V(t_id)
        P(t_id)
        weave(steps, [0, 1])
        W.fill(1)
        V(t_pc)
        weave(steps, [0, 1])
        trb, rows_ = [], Ring(low)
        for h in range(8):
            bank = rows_.take()
            a = PC["relb"][0] + h
            tp = P.done(P(t_oh, t_pc, bank.free).matmul(bank.t[:, 0:384], pc[0:32, a:a + 1].to_broadcast([32, 128]),
                                                       onehot[0:32, :], start=True, stop=True))
            t = V.done(V(tp).tensor_copy(rb[:, 384 * h:384 * h + 384], bank.t[:, 0:384]))
            bank.free = [t]
            trb.append(t)
        W.fill()

        scr = nc.dram_tensor("scr_mem", (4, 128, 1024), F32, kind="Internal").ap()
        state["gb"] = fence()[0:2]
        t_x = [dma(f"d_x{i}", xn[:, i, :], T["x"][0, 128 * i:128 * i + 128]) for i in range(2)]
        t_w = dma("d_skw", skew.rearrange("h (p n) -> p h n", n=384), rb.rearrange("p (h n) -> p h n", h=8), trb)
        t_cc = dma("d_cc", cc[:, 128:], T["c_f32"][:, 128:])
        t_cb = dma("d_cb", ar[:, 8500:8884], T["c_mask"])
        t_scr = []
        xs = []
        state["xn"] = list(t_x)
        for l in range(2):
            tk = []
            for j in range(2):
                bank, tok = project_T("mem_k", xm, high, MS)
                t = A.done(A(tok).activation(kv[2 * l][:, 512 * j:512 * j + 512], bank.t[:, :], ACT.Copy))
                bank.free = [t]
                tk.append(t)
            t_scr.append(dma(f"d_scr{2 * l}", scr[2 * l], kv[2 * l], tk))
            acc = [[low[2 * l]], [low[2 * l + 1]]]
            toks = natural("mem_v", MS, [at(xm, k) for k in range(8)], 8, 512, acc)
            tv = []
            for tt in range(2):
                t = V.done(V(toks[tt]).tensor_copy(kv[2 * l + 1][:, 512 * tt:512 * tt + 512], acc[tt][0].t[:, :]))
                acc[tt][0].free = [t]
                tv.append(t)
            t_scr.append(dma(f"d_scr{2 * l + 1}", scr[2 * l + 1], kv[2 * l + 1], tv))
            if l == 0:
                t_cb = V.done(V(t_cb).tensor_copy(cb[:, :], ar[:, 8500:8884]))
                P(t_cc, t_cb)
                for tt in range(2):
                    r = []
                    for q in range(2):
                        bank = high.take()
                        P(t_x[tt], bank.free)
                        for i in range(4):
                            k = 4 * q + i
                            last = nc.tensor.transpose(bank.t[:, 128 * i:128 * i + 128], xn[:, tt, 128 * k:128 * k + 128],
                                                       ident)
                        tp = P.done(last)
                        bv = bank.t[:, :].rearrange("p (k t) -> p k t", k=4)
                        t2 = split_to(XS[:, 4 * q:4 * q + 4, 128 * tt:128 * tt + 128],
                                      XS[:, 4 * q:4 * q + 4, 256 + 128 * tt:384 + 128 * tt], bv, tp)
                        bank.free = [t2]
                        r.append(t2)
                    xs.append(r)

        def even(xs):
            fz = [t_w, fence(), t_scr]
            R = Arena()
            Bh, RH = R(2048), gb[:, :, :].rearrange("p a d -> p (a d)")
            L, FW, FZ, CT = R(256), R(256), R(256), R(256)
            QI, KI, QB, KB, QA, VB = R(1024), R(256), R(1024), R(1024), R(1024), R(1024)
            CN, WK, WV = R(256), R(512), R(512)
            S, WI, M8 = R(384), R(32), R(16)
            rr = Ring([R(384) for _ in range(2)])
            MB = R(192).bitcast(BF16)
            Pr = Ring([R(384) for _ in range(3)] + rr.slots[0:1])
            PTr = Ring([R(384) for _ in range(2)])
            nmr = Ring([R(8) for _ in range(4)])
            QLr = Ring([R(256) for _ in range(2)])
            OAr = Ring([R(256) for _ in range(2)])
            W.share = 4
            t_bh = dma("d_bh", Bh.rearrange("p (h n) -> p h n", h=8),
                       bass.AP(tensor=skew.tensor, offset=127, ap=[[383, 128], [128 * 384, 8], [1, 256]]), fz)
            t_wk = dma("d_wk", WK, T["w_uk"], fz)
            t_wv = dma("d_wv", WV, T["w_uv"], fz)
            t0 = V.done(V(fz).memset(L, 0.0))
            t0 = V.done(V(t0).memset(L[32:40, :], 1.0))
            t0 = V.done(V(t0).memset(L[96:104, :], 1.0))
            t0 = V.done(V(t0).memset(RH, 0.0))
            ring = allb

            def out_of(bank, i, dst, tok, scale=1.0, rows=128):
                return A.done(A(tok, fz).activation(dst, bank.t[0:rows, 256 * i:256 * i + 256], ACT.Copy, scale=scale))

            bank, tok = project_T("ev_a", xs, ring)
            t_fw = out_of(bank, 0, FW, tok)
            t_ki = out_of(bank, 1, KI, tok)
            bank.free = [t_ki]
            t_qi = []
            for j in range(2):
                bank, tok = project_T("ev_a", xs, ring)
                t = A.done(A(tok, fz).activation(QI[:, 512 * j:512 * j + 512], bank.t[:, :], ACT.Copy, scale=0.125))
                bank.free = [t]
                t_qi.append(t)
            bank = ring.take()
            P(t_fw, bank.free)
            for tt in range(2):
                last = nc.tensor.transpose(bank.t[:, 16 * tt:16 * tt + 16], FW[0:16, 128 * tt:128 * tt + 128], ident[0:16, 0:16])
            t_fwt = P.done(last)
            t_wi = V.done(V(t_fwt, fz).tensor_scalar(WI, bank.t[:, 0:32], float(np.float32(8 ** -0.5)), None, ALU.mult))
            bank.free = [t_wi]
            ts = [None, None]
            segs = [(0, 128), (128, 384)]
            for h in range(8):
                bank = ring.take()
                P(t_qi[h // 4], t_ki, bank.free)
                q = slice(64 * (h % 2), 64 * (h % 2) + 64)
                for tt in range(2):
                    a, b = segs[tt]
                    c = 256 * (h // 2) + 128 * tt
                    last = nc.tensor.matmul(bank.t[:, a:b], QI[q, c:c + 128], KI[q, 0:b - a], start=True, stop=True)
                tp = P.done(last)
                r = rr.take()
                t = A.done(A(tp, r.free).activation(r.t[:, :], bank.t[:, 0:384], ACT.Relu))
                bank.free = [t]
                for tt in range(2):
                    a, b = segs[tt]
                    w = WI[:, 16 * tt + 8 + h:16 * tt + 9 + h]
                    if h == 0:
                        ts[tt] = V.done(V(t, t_wi).tensor_scalar(S[:, a:b], r.t[:, a:b], w, None, ALU.mult))
                    else:
                        ts[tt] = V.done(V(t, ts[tt]).scalar_tensor_tensor(S[:, a:b], r.t[:, a:b], w, S[:, a:b],
                                                                          ALU.mult, ALU.add))
                r.free = [ts[0], ts[1]]
            cmf = C("cmf")
            ts[0] = V.done(V(ts[0], t_cc).tensor_tensor(S[:, 0:128], S[:, 0:128], cmf, ALU.add))
            ts[1] = V.done(V(ts[1], t_cc).tensor_tensor(S[:, 256:384], S[:, 256:384], cmf, ALU.add))
            rounds = [0, 1] * 8

            def select(n):
                for _ in range(n):
                    tt = rounds.pop(0)
                    a, b = segs[tt]
                    m8 = M8[:, 8 * tt:8 * tt + 8]
                    t = V.done(V(ts[tt]).max(m8, S[:, a:b]))
                    ts[tt] = V.done(V(t).match_replace(S[:, a:b], m8, S[:, a:b], TAKEN))

            z = slice(0, 104)
            tz = V.done(V(t_fw, t_pc).tensor_scalar(FZ[z, :], FW[z, :], col("bf", 0, 104), None, ALU.add))
            nc.scalar.preload_act_table_set("natural_log_exp_and_others")
            t = tab = A.done(A(tz, t_fwt).activation(FW[z, :], FZ[z, :], ACT.Abs))
            t = A.done(A(t).activation(FW[z, :], FW[z, :], ACT.Exp, scale=-1.0))
            t = A.done(A(t).activation(FW[z, :], FW[z, :], ACT.Ln, bias=1.0))
            tz = V.done(V(tab).tensor_scalar(FZ[z, :], FZ[z, :], 0.0, None, ALU.min))
            tz = V.done(V(t, tz).tensor_tensor(FZ[z, :], FZ[z, :], FW[z, :], ALU.subtract))
            tz = V.done(V(tz).tensor_tensor_scan(FW[z, :], C("ones", 104), FZ[z, :], 0.0, ALU.mult, ALU.add))
            rv = RH.rearrange("p (h t) -> p h t", h=8)
            t_cum = []
            for a in (0, 64):
                b = a + 32
                tl = V.done(V(tz, t0).tensor_copy(L[a:a + 8, :], FW[a:a + 8, :]))
                t1 = V.done(V(t0, t_cc).tensor_copy(rv[a:a + 8], ident[a:a + 8, a:a + 8].unsqueeze(2).to_broadcast([8, 8, 256])))
                tn = V.done(V(tz).tensor_scalar(FZ[b:b + 8, :], FW[b:b + 8, :], -1.0, None, ALU.mult))
                t2 = V.done(V(tn, t1).tensor_tensor(rv[b:b + 8], ident[b:b + 8, b:b + 8].unsqueeze(2).to_broadcast([8, 8, 256]),
                                                    FZ[b:b + 8, :].unsqueeze(1).to_broadcast([8, 8, 256]), ALU.mult))
                t_cum += [tl, t1, t2]

            select(2)
            bank, tok = project_T("ev_a", xs, ring)
            t_ct = out_of(bank, 0, CT, tok)
            t_qb = [out_of(bank, 1, QB[:, 0:256], tok, 0.125)]
            bank.free = [t_qb[0]]
            t_kb = []
            for j in range(3):
                select(2)
                bank, tok = project_T("ev_a", xs, ring)
                t_kb.append(out_of(bank, 0, KB[:, 256 * j:256 * j + 256], tok))
                t_qb.append(out_of(bank, 1, QB[:, 256 * j + 256:256 * j + 512], tok, 0.125))
                bank.free = [t_qb[-1]]
            select(2)
            accv = [[ring.take()], [ring.take()]]
            toks = natural("ev_v", XS, [at(xs, k) for k in range(8)], 8, 512, accv)
            select(4)
            t_vb = []
            for tt in range(2):
                t = A.done(A(toks[tt]).activation(VB[:, 512 * tt:512 * tt + 512], accv[tt][0].t[:, :], ACT.Copy))
                accv[tt][0].free = [t]
                t_vb.append(t)
            bank, tok = project_T("ev_b", xs, ring)
            t_kb.append(out_of(bank, 0, KB[:, 768:1024], tok))
            t_qa = [out_of(bank, 1, QA[:, 0:256], tok)]
            bank.free = [t_qa[0]]

            select(2)
            t = V.done(V(ts).tensor_scalar(S, S, -2e38, 1e30, ALU.is_lt, ALU.mult))
            t_mb = [V.done(V(t, fz).tensor_scalar(MB[:, 128:256], S[:, 128:256], NEG, None, ALU.add))]
            for a in (0, 256):
                t_mb.append(V.done(V(t, fz).scalar_tensor_tensor(MB[:, a:a + 128], S[:, a:a + 128], NEG, cmb, ALU.add, ALU.add)))

            outb = {}

            def b_score(h):
                q = slice(64 * (h % 2), 64 * (h % 2) + 64)
                g = slice(64 * (h % 2), 64 * (h % 2) + 40)

                def go(bt):
                    P(t_qb[h // 2], t_kb[h // 2], t_cum)
                    for tt in range(2):
                        a, b = segs[tt]
                        c = 256 * (h // 2)
                        o = bt[:, a:b]
                        nc.tensor.matmul(o, QB[q, c + 128 * tt:c + 128 * tt + 128], KB[q, c:c + b - a], start=True, stop=False)
                        nc.tensor.matmul(o, L[g, 128 * tt:128 * tt + 128], rv[g, h, 0:b - a], start=False, stop=False)
                        last = nc.tensor.matmul(bt[:, b - 128:b], identb, cmb, start=False, stop=True)
                    return P.done(last)
                return go

            def pair_out(h, chunk):
                if h % 2 == 0:
                    outb[0] = ring.take()
                    P(outb[0].free)
                return outb[0], slice(64 * (h % 2), 64 * (h % 2) + 64)

            def put(h, chunk, bank, tp):
                if h % 2:
                    t = split_to(MS[:, chunk, 0:256], MS[:, chunk, 256:512], bank.t[:, 0:256], tp)
                    bank.free = [t]
                    ms[chunk] = t

            def b_value(h):
                def go(pt, t):
                    bank, q = pair_out(h, 4 + h // 2)
                    P(t, t_vb)
                    v = slice(64 * h, 64 * h + 64)
                    nc.tensor.matmul(bank.t[q, 0:256], VB[:, v], pt[:, 0:256], start=True, stop=False)
                    tp = P.done(nc.tensor.matmul(bank.t[q, 128:256], VB[:, 512 + 64 * h:576 + 64 * h], pt[:, 256:384],
                                                 start=False, stop=True))
                    put(h, 4 + h // 2, bank, tp)
                    return tp
                return go

            ms = {}
            t_last = {}

            def rest_of_qa():
                t_last["qa"] = project_T("ev_b", xs, ring)

            def rest_of_qa_2():
                bank, tok = t_last["qa"]
                t = A.done(A(tok).activation(QA[:, 256:768], bank.t[:, :], ACT.Copy))
                bank.free = [t]
                t_qa.extend([t, t])

            def latents_by_key():
                t_last["qc"] = project_T("ev_c", xs, ring)
                bank = t_last["cb"] = ring.take()
                P(t_ct, bank.free)
                for tt in range(2):
                    last = nc.tensor.transpose(bank.t[:, 128 * tt:128 * tt + 128], CT[:, 128 * tt:128 * tt + 128], ident)
                t_last["ct"] = P.done(last)

            def latents_by_key_2():
                bank, tok = t_last["qc"]
                t_qa.append(out_of(bank, 0, QA[:, 768:1024], tok))
                bank.free = [t_qa[-1]]
                bank = t_last["cb"]
                t_last["cn"] = V.done(V(t_last["ct"]).tensor_copy(CN, bank.t[:, 0:256]))
                bank.free = [t_last["cn"]]

            lat, mixed = {}, {}

            def a_prep(h):
                q = slice(64 * (h % 2), 64 * (h % 2) + 64)

                def go():
                    bank = ring.take()
                    c = 256 * (h // 2)
                    tp = P.done(P(t_qa[h // 2], t_wk, bank.free).matmul(
                        bank.t[:, 0:256], WK[q, 128 * (h // 2):128 * (h // 2) + 128], QA[q, c:c + 256], start=True, stop=True))
                    ql = QLr.take()
                    t = A.done(A(tp, ql.free).activation(ql.t, bank.t[:, 0:256], ACT.Copy, scale=0.125))
                    bank.free = [t]
                    lat[h] = ql, t
                return go

            def a_score(h):
                def go(bt):
                    ql, t = lat[h]
                    P(t, t_ct, t_bh, t_mb)
                    for tt in range(2):
                        a, b = segs[tt]
                        o = bt[:, a:b]
                        nc.tensor.matmul(o, ql.t[:, 128 * tt:128 * tt + 128], CT[:, 0:b - a], start=True, stop=False)
                        nc.tensor.matmul(o, ident, Bh[:, 256 * h + 128 - 128 * tt:256 * h + 256], start=False, stop=False)
                        last = nc.tensor.matmul(o, identb, MB[:, a:b], start=False, stop=True)
                    tp = P.done(last)
                    ql.free = [tp]
                    return tp
                return go

            def a_value(h):
                def go(pt, t):
                    bank = ring.take()
                    P(t, t_last["cn"], bank.free)
                    nc.tensor.matmul(bank.t[:, 0:256], CN[:, 0:128], pt[:, 0:256], start=True, stop=False)
                    tp = P.done(nc.tensor.matmul(bank.t[:, 128:256], CN[:, 128:256], pt[:, 256:384], start=False, stop=True))
                    oa = OAr.take()
                    t = V.done(V(tp, oa.free).tensor_copy(oa.t, bank.t[:, 0:256]))
                    bank.free = [t]
                    mixed[h] = oa, t
                    return tp
                return go

            def a_post(h):
                def go():
                    oa, t = mixed[h]
                    b2, q = pair_out(h, h // 2)
                    t2 = P.done(P(t, t_wv).matmul(b2.t[q, 0:256], WV[:, 64 * h:64 * h + 64], oa.t, start=True, stop=True))
                    oa.free = [t2]
                    put(h, h // 2, b2, t2)
                return go

            QLr.slots.append(Slot(rr.slots[1].t[:, 0:256]))
            QLr.slots[-1].free = rr.slots[1].free
            heads = [{"score": b_score(h), "value": b_value(h)} for h in range(8)]
            heads[2]["prep"] = rest_of_qa
            heads[3]["prep"] = rest_of_qa_2
            heads[5]["prep"] = latents_by_key
            heads[6]["prep"] = latents_by_key_2
            heads += [{"prep": a_prep(h), "score": a_score(h), "value": a_value(h), "post": a_post(h)} for h in range(8)]
            attend(heads, True, Pr, PTr, nmr, ring)
            state["gb"] = [("p", P.n)]
            W.share = 3
            return natural("ev_o", MS, ms, 8, 1024, accs, 2)

        def ffn(xs, layer, kind):
            fz = fence()
            R = Arena()
            hbr = [Slot(R(520)) for _ in range(2)]
            gr = Ring([R(512) for _ in range(3)])
            hr = Ring([R(256) for _ in range(3)])
            for s in hbr:
                t = V.done(V(fz).memset(s.t[:, 0:2], 0.0))
                t = V.done(V(fz).memset(s.t[:, 258:262], 0.0))
                s.free = [t]
            hbr = Ring(hbr)
            up, down = ("up1", "down1") if kind == 1 else ("up2", "down2")
            hs = {}

            def one(j):
                bank, tok = project_T(up, xs, high)
                hb, g, h = hbr.take(), gr.take(), hr.take()
                if kind == 1:
                    v = hb.t.rearrange("p (a n) -> p a n", a=2)
                    w = [[col("fc1", 132 * layer + 66 * a + 3 * j + i) for i in range(3)] for a in range(2)]
                    tc = A.done(A(tok, hb.free, fz).activation(
                        v[:, :, 2:258], bank.t[:, :].rearrange("p (a n) -> p a n", a=2), ACT.Copy))
                    ts = []
                    for a in range(2):
                        o = g.t[:, 256 * a:256 * a + 256]
                        t = A.done(A(tc, g.free).activation(o, bank.t[:, 256 * a:256 * a + 256], ACT.Copy, scale=w[a][2]))
                        bank.free = [t]
                        t = V.done(V(t, tc).scalar_tensor_tensor(o, v[:, a, 1:257], w[a][1], o, ALU.mult, ALU.add))
                        t = V.done(V(t).scalar_tensor_tensor(o, v[:, a, 0:256], w[a][0], o, ALU.mult, ALU.add))
                        ts.append(t)
                    hb.free = [ts[1]]
                    t = A.done(A(ts[0], h.free).activation(h.t, g.t[:, 0:256], ACT.Silu))
                    t = V.done(V(t, ts[1]).tensor_tensor(h.t, h.t, g.t[:, 256:512], ALU.mult))
                    g.free = [t]
                else:
                    w = [col("fc2", 66 * layer + 3 * j + i) for i in range(3)]
                    o = g.t[:, 0:256]
                    tc = A.done(A(tok, hb.free, fz).activation(hb.t[:, 2:258], bank.t[:, 0:256], ACT.Copy))
                    t = A.done(A(tc, g.free).activation(o, bank.t[:, 0:256], ACT.Identity, scale=w[1],
                                                        bias=col("fb2", 22 * layer + j)))
                    tg = t
                    t = V.done(V(t, tc).scalar_tensor_tensor(o, hb.t[:, 1:257], w[0], o, ALU.mult, ALU.add))
                    t = V.done(V(t).scalar_tensor_tensor(o, hb.t[:, 3:259], w[2], o, ALU.mult, ALU.add))
                    hb.free = [t]
                    t = A.done(A(t, h.free).activation(h.t, o, ACT.Gelu_apprx_tanh))
                    g.free = [t]
                    t = V.done(V(t, tg).tensor_tensor(h.t, h.t, bank.t[:, 256:512], ALU.mult))
                    bank.free = [t]
                k = j % 6
                hs[j] = split_to(MS[:, k, 0:256], MS[:, k, 256:512], h.t, t, fz)
                h.free = [hs[j]]

            def down_of(m, last=False):
                js = range(2 * m, 2 * m + (4 if last else 2))
                return accumulate(down, MS, [j % 6 for j in js], {j % 6: hs[j] for j in js}, 1024, accs, m == 0, last,
                                  2 if last else 1, False, last)

            for m in range(11):
                if m == 5:
                    load_gains()
                one(2 * m)
                one(2 * m + 1)
                if 0 < m < 10:
                    down_of(m - 1)
            return down_of(9, True)

        def odd(xs):
            fz = fence()
            R = Arena()
            VG, XC = R(1024), R(1024)
            GN, SW, SB = R(512), R(1024), R(128)
            S1, S2, S3 = R(16), R(16), R(16)
            U = R(1024)
            gcr = Ring([R(256) for _ in range(2)])
            zr = [Slot(R(260)) for _ in range(4)]
            yr = [R(256) for _ in range(4)]
            xr = Ring([R(256) for _ in range(2)])
            W.share = 4
            t_gn = dma("d_gn", GN, bass.AP(tensor=T["od_sgu_g"].tensor, offset=0, ap=[[0, 128], [1, 512]]), fz)
            t_sw = dma("d_sw", SW, T["sgu_w"], fz)
            t_sb = dma("d_sb", SB[0:8, :], T["od_sgu_b"][0], fz)
            tm = V.done(V(t_sw).tensor_tensor(SW.rearrange("p (g t) -> p g t", g=8), SW.rearrange("p (g t) -> p g t", g=8),
                                              C("tril").unsqueeze(1).to_broadcast([128, 8, 128]), ALU.mult))
            tz = []
            for s in zr:
                tz.append(V.done(V(fz).memset(s.t[:, 0:2], 0.0)))
            acc = [[low[0]], [low[1]]]
            toks = natural("od_v", XS, [at(xs, k) for k in range(8)], 8, 512, acc, 1, 2)
            tg = []
            for tt in range(2):
                t = A.done(A(toks[tt], fz).activation(VG[:, 512 * tt:512 * tt + 512], acc[tt][0].t[:, :], ACT.Gelu_apprx_tanh))
                acc[tt][0].free = [t]
                tg.append(t)
            tu = []
            for j in range(2):
                bank, tok = project_T("od_t", xs, high)
                t = A.done(A(tok, fz).activation(U[:, 512 * j:512 * j + 512], bank.t[:, :], ACT.Gelu_apprx_tanh))
                bank.free = [t]
                tu += [t, t]
            v3 = VG.rearrange("p (g d) -> p g d", d=64)
            x3 = XC.rearrange("p (g d) -> p g d", d=64)
            t = V.done(V(tg).tensor_reduce(S1, v3, AX.X, ALU.add))
            t = V.done(V(t).tensor_scalar(S1, S1, 1.0 / 64, None, ALU.mult))
            t = V.done(V(t).tensor_tensor(v3, v3, S1.unsqueeze(2).to_broadcast([128, 16, 64]), ALU.subtract))
            ta = A.done(A(t, fz).activation(XC, VG, ACT.Square))
            t = V.done(V(ta).tensor_reduce(S2, x3, AX.X, ALU.add))
            t = rstd_of(S3, S2, 1.0 / 64, LN_EPS, t)
            t = V.done(V(t).tensor_tensor(x3, v3, S3.unsqueeze(2).to_broadcast([128, 16, 64]), ALU.mult))
            t_vn = V.done(V(t, t_gn).tensor_tensor(XC.rearrange("p (t d) -> p t d", t=2), XC.rearrange("p (t d) -> p t d", t=2),
                                                   GN.unsqueeze(1).to_broadcast([128, 2, 512]), ALU.mult))
            ty = []
            for i in range(4):
                bank, tok = project_T("od_t", xs, high)
                gc = gcr.take()
                w = [col("oc", 3 * i + k) for k in range(3)]
                t = A.done(A(tok, gc.free, fz).activation(gc.t, bank.t[:, 0:256], ACT.Copy))
                zb, y = zr[i].t, yr[i]
                t = V.done(V(t, tz[i]).tensor_tensor(zb[:, 2:258], gc.t, bank.t[:, 256:512], ALU.mult))
                bank.free = gc.free = [t]
                t = V.done(V(t, fz).tensor_scalar(y, zb[:, 2:258], w[2], None, ALU.mult))
                t = V.done(V(t).scalar_tensor_tensor(y, zb[:, 1:257], w[1], y, ALU.mult, ALU.add))
                t = V.done(V(t).scalar_tensor_tensor(y, zb[:, 0:256], w[0], y, ALU.mult, ALU.add))
                ty.append(t)
            ms = {}
            for c in range(4):
                bank = high.take()
                P(t_vn, tm, t_sb, t_cc, bank.free)
                for g in (2 * c, 2 * c + 1):
                    q = slice(64 * (g % 2), 64 * (g % 2) + 64)
                    for tt in range(2):
                        o = bank.t[q, 128 * tt:128 * tt + 128]
                        nc.tensor.matmul(o, XC[:, 512 * tt + 64 * g:512 * tt + 64 * g + 64], SW[:, 128 * g:128 * g + 128],
                                         start=True, stop=False)
                        last = nc.tensor.matmul(o, ident[0:8, g:g + 1].to_broadcast([8, 64]), SB[0:8, :], start=False, stop=True)
                tp = P.done(last)
                x = xr.take()
                t = V.done(V(tp, tu[c], x.free).tensor_tensor(x.t, U[:, 256 * c:256 * c + 256], bank.t[:, 0:256], ALU.mult))
                bank.free = [t]
                ms[c] = split_to(MS[:, c, 0:256], MS[:, c, 256:512], x.t, t)
                x.free = [ms[c]]
            for j in range(2):
                bank, tok = project_T("od_t", xs, high)
                for i in range(2):
                    c = 2 * j + i
                    x = xr.take()
                    t = V.done(V(tok, ty[c], x.free).tensor_tensor(x.t, yr[c], bank.t[:, 256 * i:256 * i + 256], ALU.mult))
                    bank.free = [t]
                    ms[4 + c] = split_to(MS[:, 4 + c, 0:256], MS[:, 4 + c, 256:512], x.t, t)
                    x.free = [ms[4 + c]]
            W.share = 3
            return natural("od_o", MS, ms, 8, 1024, accs, 2)

        def cross_heads(R, name, xs, layer, fz, ring, ms):
            MK, MV, XQ = R(1024), R(1024), R(1024)
            t_mk = dma(f"d_mk{layer}", MK, scr[2 * layer], fz, t_scr)
            t_mv = dma(f"d_mv{layer}", MV, scr[2 * layer + 1], fz, t_scr)
            tq = {}

            def project(j):
                tq[j] = project_T(name, xs, ring)

            def scaled(j):
                bank, tok = tq[j]
                t = A.done(A(tok, fz).activation(XQ[:, 512 * j:512 * j + 512], bank.t[:, :], ACT.Copy,
                                                 scale=float(np.float32(128 ** -0.5))))
                bank.free = [t]
                tq[j] = t

            def score(h):
                def go(bt):
                    P(tq[h // 2], t_mk)
                    for tt in range(2):
                        c = 256 * h + 128 * tt
                        last = nc.tensor.matmul(bt[:, 256 * tt:256 * tt + 256], XQ[:, c:c + 128], MK[:, 256 * h:256 * h + 256],
                                                start=True, stop=True)
                    return P.done(last)
                return go

            def value(h):
                def go(pt, t):
                    bank = ring.take()
                    P(t, t_mv, bank.free)
                    for s in range(2):
                        last = nc.tensor.matmul(bank.t[:, 0:256], MV[:, 512 * s + 128 * h:512 * s + 128 * h + 128],
                                                pt[:, 256 * s:256 * s + 256], start=(s == 0), stop=(s == 1))
                    tp = P.done(last)
                    t = split_to(MS[:, 8 + h, 0:256], MS[:, 8 + h, 256:512], bank.t[:, 0:256], tp)
                    bank.free = [t]
                    ms[8 + h] = t
                    return tp
                return go

            return [{"score": score(h), "value": value(h)} for h in range(4)], [lambda f=f, j=j: f(j) for j in range(2) for f in (project, scaled)]

        def window(xs):
            fz = fence()
            R = Arena()
            KR, QR, VN = R(512), R(2048), R(512)
            qr = Ring([R(512) for _ in range(2)])
            tr = Ring([R(512) for _ in range(2)])
            Pr = Ring([R(512) for _ in range(4)])
            PTr = Ring([R(512) for _ in range(2)])
            nmr = Ring([R(8) for _ in range(4)])
            NS = R(16)
            ring = allb
            W.share = 4
            a, b = PC["sink"]
            t_ns = V.done(V(t_pc, fz).tensor_scalar(NS, pc[:, a:b], -1.0, None, ALU.mult))

            v2 = lambda ap: ap.rearrange("p (a n) -> p a n", a=2)
            bc = lambda name: C(name).unsqueeze(1).to_broadcast([128, 2, 256])

            def turned(bank, tok, scale):
                q = qr.take()
                t = A.done(A(tok, q.free, fz).activation(q.t, bank.t[:, :], ACT.Copy, scale=scale))
                bank.free = [t]
                rb = ring.take()
                return q, t, rb, P.done(P(t, rb.free).matmul(rb.t[:, :], C("rot"), q.t, start=True, stop=True))

            def rope(dst, q, t, rb, tp):
                x = tr.take()
                t1 = V.done(V(tp, x.free, fz).tensor_tensor(v2(x.t), v2(rb.t[:, :]), bc("sin"), ALU.mult))
                rb.free = [t1]
                t2 = V.done(V(t, fz).tensor_tensor(v2(dst), v2(q.t), bc("cos"), ALU.mult))
                t3 = V.done(V(t1, t2).tensor_tensor(dst, dst, x.t, ALU.add))
                x.free = [t3]
                q.free = [t3]
                return t3

            bank, tok = project_T("wa_k", xs, ring)
            tk = rope(KR, *turned(bank, tok, 1.0))
            accv = [[ring.take()], [ring.take()]]
            toks = natural("wa_v", XS, [at(xs, k) for k in range(8)], 8, 256, accv)
            tv = []
            for tt in range(2):
                t = A.done(A(toks[tt], fz).activation(VN[:, 256 * tt:256 * tt + 256], accv[tt][0].t[:, 0:256], ACT.Copy))
                accv[tt][0].free = [t]
                tv.append(t)
            tq = []

            def queries(j):
                got = {}

                def one():
                    got[0] = project_T("wa_q", xs, ring)

                def two():
                    got[1] = turned(*got[0], 0.125)

                def three():
                    t = rope(QR[:, 512 * j:512 * j + 512], *got[1])
                    tq.extend([t, t])

                return one, two, three

            for step in queries(0):
                step()
            ms = {}
            outb = {}

            def score(c, r):
                q = slice(64 * r, 64 * r + 64)

                def go(bt):
                    P(tq[c], tk, t_cb)
                    kc = 256 * (c // 4)
                    for tt in range(2):
                        nc.tensor.matmul(bt[:, 256 * tt:256 * tt + 256], QR[q, 256 * c + 128 * tt:256 * c + 128 * tt + 128],
                                         KR[q, kc:kc + 256], start=True, stop=False)
                        o = bt[:, 128:256] if tt == 0 else bt[:, 256:384]
                        last = nc.tensor.matmul(o, identb, cmb if tt == 0 else cmb2, start=False, stop=True)
                    return P.done(last)
                return go

            def value(c, r):
                kvh = 2 * (c // 4) + r

                def go(pt, t):
                    if r == 0:
                        outb[0] = ring.take()
                        P(outb[0].free)
                    bank = outb[0]
                    q = slice(64 * r, 64 * r + 64)
                    P(t, tv)
                    for s in range(2):
                        last = nc.tensor.matmul(bank.t[q, 0:256], VN[:, 256 * s + 64 * kvh:256 * s + 64 * kvh + 64],
                                                pt[:, 256 * s:256 * s + 256], start=(s == 0), stop=(s == 1))
                    tp = P.done(last)
                    if r:
                        t = split_to(MS[:, c, 0:256], MS[:, c, 256:512], bank.t[:, 0:256], tp)
                        bank.free = [t]
                        ms[c] = t
                    return tp
                return go

            V(t_ns)
            A(t_ns)
            heads = []
            for c in range(8):
                for r in range(2):
                    h = (c % 4) + 4 * r + 8 * (c // 4)
                    heads.append({"score": score(c, r), "sink": (col("sink", h), NS[:, h:h + 1]), "value": value(c, r)})
            more, cross = cross_heads(R, "wa_x", xs, 0, fz, ring, ms)
            for j in range(1, 4):
                for i, step in enumerate(queries(j)):
                    heads[4 * j - 3 + i]["prep"] = step
            for i, h in enumerate((12, 13, 14, 15)):
                heads[h]["prep"] = cross[i]
            attend(heads + more, False, Pr, PTr, nmr, ring)
            W.share = 3
            return natural("wa_o", MS, ms, 12, 1024, accs, 2)

        def hgrn(xs):
            fz = fence()
            R = Arena()
            VN = yb
            SZ, SQ = Slot(R(512)), Slot(R(512))
            FF, LF, CS, E0 = R(512), R(514), R(1024), R(512)
            KKr = Ring([R(512) for _ in range(2)])
            QQr = Ring([R(256) for _ in range(2)])
            GTr = Ring([R(256) for _ in range(4)])
            X0, X1 = Slot(R(1024)), Slot(R(1536))
            STr = Ring([R(512) for _ in range(2)])
            ONr = Ring([R(256) for _ in range(2)])
            UD = R(64)
            DD = gb[:, :, :].rearrange("p a d -> p (a d)")
            stat = Ring([st[:, 32 * i:32 * i + 8] for i in range(2)])
            t = V.done(V(fz).memset(LF[:, 0:1], 0.0))
            t_lf = V.done(V(fz).memset(LF[:, 257:258], 0.0))
            lo0 = PC["lbl"][0]
            l0, l1 = pc[:, lo0:lo0 + 16], pc[:, lo0 + 16:lo0 + 32]
            m, e0, e1 = lb[:, 0:16], lb[:, 16:32], lb[:, 32:48]
            t = V.done(V(t_pc, fz).tensor_tensor(m, l0, l1, ALU.max))
            t1 = V.done(V(t).tensor_tensor(e0, l0, m, ALU.subtract))
            t2 = V.done(V(t).tensor_tensor(e1, l1, m, ALU.subtract))
            t = A.done(A(t1, t2).activation(lb[:, 16:48], lb[:, 16:48], ACT.Exp))
            t = V.done(V(t).tensor_tensor(m, e0, e1, ALU.add))
            t = V.done(V(t).reciprocal(m, m))
            t1 = V.done(V(t).tensor_tensor(e0, e0, m, ALU.mult))
            t2 = V.done(V(t).tensor_tensor(e1, e1, m, ALU.mult))
            t = V.done(V(t1, t2).tensor_tensor(m, e0, e1, ALU.add))
            t = V.done(V(t).tensor_tensor(m, m, e0, ALU.subtract))
            t_lb = V.done(V(t).tensor_scalar(e0, m, -1.0, 1.0, ALU.mult, ALU.add))
            vacc = [[low[0], low[1]], [low[2], low[3]]]
            toks = natural("hg_v", XS, [at(xs, k) for k in range(8)], 8, 1024, vacc, 1, 2)
            tv = []
            for tt in range(2):
                for h in range(2):
                    t = A.done(A(toks[tt], fz, state["yb"][tt]).activation(
                        VN[:, tt, 512 * h:512 * h + 512], vacc[tt][h].t[:, :], ACT.Copy))
                    vacc[tt][h].free = [t]
                    tv.append(t)
            ring = allb
            free = {"FF": [], "LF": [t_lf], "CS": [], "E0": [], "DD": [state["gb"]], "UD": []}
            D4 = DD.rearrange("p (l d t) -> p l d t", l=4, d=2)
            C3 = CS.rearrange("p (k d t) -> p k d t", k=2, d=2)
            ms = {}

            def gates(h, bz, tz, bq, tq):
                ta = A.done(A(tz, SZ.free, fz).activation(SZ.t, bz.t[:, :], ACT.Sigmoid))
                bz.free = [ta]
                tb = A.done(A(tq, SQ.free, fz).activation(SQ.t, bq.t[:, :], ACT.Sigmoid))
                for d in range(2):
                    o = 8 * d + h
                    tf = V.done(V(ta, t_lb, free["FF"]).tensor_scalar(
                        FF[:, 256 * d:256 * d + 256], SZ.t[:, 256 * d:256 * d + 256], e0[:, o:o + 1], m[:, o:o + 1],
                        ALU.mult, ALU.add))
                SZ.free = [tf]
                kk, qq, gt = KKr.take(), QQr.take(), GTr.take()
                tk = V.done(V(tf, kk.free).tensor_scalar(kk.t, FF, -1.0, 1.0, ALU.mult, ALU.add))
                t_q = V.done(V(tb, qq.free).tensor_tensor(qq.t, SQ.t[:, 0:256], bq.t[:, 0:256], ALU.mult))
                t_g = V.done(V(tb, gt.free).tensor_tensor(gt.t, SQ.t[:, 256:512], bq.t[:, 256:512], ALU.mult))
                bq.free = SQ.free = [t_g]
                return tf, tk, t_q, kk, qq, gt

            def log_f(tf, tk):
                lf = LF.rearrange("p (d t) -> p d t", d=2)
                tl = A.done(A(tf, free["LF"]).activation(lf[:, :, 1:257], FF.rearrange("p (d t) -> p d t", d=2), ACT.Ln))
                free["FF"] = [tl, tk]
                return tl

            def sums(tl):
                lf = LF.rearrange("p (d t) -> p d t", d=2)
                todo = []
                for k, mask in ((0, C("m64")), (1, C("ones"))):
                    todo.append(lambda k=k, mask=mask: V.done(V(tl, free["CS"], fz).tensor_tensor_scan(
                        C3[:, k, 0, :], mask, lf[:, 0, 1:257], 0.0, ALU.mult, ALU.add)))
                    todo.append(lambda k=k, mask=mask: V.done(V(tl, free["CS"], fz).tensor_tensor_scan(
                        C3[:, k, 1, :], lf[:, 1, 0:256], mask, 0.0, ALU.add, ALU.mult)))
                return todo

            def distances(tc):
                free["LF"] = [tc]
                V(tc, free["DD"])
                for lev in range(4):
                    n = 32 << lev
                    nb = 256 // n
                    for d in range(2):
                        src = C3[:, lev // 2, d, :].rearrange("p (b n) -> p b n", n=n)
                        dst = D4[:, lev, d, :].rearrange("p (b n) -> p b n", n=n)
                        mid = n // 2 - 1 + d
                        td = V.done(nc.vector.tensor_tensor(dst, src, src[:, :, mid:mid + 1].to_broadcast([128, nb, n]),
                                                            ALU.subtract))
                free["CS"] = [td]
                return td

            def decays(td):
                nc.scalar.preload_act_table_set("natural_log_exp_and_others")
                tn = A.done(A(td).activation(DD[:, 512:2048], DD[:, 512:2048], ACT.Abs))
                te1 = A.done(A(td, free["E0"]).activation(E0, DD[:, 0:512], ACT.Exp, scale=-1.0))
                te2 = A.done(A(te1).activation(DD[:, 0:512], DD[:, 0:512], ACT.Exp))
                te3 = A.done(A(tn).activation(DD[:, 512:2048], DD[:, 512:2048], ACT.Exp, scale=-1.0))
                return te2, te3

            def factors(kk, qq, tk, te2, te3, t_q):
                KK, QQ = kk.t, qq.t

                def mul(toks, dst, a, b):
                    return V.done(V(*toks).tensor_tensor(dst, a, b, ALU.mult))

                need = (te2, t_q, tk, X0.free, fz)
                mul(need, X0.t[:, 0:256], QQ, DD[:, 0:256])
                mul(need, X0.t[:, 256:512], KK[:, 0:256], E0[:, 0:256])
                mul(need, X0.t[:, 512:768], QQ, E0[:, 256:512])
                free["E0"] = [mul(need, X0.t[:, 768:1024], KK[:, 256:512], DD[:, 256:512])]
                need = (te3, X1.free)
                for lev in range(1, 4):
                    half = 16 << lev
                    for d in range(2):
                        v = lambda ap: ap.rearrange("p (b s n) -> p b s n", s=2, n=half)
                        dst = v(X1.t[:, 512 * (lev - 1) + 256 * d:512 * (lev - 1) + 256 * d + 256])
                        e = v(D4[:, lev, d, :])
                        vk, vq = v(KK[:, 256 * d:256 * d + 256]), v(QQ)
                        mul(need, dst[:, :, d, :], vk[:, :, d, :], e[:, :, d, :])
                        t = mul(need, dst[:, :, 1 - d, :], vq[:, :, 1 - d, :], e[:, :, 1 - d, :])
                free["DD"] = kk.free = qq.free = [t]
                return t

            mm = nc.tensor.matmul

            def scores(tx):
                main, diag = ring.take(), ring.take()
                P(tx, main.free, diag.free)
                qf, kf, qb, kb = (X0.t[:, 256 * i:256 * i + 256] for i in range(4))
                for tile in range(2):
                    for i in range(4):
                        o = 128 * tile + 32 * i
                        r = slice(32 * i, 32 * i + 32)
                        mm(main.t[r, 256 * tile + o:256 * tile + o + 32], kf[:, o:o + 32], qf[:, o:o + 32], start=True, stop=True)
                        mm(diag.t[r, 32 * tile:32 * tile + 32], kb[:, o:o + 32], qb[:, o:o + 32], start=True, stop=True)
                for lev in range(1, 4):
                    half = 16 << lev
                    xf_ = X1.t[:, 512 * (lev - 1):512 * (lev - 1) + 256]
                    xb_ = X1.t[:, 512 * (lev - 1) + 256:512 * lev]
                    for o in range(0, 256, 2 * half):
                        L_, R_ = slice(o, o + half), slice(o + half, o + 2 * half)
                        for x, ks, qs in ((xf_, L_, R_), (xb_, R_, L_)):
                            tile, r = ks.start // 128, ks.start % 128
                            last = mm(main.t[r:r + half, 256 * tile + qs.start:256 * tile + qs.stop], x[:, ks], x[:, qs],
                                      start=True, stop=True)
                tp = P.done(last)
                X0.free = [tp]
                X1.free = [tp]
                return main, diag, tp

            def masked(main, diag, tp):
                s = STr.take()
                t1 = V.done(V(tp, s.free, fz).tensor_tensor(s.t, main.t[:, :], C("m1"), ALU.mult))
                main.free = [t1]
                t2 = V.done(V(tp, free["UD"]).tensor_tensor(UD, diag.t[:, 0:64], C("mbc"), ALU.mult))
                diag.free = [t2]
                V(t1, t2)
                for i in range(4):
                    sv = s.t[32 * i:32 * i + 32, :]
                    ap = bass.AP(tensor=sv.tensor, offset=sv.offset + 32 * i, ap=[list(sv.ap[0]), [384, 2], [1, 32]])
                    uv = UD[32 * i:32 * i + 32, :].rearrange("p (a n) -> p a n", a=2)
                    ts = V.done(nc.vector.tensor_tensor(ap, ap, uv, ALU.add))
                free["UD"] = [ts]
                return s, ts

            def values(h, s, ts):
                bank = ring.take()
                P(ts, tv, bank.free)
                for tt in range(2):
                    for sb_ in range(2):
                        last = mm(bank.t[:, 128 * tt:128 * tt + 128], s.t[:, 256 * sb_ + 128 * tt:256 * sb_ + 128 * tt + 128],
                                  VN[:, sb_, 128 * h:128 * h + 128], start=(sb_ == 0), stop=(sb_ == 1))
                tp = P.done(last)
                s.free = [tp]
                return bank, tp

            def squares(bank, tp):
                on, sc = ONr.take(), stat.take()
                tq = []
                for tt in range(2):
                    tq.append(A.done(A(tp, on.free, sc.free, fz).activation(
                        on.t[:, 128 * tt:128 * tt + 128], bank.t[:, 128 * tt:128 * tt + 128], ACT.Square,
                        accum_out=sc.t[:, tt:tt + 1])))
                return on, sc, tq

            def scaled(bank, on, sc, tq, between):
                t = rstd_of(sc.t[:, 2:4], sc.t[:, 0:2], 1.0 / 128, RMS_EPS, tq, between)
                for tt in range(2):
                    to = V.done(V(t, tq).tensor_scalar(on.t[:, 128 * tt:128 * tt + 128], bank.t[:, 128 * tt:128 * tt + 128],
                                                       sc.t[:, 2 + tt:3 + tt], None, ALU.mult))
                sc.free = [to]
                bank.free = [to]
                return to

            def turned(on, to):
                b2 = ring.take()
                P(to, b2.free)
                for tt in range(2):
                    last = nc.tensor.transpose(b2.t[:, 128 * tt:128 * tt + 128], on.t[:, 128 * tt:128 * tt + 128], ident)
                return b2, P.done(last)

            def gated(h, on, gt, b2, tp):
                t = V.done(V(tp).scalar_tensor_tensor(on.t, b2.t[:, 0:256], col("bng", h), gt.t, ALU.mult, ALU.mult))
                b2.free = [t]
                gt.free = [t]
                ms[h] = split_to(MS[:, h, 0:256], MS[:, h, 256:512], on.t, t)
                on.free = [ms[h]]

            heads, cross = cross_heads(R, "hg_x", xs, 1, fz, ring, ms)
            W.share = 4
            proj, gate, csum, fact, normed = {}, {}, {}, {}, {}
            proj[0] = (*project_T("hg_t", xs, ring), *project_T("hg_t", xs, ring))
            tail = None
            for n in range(-1, 10):
                if n == 8:
                    fz2 = fence()
                    R2 = Arena()
                    Pr = Ring([R2(512) for _ in range(4)])
                    PTr = Ring([R2(512) for _ in range(2)])
                    nmr = Ring([R2(8) for _ in range(4)])
                    for ring_ in (Pr, PTr, nmr):
                        for s in ring_.slots:
                            s.free = [fz2]
                    W.share = 3
                    tail = attend_steps(heads, False, Pr, PTr, nmr, ring)
                    next(tail)
                if n - 2 in normed:
                    on, tr = normed[n - 2]
                    gated(n - 2, on, gate[n - 2][5], *tr)
                if n - 1 in fact:
                    sc_ = scores(fact[n - 1])
                if n in csum:
                    td = distances(csum[n])
                if n + 1 < 8:
                    gate[n + 1] = gates(n + 1, *proj[n + 1])
                if n in csum:
                    te2, te3 = decays(td)
                if n + 1 < 8:
                    tl = log_f(*gate[n + 1][0:2])
                if n - 1 in fact:
                    mk = masked(*sc_)
                if tail:
                    next(tail)
                    next(tail)
                if n + 2 < 8:
                    pz = project_T("hg_t", xs, ring)
                if n - 1 in fact:
                    pv = values(n - 1, *mk)
                if n in csum:
                    tf, tk, t_q, kk, qq, gt = gate[n]
                    fact[n] = factors(kk, qq, tk, te2, te3, t_q)
                todo = sums(tl) if n + 1 < 8 else []
                tc = []

                def some(count=1):
                    for _ in range(min(count, len(todo))):
                        tc[:] = [todo.pop(0)()]

                if n - 1 in fact:
                    sqs = squares(*pv)
                    to = scaled(pv[0], *sqs, some)
                some(4)
                if n + 1 < 8:
                    csum[n + 1] = tc[0]
                if n + 2 < 8:
                    proj[n + 2] = (*pz, *project_T("hg_t", xs, ring))
                elif n in (6, 7):
                    cross[2 * (n - 6)]()
                    cross[2 * (n - 6) + 1]()
                if tail:
                    next(tail)
                if n - 1 in fact:
                    normed[n - 1] = sqs[0], turned(sqs[0], to)
            state["gb"] = [free["DD"]]
            last_p = ("p", P.n)
            state["yb"] = [[last_p], [last_p]]
            for _ in tail:
                pass
            return natural("hg_o", MS, ms, 12, 1024, accs, 2)

        steps = [
            lambda xs: layer_norm(accs, even(xs), 0),
            lambda xs: layer_norm(accs, ffn(xs, 0, 1), 1),
            lambda xs: layer_norm(accs, odd(xs), 2),
            lambda xs: layer_norm(accs, ffn(xs, 1, 1), 3),
            lambda xs: residual_rms(accs, window(xs), 0, lambda k: col("rg", 8 + k)),
            lambda xs: residual_rms(accs, ffn(xs, 0, 2), 1, lambda k: col("rg", 16 + k)),
            lambda xs: residual_rms(accs, hgrn(xs), 2, lambda k: col("rg", 24 + k)),
            lambda xs: residual_rms(accs, ffn(xs, 1, 2), 3, None),
        ]
        for step in steps:
            xs = step(xs)
        finish()


def constants():
    f = np.float32
    cc = np.zeros((128, NCC), f)
    p, j = np.arange(128)[:, None], np.arange(128)[None, :]

    def put(name, a):
        lo, hi = CC[name]
        cc[:, lo:hi] = a

    put("ident", p == j)
    put("cmf", np.where(j <= p, 0.0, -1e37))
    put("tril", p <= j)
    t = np.arange(256)
    put("m64", (t % 64 != 0)[None])
    put("ones", 1.0)
    m1 = np.ones((128, 2, 256))
    mb = np.zeros((128, 2, 32))
    for tile in range(2):
        for s in range(128):
            b = s // 32
            lo = 128 * tile + 32 * b
            m1[s, tile, lo:lo + 32] = (np.arange(lo, lo + 32) >= 128 * tile + s)
            mb[s, tile] = (np.arange(lo, lo + 32) <= 128 * tile + s)
    put("m1", m1.reshape(128, 512))
    put("mbc", mb.reshape(128, 64))
    inv = f(10000.0) ** (-np.arange(32, dtype=f) / f(32))
    ang = np.arange(256, dtype=f)[None, :] * inv[:, None].astype(f)
    put("cos", np.tile(np.cos(ang), (4, 1)))
    put("sin", np.tile(np.sin(ang), (4, 1)))
    rot = np.zeros((128, 128))
    for b in (0, 64):
        for i in range(32):
            rot[b + i + 32, b + i] = -1.0
            rot[b + i, b + i + 32] = 1.0
    put("rot", rot)
    cb = np.zeros((128, 384), f)
    cb[:, 0:128] = p == j
    cb[:, 128:256] = np.where(j <= p, 0.0, NEG)
    cb[:, 256:384] = np.where(j >= p, 0.0, NEG)
    n = np.maximum(255 - np.arange(384), 0)
    large = 16 + (np.log(np.maximum(n, 1).astype(f) / f(16)) / f(np.log(8.0)) * f(16)).astype(np.int32)
    bucket = np.where(n < 16, n, np.minimum(large, 31))
    onehot = (np.arange(32)[:, None] == bucket[None, :]).astype(f)
    return cc, cb, onehot


def layouts(d):
    a = {k: np.ascontiguousarray(np.asarray(v)) for k, v in d.items()}

    def tiles(w, cols):
        k = w.shape[0] // 128
        t = np.stack([w[:, c] for c in cols]).reshape(len(cols) // 2, 2, k, 128, 128)
        return np.ascontiguousarray(t.transpose(0, 3, 1, 2, 4)).reshape(len(cols) // 2, 128, -1)

    def rows(w):
        per = 2048 // w.shape[1]
        t = w.reshape(-1, per, 128, w.shape[1]).transpose(0, 2, 1, 3)
        return np.ascontiguousarray(t).reshape(-1, 128, 2048)

    def span(lo, n=1):
        return [np.arange(lo + 128 * i, lo + 128 * i + 128) for i in range(n)]

    r = {"x": a["x"], "mem_2": a["mem_2"], "od_sgu_g": a["od_sgu_g"], "od_sgu_b": a["od_sgu_b"]}
    mk = a["w_mem_kv_2"]
    r["mem_k"] = np.concatenate([tiles(mk[l], span(0, 4)) for l in range(2)])
    r["mem_v"] = np.concatenate([rows(mk[l][:, 512:]) for l in range(2)])
    w = a["ev_w_in"][0]
    fw = np.zeros((1024, 128), w.dtype)
    fw[:, 0:8] = fw[:, 32:40] = fw[:, 64:72] = fw[:, 96:104] = w[:, 2760:2768]
    fw[:, 8:16] = w[:, 1216:1224]
    wx = np.concatenate([w, fw], axis=1)
    kd = np.concatenate([np.arange(1152, 1216)] * 2)
    qa, ck, qi = span(0, 4), span(512), span(640, 4)
    qb, kb = span(1224, 4), span(1736, 4)
    r["ev_a"] = tiles(wx, span(2768) + [kd] + qi + ck + [qb[0], kb[0], qb[1], kb[1], qb[2], kb[2], qb[3]])
    r["ev_a"] = r["ev_a"][:7]
    ev_b = tiles(wx, [kb[3], qa[0], qa[1], qa[2]])
    r["ev_b"] = ev_b
    r["ev_c"] = tiles(wx, [qa[3], qa[3]])[:, :, 0:1024].copy()
    r["ev_v"] = rows(w[:, 2248:2760])
    r["ev_o"] = rows(a["ev_w_o"][0])
    r["w_uk"] = np.ascontiguousarray(a["ev_w_uk"][0].reshape(4, 2, 128, 64).transpose(1, 3, 0, 2)).reshape(128, 512)
    r["w_uv"] = np.ascontiguousarray(a["ev_w_uv"][0].transpose(1, 0, 2)).reshape(128, 512)
    for name, src, dn in (("1", "ffn_w_up", "ffn_w_down"), ("2", "ffn_w_in_2", "ffn_w_out_2")):
        r["up" + name] = np.concatenate([
            tiles(a[src][l], [c for j in range(22) for c in (span(128 * j)[0], span(2816 + 128 * j)[0])]) for l in range(2)])
        r["down" + name] = np.concatenate([rows(a[dn][l]) for l in range(2)])
    w = a["od_w_in"][0]
    u, gb_, gc, z = span(0, 4), span(1024, 4), span(1536, 4), span(2048, 4)
    r["od_v"] = rows(w[:, 512:1024])
    r["od_t"] = tiles(w, u + [c for i in range(4) for c in (gc[i], z[i])] + gb_)
    r["od_o"] = rows(a["od_w_o"][0])
    r["sgu_w"] = np.ascontiguousarray(a["od_sgu_w"][0].transpose(2, 0, 1)).reshape(128, 1024)
    w = a["a_w_in_2"][0]
    pair = [np.concatenate([np.arange(64 * (8 * (c // 4) + c % 4), 64 * (8 * (c // 4) + c % 4) + 64),
                            np.arange(64 * (8 * (c // 4) + c % 4 + 4), 64 * (8 * (c // 4) + c % 4 + 4) + 64)])
            for c in range(8)]
    r["wa_k"] = tiles(w, span(1024, 2))
    r["wa_v"] = rows(w[:, 1280:1536])
    r["wa_q"] = tiles(w, pair)
    r["wa_x"] = tiles(w, span(1536, 4))
    order = np.concatenate(pair + [np.arange(1024, 1536)])
    r["wa_o"] = rows(a["a_w_out_2"][0][order])
    w = a["b_w_in_2"][0]
    r["hg_v"] = rows(w[:, 1024:2048])
    r["hg_t"] = tiles(w, [c for h in range(8) for c in (
        span(2048 + 128 * h)[0], span(3072 + 128 * h)[0], span(128 * h)[0], span(4096 + 128 * h)[0])])
    r["hg_x"] = tiles(w, span(5120, 4))
    r["hg_o"] = rows(a["b_w_out_2"][0])
    r["c_ln"] = np.stack([a["ln_g"].reshape(4, 1024), a["ln_b"].reshape(4, 1024)], axis=1).reshape(4, 1, 2048)
    ng = a["norm_g_2"]
    r["c_rg"] = np.stack([ng[0, 1], ng[0, 3], ng[1, 1], ng[1, 3]]).reshape(4, 1, 1024)
    cc, cb, onehot = constants()
    par = np.zeros((128, NPC), np.float32)

    def put(name, v):
        lo, hi = PC[name]
        par[:v.shape[0], lo:hi] = v

    def cols(v):
        v = v.reshape(-1, v.shape[-1] // 128, 128)
        return v.transpose(2, 0, 1).reshape(128, -1)

    put("ln", cols(r["c_ln"].reshape(4, 2, 1024)))
    put("rg", cols(np.stack([ng[0, 0], ng[0, 2], ng[1, 0], ng[1, 2]])))
    put("memg", cols(a["mem_norm_g_2"][None]))
    put("fc1", a["ffn_conv_w"].reshape(2, 3, 44, 128).transpose(3, 0, 2, 1).reshape(128, -1))
    put("fc2", a["ffn_conv_w_2"].reshape(2, 3, 22, 128).transpose(3, 0, 2, 1).reshape(128, -1))
    put("fb2", cols(a["ffn_conv_b_2"]))
    put("oc", a["od_conv_w"].reshape(3, 4, 128).transpose(2, 1, 0).reshape(128, -1))
    put("bng", cols(a["b_norm_g_2"]))
    put("lbl", a["b_lb_logits_2"].reshape(2, 2, 8, 128).transpose(3, 1, 0, 2).reshape(128, -1))
    bf = np.zeros((104, 1), np.float32)
    bf[0:8, 0] = bf[32:40, 0] = bf[64:72, 0] = bf[96:104, 0] = a["ev_b_f"][0]
    put("bf", bf)
    put("sink", np.tile(a["a_sink_2"], (128, 1)))
    put("relb", a["rel_bias"])
    r["c_f32"], r["c_par"], r["c_onehot"], r["c_mask"] = cc, par, onehot, cb
    return r


def kernel(**inputs):
    import concourse.bacc as bacc
    from concourse.bass_utils import run_bass_kernel_spmd as run

    r = layouts(inputs)
    nc = bacc.Bacc("TRN2", target_bir_lowering=False, num_devices=1)
    T = {k: nc.dram_tensor(f"in_{k}", v.shape, mybir.dt.from_np(v.dtype), kind="ExternalInput").ap() for k, v in r.items()}
    out = nc.dram_tensor("out_0", (1, 256, 1024), F32, kind="ExternalOutput").ap()
    program(nc, T, out)
    res = run(nc, [{f"in_{k}": v for k, v in r.items()}], core_ids=[0])
    return res.results[0]["out_0"]
```
